# Optimizing a Trainium2 kernel written in Bass

```python
import math
import jax
import jax.numpy as jnp
from jax import lax
import numpy as np

D_MODEL = 1024
BATCH = 1
SEQ = 1024
DEPTH = 2

GRID_W = 64
CTX_LEN = 256
N_MIXERS = 2
MIXER_MLA = 0
MIXER_CONV = 1
N_A = (DEPTH + 1) // 2
N_B = DEPTH // 2
MLA_HEADS = 8
Q_LORA = 384
KV_LORA = 128
NOPE_DIM = 128
ROPE_DIM = 64
V_DIM = 128
QK_DIM = NOPE_DIM + ROPE_DIM
ROPE_THETA = 10000.0
Q_BLOCK = 128
CONV_WIDTH = 31
FFN_DIM = 2816
FFN_CONV_WIDTH = 3
EPS = 1e-6

kernel_name = "hybrid_mla_conformer_dit_block"

def rmsnorm(x, g):
    xf = x.astype(jnp.float32)
    y = xf * lax.rsqrt(jnp.mean(xf * xf, axis=-1, keepdims=True) + EPS)
    return y.astype(x.dtype) * g

def layernorm(x, g, b):
    xf = x.astype(jnp.float32)
    mu = jnp.mean(xf, axis=-1, keepdims=True)
    var = jnp.mean(jnp.square(xf - mu), axis=-1, keepdims=True)
    y = (xf - mu) * lax.rsqrt(var + EPS)
    return y.astype(x.dtype) * g + b

def modulate(h, shift, scale):
    return h * (1 + scale) + shift

def depthwise_conv(x, w):
    k, ch = w.shape
    pad = (k - 1) // 2
    return lax.conv_general_dilated(
        x, w[:, None, :].astype(x.dtype), window_strides=(1,), padding=[(pad, pad)],
        dimension_numbers=("NWC", "WIO", "NWC"), feature_group_count=ch)

def rope_tables(seq_len):
    rows = seq_len // GRID_W
    row = jnp.repeat(jnp.arange(rows, dtype=jnp.float32), GRID_W)
    col = jnp.tile(jnp.arange(GRID_W, dtype=jnp.float32), rows)
    n = ROPE_DIM // 4
    inv = ROPE_THETA ** (-jnp.arange(n, dtype=jnp.float32) / n)
    ang_r = row[:, None] * inv
    ang_c = col[:, None] * inv
    ang = jnp.concatenate([ang_r, ang_r, ang_c, ang_c], axis=-1)
    return jnp.cos(ang), jnp.sin(ang)

def apply_rope_2d(x, cos, sin):
    xf = x.astype(jnp.float32)
    xs = xf.reshape(xf.shape[:-1] + (2, 2, ROPE_DIM // 4))
    rot = jnp.stack([-xs[..., 1, :], xs[..., 0, :]], axis=-2).reshape(xf.shape)
    out = xf * cos[None, :, None, :] + rot * sin[None, :, None, :]
    return out.astype(x.dtype)

def mla_project(h, w_dqkv, g_q, w_uq, g_kv, w_ukv, cos, sin, with_q):
    b, l, _ = h.shape
    if with_q:
        d = h @ w_dqkv
        cq, dkv = d[..., :Q_LORA], d[..., Q_LORA:]
    else:
        dkv = h @ w_dqkv[:, Q_LORA:]
    ckv, kr = dkv[..., :KV_LORA], dkv[..., KV_LORA:]
    kv = (rmsnorm(ckv, g_kv) @ w_ukv).reshape(b, l, MLA_HEADS, NOPE_DIM + V_DIM)
    k_nope, v = kv[..., :NOPE_DIM], kv[..., NOPE_DIM:]
    kr = kr[:, :, None, :]
    if cos is not None:
        kr = apply_rope_2d(kr, cos, sin)
    k = jnp.concatenate([k_nope, jnp.broadcast_to(kr, (b, l, MLA_HEADS, ROPE_DIM))], axis=-1)
    q = None
    if with_q:
        q = (rmsnorm(cq, g_q) @ w_uq).reshape(b, l, MLA_HEADS, QK_DIM)
        q_nope, q_rope = q[..., :NOPE_DIM], q[..., NOPE_DIM:]
        if cos is not None:
            q_rope = apply_rope_2d(q_rope, cos, sin)
        q = jnp.concatenate([q_nope, q_rope], axis=-1)
    return q, k, v

def mla_mixer(h_lat, h_ctx, w_dqkv, g_q, w_uq, g_kv, w_ukv, w_o, cos, sin, ctx_out):
    b, s, _ = h_lat.shape
    scale = 1.0 / math.sqrt(QK_DIM)
    q_lat, k_lat, v_lat = mla_project(h_lat, w_dqkv, g_q, w_uq, g_kv, w_ukv, cos, sin, True)
    q_ctx, k_ctx, v_ctx = mla_project(h_ctx, w_dqkv, g_q, w_uq, g_kv, w_ukv, None, None, ctx_out)
    k_all = jnp.concatenate([k_ctx, k_lat], axis=1).astype(jnp.float32)
    v_all = jnp.concatenate([v_ctx, v_lat], axis=1).astype(jnp.float32)
    n_blk = s // Q_BLOCK
    qb = q_lat.reshape(b, n_blk, Q_BLOCK, MLA_HEADS, QK_DIM).transpose(1, 0, 2, 3, 4)

    def attend_block(q_blk):
        sc = jnp.einsum("bqhd,bkhd->bhqk", q_blk.astype(jnp.float32), k_all) * scale
        p = jax.nn.softmax(sc, axis=-1)
        return jnp.einsum("bhqk,bkhd->bqhd", p, v_all).astype(q_blk.dtype)

    o = lax.map(attend_block, qb)
    o = o.transpose(1, 0, 2, 3, 4).reshape(b, s, MLA_HEADS * V_DIM)
    y_lat = o @ w_o
    y_ctx = None
    if ctx_out:
        sc = jnp.einsum("bqhd,bkhd->bhqk", q_ctx.astype(jnp.float32),
                        k_ctx.astype(jnp.float32)) * scale
        p = jax.nn.softmax(sc, axis=-1)
        oc = jnp.einsum("bhqk,bkhd->bqhd", p, v_ctx.astype(jnp.float32)).astype(h_ctx.dtype)
        y_ctx = oc.reshape(oc.shape[0], oc.shape[1], MLA_HEADS * V_DIM) @ w_o
    return y_lat, y_ctx

def conformer_conv(h, w_pw1, b_pw1, w_dw, b_dw, g_ln, b_ln, w_pw2, b_pw2):
    u = h @ w_pw1 + b_pw1
    a, g = jnp.split(u, 2, axis=-1)
    u = a * jax.nn.sigmoid(g)
    u = depthwise_conv(u, w_dw) + b_dw
    u = jax.nn.silu(layernorm(u, g_ln, b_ln))
    return u @ w_pw2 + b_pw2

def conv_ffn(h, w_up, w_dw, b_dw, w_down):
    u = depthwise_conv(h @ w_up, w_dw) + b_dw
    gate, val = jnp.split(u, 2, axis=-1)
    return (jax.nn.silu(gate) * val) @ w_down

def setup_inputs(seed: int = 0) -> dict:
    key = jax.random.key(seed)
    ks = iter(jax.random.split(key, 40))
    f32 = jnp.float32
    D = D_MODEL

    def nrm(shape, scale):
        return jax.random.normal(next(ks), shape, f32) * scale

    def gain(shape):
        return 1.0 + nrm(shape, 0.05)

    return {
        "x": nrm((BATCH, SEQ, D), 1.0),
        "c": nrm((BATCH, D), 1.0),
        "ctx": nrm((BATCH, CTX_LEN, D), 1.0),
        "c_ctx": nrm((D,), 1.0),
        "w_mod": nrm((DEPTH, D, 6 * D), 0.5 * D ** -0.5),
        "b_mod": nrm((DEPTH, 6 * D), 0.01),
        "g_pre_mix": gain((DEPTH, D)),
        "g_post_mix": gain((DEPTH, D)),
        "g_pre_ffn": gain((DEPTH, D)),
        "g_post_ffn": gain((DEPTH, D)),
        "mla_w_dqkv": nrm((N_A, D, Q_LORA + KV_LORA + ROPE_DIM), D ** -0.5),
        "mla_g_q": gain((N_A, Q_LORA)),
        "mla_w_uq": nrm((N_A, Q_LORA, MLA_HEADS * QK_DIM), Q_LORA ** -0.5),
        "mla_g_kv": gain((N_A, KV_LORA)),
        "mla_w_ukv": nrm((N_A, KV_LORA, MLA_HEADS * (NOPE_DIM + V_DIM)), KV_LORA ** -0.5),
        "mla_w_o": nrm((N_A, MLA_HEADS * V_DIM, D), (MLA_HEADS * V_DIM) ** -0.5),
        "cv_w_pw1": nrm((N_B, D, 2 * D), D ** -0.5),
        "cv_b_pw1": nrm((N_B, 2 * D), 0.01),
        "cv_w_dw": nrm((N_B, CONV_WIDTH, D), CONV_WIDTH ** -0.5),
        "cv_b_dw": nrm((N_B, D), 0.01),
        "cv_g_ln": gain((N_B, D)),
        "cv_b_ln": nrm((N_B, D), 0.01),
        "cv_w_pw2": nrm((N_B, D, D), D ** -0.5),
        "cv_b_pw2": nrm((N_B, D), 0.01),
        "ffn_w_up": nrm((DEPTH, D, 2 * FFN_DIM), D ** -0.5),
        "ffn_w_dw": nrm((DEPTH, FFN_CONV_WIDTH, 2 * FFN_DIM), FFN_CONV_WIDTH ** -0.5),
        "ffn_b_dw": nrm((DEPTH, 2 * FFN_DIM), 0.01),
        "ffn_w_down": nrm((DEPTH, FFN_DIM, D), FFN_DIM ** -0.5),
    }

def reference(x, c, ctx, c_ctx, w_mod, b_mod, g_pre_mix, g_post_mix, g_pre_ffn, g_post_ffn,
              mla_w_dqkv, mla_g_q, mla_w_uq, mla_g_kv, mla_w_ukv, mla_w_o,
              cv_w_pw1, cv_b_pw1, cv_w_dw, cv_b_dw, cv_g_ln, cv_b_ln, cv_w_pw2, cv_b_pw2,
              ffn_w_up, ffn_w_dw, ffn_b_dw, ffn_w_down):
    seq_len = x.shape[1]
    cos, sin = rope_tables(seq_len)
    x_lat, x_ctx = x, ctx
    for i in range(DEPTH):
        kind = i % N_MIXERS
        j = i // N_MIXERS
        ctx_out = any(l % N_MIXERS == MIXER_MLA for l in range(i + 1, DEPTH))
        need_ctx = ctx_out or kind == MIXER_MLA

        m_lat = jnp.split((jax.nn.silu(c) @ w_mod[i] + b_mod[i])[:, None, :], 6, axis=-1)
        h_lat = modulate(rmsnorm(x_lat, g_pre_mix[i]), m_lat[0], m_lat[1])
        h_ctx, m_ctx = None, None
        if need_ctx:
            m_ctx = jnp.split(jax.nn.silu(c_ctx) @ w_mod[i] + b_mod[i], 6, axis=-1)
            h_ctx = modulate(rmsnorm(x_ctx, g_pre_mix[i]), m_ctx[0], m_ctx[1])

        if kind == MIXER_MLA:
            y_lat, y_ctx = mla_mixer(h_lat, h_ctx, mla_w_dqkv[j], mla_g_q[j], mla_w_uq[j],
                                     mla_g_kv[j], mla_w_ukv[j], mla_w_o[j], cos, sin, ctx_out)
        else:
            conv_args = (cv_w_pw1[j], cv_b_pw1[j], cv_w_dw[j], cv_b_dw[j], cv_g_ln[j],
                         cv_b_ln[j], cv_w_pw2[j], cv_b_pw2[j])
            y_lat = conformer_conv(h_lat, *conv_args)
            y_ctx = conformer_conv(h_ctx, *conv_args) if ctx_out else None

        x_lat = x_lat + m_lat[2] * rmsnorm(y_lat, g_post_mix[i])
        h = modulate(rmsnorm(x_lat, g_pre_ffn[i]), m_lat[3], m_lat[4])
        x_lat = x_lat + m_lat[5] * rmsnorm(
            conv_ffn(h, ffn_w_up[i], ffn_w_dw[i], ffn_b_dw[i], ffn_w_down[i]), g_post_ffn[i])

        if ctx_out:
            x_ctx = x_ctx + m_ctx[2] * rmsnorm(y_ctx, g_post_mix[i])
            hc = modulate(rmsnorm(x_ctx, g_pre_ffn[i]), m_ctx[3], m_ctx[4])
            x_ctx = x_ctx + m_ctx[5] * rmsnorm(
                conv_ffn(hc, ffn_w_up[i], ffn_w_dw[i], ffn_b_dw[i], ffn_w_down[i]), g_post_ffn[i])
    return x_lat


_drawn_inputs = setup_inputs


def setup_inputs(seed=0):
    import zlib

    import numpy as np

    out = dict(_drawn_inputs(seed))
    spreads = {}
    factors = {'g_pre_mix': 3.317,
     'g_post_mix': 2.821,
     'g_post_ffn': 2.79,
     'mla_g_q': 8.0,
     'mla_g_kv': 3.296,
     'cv_b_pw1': 30.586,
     'cv_b_dw': 22.934,
     'cv_g_ln': 3.549,
     'cv_b_ln': 38.613,
     'cv_b_pw2': 28.891,
     'ffn_b_dw': 8.0}
    for name, (base, spread) in spreads.items():
        noise = np.random.default_rng([zlib.crc32(name.encode()), seed]).standard_normal(out[name].shape)
        drawn = base * np.exp(spread * noise) if base else spread * noise
        out[name] = jnp.asarray(drawn.astype(out[name].dtype))
    for name, factor in factors.items():
        out[name] = (out[name] * factor).astype(out[name].dtype)
    return out
```

```python
import math
from contextlib import ExitStack

import concourse.bass as bass
from concourse import mybir

P = 128
D = 1024
L = 1024
CTX = 256
KEYS = L + CTX
CB = D // P
HALF = 512
HEADS = 8
DN_START = 2
ROPE = 64
GRID_W = 64
NKB = KEYS // P
QLORA_B = 3
TAPS = 31
PAD = TAPS // 2
FB = 22
GROUPS = FB // 2
EPS = 1e-6
SCALE = 1.0 / math.sqrt(192.0)

U_DQKV, U_HEAD, U_WO = 0, 6, 14
U_FFN = (22, 112)
U_PW1, U_PW2 = 88, 104
UNITS = 178
M_DQKV, M_WO, M_PW1, M_PW2 = 0, 6, 58, 74
M_FFN = (14, 82)

V_C, V_CCTX, V_BMOD = 0, 8, 16
V_PREMIX, V_POSTMIX, V_PREFFN, V_POSTFFN = 112, 128, 144, 160
V_GQ, V_GKV, V_BPW1, V_WDW, V_BDW, V_GLN, V_BLN, V_BPW2 = 176, 179, 180, 196, 444, 452, 460, 468
V_FW, V_FB = 476, 740
NV = 828
C_MOD, C_MODX, C_SC, C_EPS, C_MX, C_NM, C_RS, C_RI, C_GV, C_AV, C_AX = 0, 96, 112, 128, 129, 137, 145, 153, 161, 169, 177
NC_SMALL = 185
MODS = 6 * CB

F_A, F_T, F_SQ, F_ACC, F_RT, F_MD, F_RAW, F_ACCX, F_END = 0, 8192, 10240, 12288, 13312, 14592, 17664, 19712, 19968
R_H, R_W, R_G, R_END = 0, 16384, 24576, 32768
R_CQ, R_CKV, R_KR, R_K, R_V0, R_PT, R_V1, R_Q = 0, 6144, 8704, 11264, 13824, 20480, 24576, 27136


def slot_of(u):
    return u % 4 if u < U_HEAD else (u - U_HEAD) % 2 if u < U_WO else (u + 2) % 4


def prior(u):
    return u - 14 if u in (U_WO + 2, U_WO + 3) else u - 2 if U_HEAD <= u <= U_WO + 1 else u - 4


def freed(u):
    if U_HEAD <= u < U_WO:
        return "pj", 10 * (u - U_HEAD + 1)
    if u < U_HEAD:
        return "mm", M_DQKV + u + 1
    if u < U_FFN[0]:
        return "mm", M_WO + u - U_WO + 1
    if U_PW1 <= u < U_FFN[1]:
        return "mm", M_PW1 + u - U_PW1 + 1
    layer = int(u >= U_FFN[1])
    at, m0, d0 = u - U_FFN[layer], M_FFN[layer], DN_START + CB * GROUPS * layer
    if at < 4:
        return "mm", m0 + at + 1
    group, q = divmod(at - 4, 6)
    if q < 4 and group < GROUPS - 1:
        return "mm", m0 + 4 * (group + 1) + q + 1
    return "dn", d0 + CB * (group + 1)


class Chain:

    def __init__(self, engine, sem):
        self.engine, self.sem, self.n, self.term = engine, sem, 0, 0

    def __call__(self, ins):
        ins.then_inc(self.sem, 1)
        self.n += 1
        self.engine.wait_ge(self.sem, self.term + self.n)

    def enter(self, i, per):
        self.start, self.per, self.term = self.n, per, i * per

    def leave(self, trips):
        assert self.n - self.start == self.per, (self.n - self.start, self.per)
        self.n, self.term = self.start + trips * self.per, 0


def build(nc, xT, ctxT, units, modw, vecs, ident_d, cs_d, cosd_d, sind_d, outT):
    F32, F32R = mybir.dt.float32, mybir.dt.float32r
    ALU, ACT, AX = mybir.AluOpType, mybir.ActivationFunctionType, mybir.AxisListType
    MUL, ADD, SUB = ALU.mult, ALU.add, ALU.subtract
    xs_d = nc.dram_tensor("residual", (CB, P, L), F32, kind="Internal").ap()
    os_d = nc.dram_tensor("heads_out", (HEADS, P, L), F32, kind="Internal").ap()

    with ExitStack() as ctx:
        F = ctx.enter_context(nc.sbuf_tensor("f32_region", [P, F_END], F32))
        R = ctx.enter_context(nc.sbuf_tensor("f32r_region", [P, R_END], F32R))
        V = ctx.enter_context(nc.sbuf_tensor("vectors", [P, NV], F32))
        S = ctx.enter_context(nc.sbuf_tensor("small", [P, NC_SMALL], F32))
        ones = ctx.enter_context(nc.sbuf_tensor("ones", [P, P], F32))
        ident = ctx.enter_context(nc.sbuf_tensor("ident", [P, P], F32))
        PS = ctx.enter_context(nc.psum_tensor("psum", [P, 8 * HALF], F32))

        def sem(name):
            return ctx.enter_context(nc.semaphore(name))

        small_in, x_in, ctx_in, table_in = sem("small_in"), sem("x_in"), sem("ctx_in"), sem("table_in")
        raw_in = [sem(f"raw_in{s}") for s in range(2)]
        w_hi, w_lo = sem("w_hi"), sem("w_lo")
        mm_done, mm_free = sem("mm_done"), sem("mm_free")
        const_set = sem("const_set")
        sq_ready, sq_used = sem("sq_ready"), sem("sq_used")
        acc_ready, sums_out, std_ready, rstd_ready = sem("acc_ready"), sem("sums_out"), sem("std_ready"), sem("rstd_ready")
        silu_c = sem("silu_c")
        mod_in = [sem(f"mod_in{s}") for s in range(2)]
        mod_part, modc_acc, mod_acc, mod_mm, mod_out = sem("mod_part"), sem("modc_acc"), sem("mod_acc"), sem("mod_mm"), sem("mod_out")
        ht_ready, h_act, h_hi, h_lo = sem("ht_ready"), sem("h_act"), sem("h_hi"), sem("h_lo")
        latent_in, mmx_done, rope_k, lat_hi, lat_lo = sem("latent_in"), sem("mmx_done"), sem("rope_k"), sem("lat_hi"), sem("lat_lo")
        pj_done, pj_free, pj_t, pj_hi = sem("pj_done"), sem("pj_free"), sem("pj_t"), sem("pj_hi")
        s_done, s_max, s_free, p_ready = sem("s_done"), sem("s_max"), sem("s_free"), sem("p_ready")
        tp_done, tp_hi, tp_lo, pt_free, o_free = sem("tp_done"), sem("tp_hi"), sem("tp_lo"), sem("pt_free"), sem("o_free")
        o_stored = [sem(f"o_stored{s}") for s in range(2)]
        blk_in = [sem(f"blk_in{k}") for k in range(CB)]
        blk_out = sem("blk_out")
        y_ready, y_new = sem("y_ready"), sem("y_new")
        y_zero, ckv_sq = sem("y_zero"), sem("ckv_sq")
        tap_done, silu_g, gp_ready, g_hi, g_lo = sem("tap_done"), sem("silu_g"), sem("gp_ready"), sem("g_hi"), sem("g_lo")
        dn_done, dn_free = sem("dn_done"), sem("dn_free")
        sig_ready, u_ready = sem("sig_ready"), sem("u_ready")
        dve_chain, act_chain, pool_chain = sem("dve_chain"), sem("act_chain"), sem("pool_chain")

        def f(at, n=L):
            return F[:, at:at + n]

        def r(at, n=L):
            return R[:, at:at + n]

        def A(k):
            return f(F_A + k * L)

        def h(k, part, half=None):
            at = R_H + part * CB * L + k * L
            return r(at) if half is None else r(at + half * HALF, HALF)

        def hx(k, part):
            return r(R_G + part * CB * CTX + k * CTX, CTX)

        def raw(s):
            return f(F_RAW + s * L)

        def w(slot, part, at=0, n=L):
            return r(R_W + slot * 2 * L + part * L + at, n)

        def sq(i):
            return f(F_SQ + (i % 2) * L)

        def pair(m):
            return PS[:, (m % 2) * 2 * HALF:(m % 2 + 1) * 2 * HALF]

        def bank(b, n=HALF, at=0):
            return PS[:, b * HALF + at:b * HALF + at + n]

        def dn(c):
            return PS[:, (4 + 2 * (c % 2)) * HALF:(6 + 2 * (c % 2)) * HALF]

        SUMS, SUMSX, MODB = PS[:, 4 * HALF:6 * HALF], bank(6, CTX), bank(7, CB)
        RT, RTX = f(F_RT), f(F_RT + L, CTX)
        CQ, CKV, KRF = [f(F_A + k * L) for k in range(3)], f(3072, KEYS), f(4352, KEYS)
        COSD, SIND = f(5632), f(6656)
        CS, ROPET, OST = f(F_SQ), [f(F_SQ + L + i * HALF, HALF) for i in range(2)], [f(F_ACC + i * HALF, HALF) for i in range(2)]
        VS = [R_V0, R_V1]

        def Pt(n, s):
            return f(F_A + ((n % 2) * 4 + s) * KEYS, KEYS)

        def G(g, jj, part, half=None):
            at = R_G + (g % 2) * 4 * L + jj * 2 * L + part * L
            return r(at) if half is None else r(at + half * HALF, HALF)

        def wait(engine, s, value):
            if not isinstance(value, int) or value > 0:
                engine.wait_ge(s, value)

        KP = [(0, HALF), (HALF, HALF), (2 * HALF, CTX)]
        PIECES = ([("v", a, n) for a, n in KP] + [("k", a, n) for a, n in KP]
                  + [("q", a * HALF, HALF) for a in range(2)] + [("qr", a * HALF, HALF) for a in range(2)])

        def piece_at(kind, head, start, n, part):
            base = VS[head % 2] if kind == "v" else {"k": R_K, "q": R_Q, "qr": R_Q + 2 * L}[kind]
            return r(base + part * (KEYS if kind in "vk" else L) + start, n)

        TP_AFTER = [[0, 1, 2], [3, 4, 5], [6, 7, 8, 9], []]
        PV_AFTER = [[0], [1, 2, 3], [4, 5, 6, 7], [8, 9]]

        block = ctx.enter_context(nc.Block())

        @block.sync
        def _(sp):
            sp.dma_start(V[:, :], vecs).then_inc(small_in, 16)
            sp.dma_start(ident[:, :], ident_d).then_inc(small_in, 16)
            sp.dma_start(f(F_T, CB * CTX).rearrange("p (k n) -> p k n", k=CB), ctxT.rearrange("k p n -> p k n")).then_inc(ctx_in, 16)
            for k in range(0, CB, 4):
                sp.dma_start(f(F_A + k * L, 4 * L).rearrange("p (k n) -> p k n", k=4),
                             xT[k:k + 4].rearrange("k p n -> p k n")).then_inc(x_in, 16)
            for s in range(2):
                sp.dma_start(raw(s), units[s]).then_inc(raw_in[s], 16)
            with sp.Fori(1, UNITS // 2) as i:
                for s in range(2):
                    sp.wait_ge(w_lo, 2 * i + (s - 1))
                    sp.dma_start(raw(s), units[2 * i + s]).then_inc(raw_in[s], 16)

        @block.gpsimd
        def _(pool):
            chain = Chain(pool, pool_chain)
            for t in range(2 * CB):
                if t >= 2:
                    pool.wait_ge(mod_part, 2 * (t - 1))
                pool.dma_start(f(F_MD + (t % 2) * L), modw[t // CB, t % CB]).then_inc(mod_in[t % 2], 16)
            pool.wait_ge(silu_c, 2)
            pool.wait_ge(mod_part, 2 * 2 * CB)
            for t in range(10):
                for k in range(2):
                    pool.dma_start(f(F_MD + k * L), modw[t + 2, k]).then_inc(mod_in[k], 16)
                for k in range(CB):
                    pool.wait_ge(mod_in[k % 2], 16 * (CB + 1) + t * (16 * CB // 2) + 16 * (k // 2))
                    part = f(F_MD + (k % 2) * L)
                    acc = f(F_MD + 2 * L)
                    if k == 0:
                        pool.wait_ge(mod_mm, t + 2)
                        chain(pool.tensor_scalar(acc, part, S[:, C_SC:C_SC + 1], 1.0, MUL, MUL))
                    else:
                        chain(pool.tensor_scalar(part, part, S[:, C_SC + k:C_SC + k + 1], 1.0, MUL, MUL))
                        add = pool.tensor_tensor(acc, acc, part, ADD)
                        if k < CB - 1:
                            chain(add)
                        else:
                            add.then_inc(mod_acc, 1)
                            pool.wait_ge(mod_acc, t + 1)
                    if k + 2 < CB:
                        pool.dma_start(part, modw[t + 2, k + 2]).then_inc(mod_in[k % 2], 16)

        @block.scalar
        def _(act):
            n_sq, n_norm, n_h, n_act = [0], [0], [0], [0]


            def copy(out, in_, scale=1.0):
                return act.activation(out, in_, ACT.Copy, scale=scale)

            def raw_count(u):
                return 16 * (u // 2 + 1)

            def split(u):
                if u >= UNITS:
                    return
                act.wait_ge(raw_in[u % 2], raw_count(u))
                if prior(u) >= 0:
                    by, count = freed(prior(u))
                    act.wait_ge({"mm": mm_done, "pj": pj_done, "dn": dn_done}[by], count)
                copy(w(slot_of(u), 0), raw(u % 2)).then_inc(w_hi, 1)

            def square(src, n=L):
                wait(act, sq_used, n_sq[0] - 1)
                out = f(F_SQ + (n_sq[0] % 2) * L, n)
                act.activation(out, src, ACT.Square).then_inc(sq_ready, 1)
                n_sq[0] += 1

            def std(src, dst, width):
                act.wait_ge(sums_out, n_norm[0] + 1)
                act.activation(dst, src, ACT.Sqrt, scale=1.0 / width, bias=S[:, C_EPS:C_EPS + 1]).then_inc(std_ready, 1)
                n_norm[0] += 1

            def h_parts(src, dst, shift, func=None):
                n_h[0] += 1
                act.wait_ge(ht_ready, n_h[0])
                if func is not None:
                    act.activation(src, src, func, bias=shift).then_inc(h_act, 1)
                    n_act[0] += 1
                    act.wait_ge(h_act, n_act[0])
                    copy(dst, src).then_inc(h_hi, 1)
                else:
                    act.activation(dst, src, ACT.Identity, bias=shift).then_inc(h_hi, 1)

            act.wait_ge(small_in, 32)
            act.wait_ge(const_set, 3)
            act.activation(S[:, C_SC:C_SC + CB], V[:, V_C:V_C + CB], ACT.Silu).then_inc(silu_c, 1)
            act.activation(S[:, C_SC + CB:C_SC + 2 * CB], V[:, V_CCTX:V_CCTX + CB], ACT.Silu).then_inc(silu_c, 1)
            act.wait_ge(ctx_in, 16)
            for k in range(CB):
                square(f(F_T + k * CTX, CTX), CTX)
            act.wait_ge(x_in, 32)
            for k in range(CB):
                square(A(k))
            std(SUMSX, RTX, D)
            std(SUMS, RT, D)
            for u in range(3):
                split(u)
            for k in range(CB):
                h_parts(sq(k), h(k, 0), S[:, C_MOD + k:C_MOD + k + 1])
            for k in range(CB):
                h_parts(f(F_SQ + (k % 2) * L, CTX), hx(k, 0), S[:, C_MODX + k:C_MODX + k + 1])

            for n in range(6):
                if n < 3:
                    split(n + 3)
                act.wait_ge(mm_done, M_DQKV + n + 1)
                if n < 3:
                    copy(CQ[n], pair(n)).then_inc(mm_free, 1)
                    if n == 0:
                        act.dma_start(COSD, cosd_d).then_inc(table_in, 16)
                        act.dma_start(SIND, sind_d).then_inc(table_in, 16)
                elif n == 3:
                    act.wait_ge(mmx_done, 1)
                    act.activation(f(3072, CTX), bank(4, CTX), ACT.Copy).then_inc(latent_in, 1)
                    copy(f(3072 + CTX), pair(n)).then_inc(mm_free, 1)
            split(U_HEAD)
            act.wait_ge(mm_free, 4)
            act.wait_ge(latent_in, 1)
            for k in range(QLORA_B):
                square(CQ[k])
            std(SUMS, RT, QLORA_B * P)
            act.wait_ge(sq_used, n_sq[0])
            act.wait_ge(rstd_ready, n_norm[0])
            act.wait_ge(rope_k, 1)
            act.activation(f(F_SQ, KEYS), CKV, ACT.Square).then_inc(ckv_sq, 1)
            copy(r(R_KR, KEYS), KRF).then_inc(lat_hi, 1)
            for k in range(QLORA_B):
                act.wait_ge(lat_lo, k + 1)
                copy(r(R_CQ + k * L), CQ[k]).then_inc(lat_hi, 1)
            act.wait_ge(sums_out, n_norm[0] + 1)
            act.activation(f(F_RT, KEYS), PS[:, 4 * HALF:4 * HALF + KEYS], ACT.Sqrt, scale=1.0 / P,
                           bias=S[:, C_EPS:C_EPS + 1]).then_inc(std_ready, 1)
            n_norm[0] += 1
            act.wait_ge(lat_lo, QLORA_B + 1)
            copy(r(R_CKV, KEYS), CKV).then_inc(lat_hi, 1)
            act.dma_start(CS, cs_d).then_inc(table_in, 16)

            def proj_hi(head, par, arrivals, par_next):
                for i, (kind, start, width) in enumerate(PIECES):
                    if kind == "qr":
                        act.wait_ge(pj_t, 2 * head + (start // HALF + 1))
                        src = ROPET[start // HALF]
                    else:
                        act.wait_ge(pj_done, 10 * head + (i + 1))
                        src = bank(6 + i % 2, width)
                    copy(piece_at(kind, par, start, width, 0), src).then_inc(pj_hi, 1)
                act.wait_ge(raw_in[par_next], arrivals)
                if isinstance(head, int) and head == 0:
                    act.wait_ge(mm_done, M_DQKV + 6)
                else:
                    act.wait_ge(pj_done, 10 * head)
                copy(w(par_next, 0), raw(par_next)).then_inc(w_hi, 1)

            def exps(n, par, s):
                act.wait_ge(s_max, 4 * n + (s + 1))
                c = (par % 2) * 4 + s
                act.activation(Pt(par, s), PS[:, 0:KEYS], ACT.Exp, bias=S[:, C_NM + c:C_NM + c + 1], scale=SCALE,
                               accum_out=S[:, C_RS + c:C_RS + c + 1]).then_inc(s_free, 1)

            def tp_copy(n, par, kb):
                kbn = NKB * par + kb
                act.wait_ge(tp_done, NKB * n + (kb + 1))
                act.wait_ge(pt_free, NKB * n + (kb + 1))
                copy(r(R_PT + (kbn % 4) * L, HALF), bank(3 + kbn % 2)).then_inc(tp_hi, 1)

            def out_copy(n, par, head):
                act.wait_ge(pt_free, NKB * n + (4 + NKB))
                half = par % 2
                act.wait_ge(o_stored[half], 16 * head + 16)
                copy(OST[half], bank(5)).then_inc(o_free, 1)
                act.wait_ge(o_free, n + 2)
                act.dma_start(os_d[head, :, half * HALF:(half + 1) * HALF], OST[half]).then_inc(o_stored[half], 16)

            def step(n, par, i, last=False):
                for s in range(4):
                    if not last:
                        exps(n, par, s)
                        if s == 3 and par % 2 == 1 and not (isinstance(n, int) and n == 15):
                            c = (par + 1) // 2
                            proj_hi(2 * i + c, c % 2, 16 * i + raw_count(U_HEAD + c + 1), (c + 1) % 2)
                    for kb in TP_AFTER[s]:
                        tp_copy(n - 1, par - 1, kb)
                out_copy(n - 1, par - 1, 2 * i + (par - 1) // 2)

            proj_hi(0, 0, raw_count(U_HEAD + 1), 1)
            for s in range(4):
                exps(0, 0, s)
            with act.Fori(0, 3) as i:
                for q in range(1, 5):
                    step(4 * i + q, q, i)
            for q in range(1, 4):
                step(12 + q, q, 3)
            step(16, 4, 3, last=True)
            for u in (U_WO + 1, U_WO + 2):
                split(u)
            for half in range(2):
                act.wait_ge(o_stored[half], 16 * HEADS + 16)
            for k in range(CB):
                act.dma_start(A(k), os_d[k]).then_inc(blk_in[k], 16)
            for k in range(CB):
                act.wait_ge(blk_in[k], 16)
                copy(h(k, 0), A(k)).then_inc(h_hi, 1)

            def y_blocks(u0, m0, bias):
                for n in range(CB):
                    split(u0 + n + 3)
                    act.wait_ge(mm_done, m0 + n + 1)
                    if bias is None:
                        copy(A(n), pair(n)).then_inc(mm_free, 1)
                    else:
                        act.activation(A(n), pair(n), ACT.Identity, bias=V[:, bias + n:bias + n + 1]).then_inc(mm_free, 1)
                    act.wait_ge(mm_free, m0 + n + 1)
                    square(A(n))

            def residual(b, x_src, out_dst, more, shift):
                if b:
                    act.wait_ge(blk_out, 16 * CB * b)
                for k in range(2):
                    act.dma_start(f(F_T + k * L), x_src[k]).then_inc(blk_in[k], 16)
                std(SUMS, RT, D)
                for k in range(CB):
                    act.wait_ge(y_new, CB * b + k + 1)
                    act.dma_start(out_dst[k], A(k)).then_inc(blk_out, 16)
                    if k + 2 < CB:
                        act.dma_start(f(F_T + (k % 2) * L), x_src[k + 2]).then_inc(blk_in[k + 2], 16)
                    if more:
                        square(A(k))
                if more:
                    std(SUMS, RT, D)
                    for k in range(CB):
                        h_parts(sq(k), h(k, 0), S[:, shift + k:shift + k + 1])

            y_blocks(U_WO, M_WO, None)
            residual(0, xT, xs_d, True, C_MOD + 3 * CB)

            def ffn(layer, b):
                u0, m0, j0, d0 = U_FFN[layer], M_FFN[layer], FB * layer, DN_START + CB * GROUPS * layer

                def splitr(i, c):
                    u = u0 + c
                    act.wait_ge(raw_in[u % 2], 96 * i + raw_count(u))
                    by, count = freed(prior(u))
                    if by == "mm":
                        act.wait_ge(mm_done, 8 * i + count)
                    if by == "dn" or c < 8:
                        act.wait_ge(dn_done, 2 * CB * i + (count if by == "dn" else d0))
                    copy(w(slot_of(u), 0), raw(u % 2)).then_inc(w_hi, 1)

                def g_part(i, j, g):
                    if j % 2 == 0:
                        wait(act, dn_done, 2 * CB * i + (d0 + CB * (g - 1)))
                    act.wait_ge(gp_ready, 4 * i + (j0 + j + 1))
                    copy(G(g, j % 2, 0), f(F_T + L)).then_inc(g_hi, 1)

                def up(i, g, q):
                    m, j, val = m0 + 4 * g + q, 2 * g + q // 2, q % 2
                    mi, ji = 8 * i + m, 4 * i + j
                    act.wait_ge(mm_done, mi + 1)
                    col = ji + FB * val
                    if val:
                        if not (isinstance(i, int) and j0 + j == 0):
                            act.wait_ge(g_lo, ji + j0)
                    elif not (isinstance(i, int) and j0 + j == 0):
                        act.wait_ge(gp_ready, ji + j0)
                    wv = V_FW + layer * 3 * 2 * FB
                    act.activation(f(F_T + val * L), pair(q), ACT.Identity, scale=V[:, bass.ds(wv + 2 * FB + col, 1)],
                                   bias=V[:, bass.ds(V_FB + layer * 2 * FB + col, 1)]).then_inc(tap_done, 1)
                    if not val:
                        if not (isinstance(i, int) and j == 0):
                            g_part(i, j - 1, (j - 1) // 2)
                        act.wait_ge(mm_free, mi + 1)
                        act.activation(f(F_T), f(F_T), ACT.Silu).then_inc(silu_g, 1)

                for q in range(4):
                    if q < 3:
                        split(u0 + q + 3)
                    up(0, 0, q)
                with act.Fori(0, (GROUPS - 1) // 2) as i:
                    for g in (1, 2):
                        n0 = 4 + 6 * (g - 1)
                        splitr(i, n0 + 2)
                        for q in range(4):
                            splitr(i, n0 + q + 3)
                            up(i, g, q)
                        splitr(i, n0 + 7)
                g_part(0, FB - 1, GROUPS - 1)
                split(u0 + 66)
                split(u0 + 67)
                for c in range(CB):
                    act.wait_ge(dn_free, d0 + CB * (GROUPS - 1) + c + 1)
                    square(A(c))
                split(u0 + 68)

            ffn(0, 1)
            residual(1, xs_d, xs_d, True, C_MOD + MODS)

            for i in range(CB):
                split(U_PW1 + 2 * i + 3)
                split(U_PW1 + 2 * i + 4)
                act.wait_ge(mm_done, M_PW1 + 2 * i + 2)
                act.activation(f(F_SQ + L), pair(1), ACT.Sigmoid,
                               bias=V[:, V_BPW1 + CB + i:V_BPW1 + CB + i + 1]).then_inc(sig_ready, 1)
            act.wait_ge(sums_out, n_norm[0] + 1)
            act.activation(RT, SUMS, ACT.Copy, scale=1.0 / D).then_inc(std_ready, 1)
            n_norm[0] += 1
            for k in range(CB):
                act.wait_ge(y_ready, k + 1)
                square(A(k))
            std(SUMS, RT, D)
            for k in range(CB):
                h_parts(sq(k), h(k, 0), V[:, V_BLN + k:V_BLN + k + 1], ACT.Silu)
            y_blocks(U_PW2, M_PW2, V_BPW2)
            residual(2, xs_d, xs_d, True, C_MOD + MODS + 3 * CB)
            ffn(1, 3)
            residual(3, xs_d, outT, False, None)
            act.wait_ge(blk_out, 16 * CB * 4)

        @block.vector
        def _(dve):
            n_sq, n_norm, n_h, n_rstd = [0], [0], [0], [0]
            chain = Chain(dve, dve_chain)

            def split(u):
                if u >= UNITS:
                    return
                dve.wait_ge(w_hi, u + 1)
                dve.tensor_tensor(w(slot_of(u), 1), raw(u % 2), w(slot_of(u), 0), SUB).then_inc(w_lo, 1)

            def add_square(first, acc, n=L):
                dve.wait_ge(sq_ready, n_sq[0] + 1)
                src = f(F_SQ + (n_sq[0] % 2) * L, n)
                if first:
                    dve.tensor_copy(acc, src).then_inc(sq_used, 1)
                else:
                    wait(dve, sq_used, n_sq[0])
                    dve.tensor_tensor(acc, acc, src, ADD).then_inc(sq_used, 1)
                n_sq[0] += 1

            def rstd(dst):
                dve.wait_ge(std_ready, n_norm[0] + 1)
                n_norm[0] += 1
                n_rstd[0] += 1
                dve.reciprocal(dst, dst).then_inc(rstd_ready, 1)
                dve.wait_ge(rstd_ready, n_rstd[0])

            def h_blocks(src, gain, rt, dst_hi, dst_lo, shift, n=L, done=None):
                def lo(k):
                    dve.wait_ge(h_hi, n_h[0] + k + 1)
                    t = f(F_SQ + (k % 2) * L, n)
                    if shift is None:
                        dve.tensor_tensor(dst_lo(k), t, dst_hi(k), SUB).then_inc(h_lo, 1)
                    else:
                        dve.scalar_tensor_tensor(out=dst_lo(k), in0=t, scalar=shift(k), in1=dst_hi(k), op0=ADD, op1=SUB).then_inc(h_lo, 1)
                for k in range(CB):
                    if k >= 2:
                        dve.wait_ge(h_lo, n_h[0] + k - 1)
                    dve.scalar_tensor_tensor(out=f(F_SQ + (k % 2) * L, n), in0=src(k), scalar=gain(k), in1=rt,
                                             op0=MUL, op1=MUL).then_inc(ht_ready, 1)
                    if k >= 1:
                        lo(k - 1)
                lo(CB - 1)
                n_h[0] += CB
                dve.wait_ge(h_lo, n_h[0])

            dve.memset(ones[:, :], 1.0).then_inc(const_set, 1)
            dve.memset(S[:, :], 0.0).then_inc(const_set, 1)
            dve.wait_ge(const_set, 2)
            dve.memset(S[:, C_EPS:C_EPS + 1], EPS).then_inc(const_set, 1)
            dve.wait_ge(small_in, 32)
            ACCX = f(F_ACCX, CTX)
            for k in range(CB):
                add_square(k == 0, ACCX, CTX)
            for k in range(CB):
                add_square(k == 0, f(F_ACC))
            rstd(RTX)
            rstd(RT)
            dve.wait_ge(silu_c, 2)
            for t in range(2 * CB):
                vec, k = t // CB, t % CB
                dve.wait_ge(mod_in[t % 2], 16 * (t // 2 + 1))
                for s, acc in enumerate((f(F_MD + 2 * L), f(F_SQ))):
                    col = S[:, C_SC + s * CB + k:C_SC + s * CB + k + 1]
                    if k == 0:
                        wait(dve, mod_mm, vec)
                        dve.tensor_scalar(acc, f(F_MD + (t % 2) * L), col, None, MUL).then_inc(mod_part, 1)
                    else:
                        dve.wait_ge(mod_part, 2 * t - 1 + s)
                        dve.scalar_tensor_tensor(out=acc, in0=f(F_MD + (t % 2) * L), scalar=col, in1=acc,
                                                 op0=MUL, op1=ADD).then_inc(mod_part, 1)
                if k == CB - 1:
                    dve.wait_ge(mod_mm, vec + 1)
                    b = V[:, V_BMOD + vec * CB:V_BMOD + (vec + 1) * CB]
                    chain(dve.tensor_tensor(S[:, C_MOD + vec * CB:C_MOD + (vec + 1) * CB], bank(7, CB), b, ADD))
                    dve.tensor_tensor(S[:, C_MODX + vec * CB:C_MODX + (vec + 1) * CB], bank(7, CB, CB), b, ADD).then_inc(mod_out, 1)
                    dve.wait_ge(mod_out, vec + 1)

            def gain(dst, g, mod, one):
                chain(dve.scalar_tensor_tensor(out=S[:, dst:dst + CB], in0=S[:, mod:mod + CB], scalar=float(one),
                                               in1=V[:, g:g + CB], op0=ADD, op1=MUL))

            gain(C_AV, V_PREMIX, C_MOD + CB, 1)
            gain(C_AX, V_PREMIX, C_MODX + CB, 1)

            def col(at):
                return lambda k: S[:, at + k:at + k + 1]

            for u in range(3):
                split(u)
            h_blocks(A, col(C_AV), RT, lambda k: h(k, 0), lambda k: h(k, 1), col(C_MOD))
            h_blocks(lambda k: f(F_T + k * CTX, CTX), col(C_AX), RTX, lambda k: hx(k, 0), lambda k: hx(k, 1), col(C_MODX), CTX)

            for n in range(6):
                if n < 3:
                    split(n + 3)
            dve.wait_ge(table_in, 32)
            dve.wait_ge(mmx_done, 2)
            chain(dve.tensor_copy(f(4352, CTX), bank(5, CTX)))
            dve.wait_ge(mm_done, M_DQKV + 5)
            dve.wait_ge(mm_free, M_DQKV + 4)
            dve.tensor_tensor(f(4352 + CTX), pair(0), COSD, MUL).then_inc(mm_free, 1)
            dve.wait_ge(mm_done, M_DQKV + 6)
            dve.tensor_tensor(f(F_T), pair(1), SIND, MUL).then_inc(mm_free, 1)
            dve.wait_ge(mm_free, 6)
            dve.tensor_tensor(f(4352 + CTX), f(4352 + CTX), f(F_T), ADD).then_inc(rope_k, 1)
            split(U_HEAD)
            for k in range(QLORA_B):
                add_square(k == 0, f(F_ACC))
            rstd(RT)
            dve.wait_ge(lat_hi, 1)
            chain(dve.tensor_tensor(r(R_KR + KEYS, KEYS), KRF, r(R_KR, KEYS), SUB))
            for k in range(QLORA_B):
                dve.scalar_tensor_tensor(out=CQ[k], in0=CQ[k], scalar=V[:, V_GQ + k:V_GQ + k + 1], in1=RT,
                                         op0=MUL, op1=MUL).then_inc(lat_lo, 1)
            for k in range(QLORA_B):
                dve.wait_ge(lat_hi, k + 2)
                chain(dve.tensor_tensor(r(R_CQ + (QLORA_B + k) * L), CQ[k], r(R_CQ + k * L), SUB))
            rstd(f(F_RT, KEYS))
            dve.scalar_tensor_tensor(out=CKV, in0=CKV, scalar=V[:, V_GKV:V_GKV + 1], in1=f(F_RT, KEYS),
                                     op0=MUL, op1=MUL).then_inc(lat_lo, 1)
            dve.wait_ge(lat_hi, QLORA_B + 2)
            dve.tensor_tensor(r(R_CKV + KEYS, KEYS), CKV, r(R_CKV, KEYS), SUB).then_inc(lat_lo, 1)
            dve.wait_ge(lat_lo, QLORA_B + 2)
            dve.wait_ge(table_in, 48)

            def proj_lo(head, par):
                for i, (kind, start, width) in enumerate(PIECES):
                    if kind == "qr":
                        half = start // HALF
                        dve.wait_ge(pj_done, 10 * head + (i + 1))
                        dve.tensor_tensor(ROPET[half], bank(6 + i % 2), CS[:, start:start + HALF], MUL).then_inc(pj_t, 1)
                        src = ROPET[half]
                    else:
                        src = bank(6 + i % 2, width)
                    dve.wait_ge(pj_hi, 10 * head + (i + 1))
                    dve.tensor_tensor(piece_at(kind, par, start, width, 1), src,
                                      piece_at(kind, par, start, width, 0), SUB).then_inc(pj_free, 1)
                dve.wait_ge(w_hi, U_HEAD + 2 + head)
                other = (par + 1) % 2
                dve.tensor_tensor(w(other, 1), raw(other), w(other, 0), SUB).then_inc(w_lo, 1)

            def maxes(n, par, s):
                c = (par % 2) * 4 + s
                dve.wait_ge(s_done, 4 * n + (s + 1))
                chain(dve.reduce_max(S[:, C_MX + c:C_MX + c + 1], PS[:, 0:KEYS], AX.X))
                dve.tensor_scalar(S[:, C_NM + c:C_NM + c + 1], S[:, C_MX + c:C_MX + c + 1], -SCALE, None, MUL).then_inc(s_max, 1)

            def scales(n, par, s):
                c = (par % 2) * 4 + s
                dve.wait_ge(s_free, 4 * n + (s + 1))
                chain(dve.reciprocal(S[:, C_RI + c:C_RI + c + 1], S[:, C_RS + c:C_RS + c + 1]))
                dve.tensor_scalar(Pt(par, s), Pt(par, s), S[:, C_RI + c:C_RI + c + 1], None, MUL).then_inc(p_ready, 1)

            def tp_sub(n, par, kb):
                kbn = NKB * par + kb
                dve.wait_ge(tp_hi, NKB * n + (kb + 1))
                at = R_PT + (kbn % 4) * L
                dve.tensor_tensor(r(at + HALF, HALF), bank(3 + kbn % 2), r(at, HALF), SUB).then_inc(tp_lo, 1)

            def mod_add(t, dst):
                dve.wait_ge(mod_mm, t + 3)
                dve.tensor_tensor(S[:, bass.ds(C_MOD + dst, CB)], bank(7, CB), V[:, bass.ds(V_BMOD + dst, CB)],
                                  ADD).then_inc(mod_out, 1)

            def step(n, par, i, last=False):
                for s in range(4):
                    if not last:
                        maxes(n, par, s)
                        if s == 3 and par % 2 == 1 and not (isinstance(n, int) and n == 15):
                            proj_lo(2 * i + (par + 1) // 2, ((par + 1) // 2) % 2)
                    for kb in TP_AFTER[s]:
                        tp_sub(n - 1, (par - 1) % 4, kb)
                    if not last:
                        scales(n, par, s)
                if par == 2:
                    mod_add(i, CB * i + 2 * CB)

            proj_lo(0, 0)
            for s in range(4):
                maxes(0, 0, s)
                scales(0, 0, s)
            with dve.Fori(0, 3) as i:
                chain.enter(i, 32)
                for q in range(1, 5):
                    step(4 * i + q, q, i)
                chain.leave(3)
            for q in range(1, 4):
                step(12 + q, q, 3)
            step(16, 4, 3, last=True)
            dve.wait_ge(mod_out, 6)
            for u in (U_WO + 1, U_WO + 2):
                split(u)
            for k in range(CB):
                dve.wait_ge(h_hi, n_h[0] + k + 1)
                dve.tensor_tensor(h(k, 1), A(k), h(k, 0), SUB).then_inc(h_lo, 1)
            n_h[0] += CB
            dve.wait_ge(h_lo, n_h[0])

            def y_blocks(u0):
                for n in range(CB):
                    split(u0 + n + 3)
                    add_square(n == 0, f(F_ACC))

            def residual(b, g_post, gate, more, g_pre, scale, shift):
                gain(C_GV, g_post, gate, 0)
                if more:
                    gain(C_AV, g_pre, scale, 1)
                rstd(RT)
                for k in range(CB):
                    chain(dve.scalar_tensor_tensor(out=A(k), in0=A(k), scalar=S[:, C_GV + k:C_GV + k + 1], in1=RT, op0=MUL, op1=MUL))
                    dve.wait_ge(blk_in[k], 16 * (b + 2))
                    dve.tensor_tensor(A(k), A(k), f(F_T + (k % 2) * L), ADD).then_inc(y_new, 1)
                    if more and k >= 1:
                        add_square(k == 1, f(F_ACC))
                if more:
                    add_square(False, f(F_ACC))
                    rstd(RT)
                    h_blocks(A, col(C_AV), RT, lambda k: h(k, 0), lambda k: h(k, 1), col(shift))

            y_blocks(U_WO)
            residual(0, V_POSTMIX, C_MOD + 2 * CB, True, V_PREFFN, C_MOD + 4 * CB, C_MOD + 3 * CB)

            def ffn(layer, b):
                u0, m0, j0, d0 = U_FFN[layer], M_FFN[layer], FB * layer, DN_START + CB * GROUPS * layer

                def splitr(i, c):
                    u = u0 + c
                    dve.wait_ge(w_hi, 12 * i + (u + 1))
                    dve.tensor_tensor(w(slot_of(u), 1), raw(u % 2), w(slot_of(u), 0), SUB).then_inc(w_lo, 1)

                def g_part(i, j, g):
                    ji = 4 * i + j
                    dve.wait_ge(g_hi, ji + (j0 + 1))
                    dve.tensor_tensor(G(g, j % 2, 1), f(F_T + L), G(g, j % 2, 0), SUB).then_inc(g_lo, 1)

                def up(i, g, q):
                    m, j, val = m0 + 4 * g + q, 2 * g + q // 2, q % 2
                    mi, ji = 8 * i + m, 4 * i + j
                    c = ji + FB * val
                    wv = V_FW + layer * 6 * FB
                    at = F_T + val * L
                    dve.wait_ge(tap_done, 8 * i + (2 * FB * layer + 4 * g + q + 1))
                    chain(dve.scalar_tensor_tensor(out=f(at + 1, L - 1), in0=PS[:, (q % 2) * L:(q % 2) * L + L - 1],
                                                   scalar=V[:, bass.ds(wv + c, 1)], in1=f(at + 1, L - 1), op0=MUL, op1=ADD))
                    dve.scalar_tensor_tensor(out=f(at, L - 1), in0=PS[:, (q % 2) * L + 1:(q % 2) * L + L],
                                             scalar=V[:, bass.ds(wv + 4 * FB + c, 1)], in1=f(at, L - 1), op0=MUL, op1=ADD).then_inc(mm_free, 1)
                    if val:
                        dve.wait_ge(silu_g, ji + (j0 + 1))
                        dve.wait_ge(mm_free, mi + 1)
                        dve.tensor_tensor(f(F_T + L), f(F_T + L), f(F_T), MUL).then_inc(gp_ready, 1)
                    elif not (isinstance(i, int) and j == 0):
                        g_part(i, j - 1, (j - 1) // 2)

                def down(i, g):
                    dve.wait_ge(dn_free, 2 * CB * i + (d0 + CB * g))
                    for c in range(CB):
                        dve.wait_ge(dn_done, 2 * CB * i + (d0 + CB * g + c + 1))
                        dve.tensor_tensor(A(c), A(c), dn(c), ADD).then_inc(dn_free, 1)

                mods = layer == 0
                if mods:
                    mod_add(4, CB * 4 + 2 * CB)
                for q in range(4):
                    if q < 3:
                        split(u0 + q + 3)
                    up(0, 0, q)
                dve.wait_ge(blk_out, 16 * CB * b)
                for c in range(CB):
                    dve.memset(A(c), 0.0).then_inc(y_zero, 1)
                dve.wait_ge(y_zero, CB * (layer + 1))
                with dve.Fori(0, (GROUPS - 1) // 2) as i:
                    chain.enter(i, 8)
                    for g in (1, 2):
                        n0 = 4 + 6 * (g - 1)
                        splitr(i, n0 + 2)
                        for q in range(4):
                            splitr(i, n0 + q + 3)
                            up(i, g, q)
                            if mods and g == 1 and q == 0:
                                mod_add(i + 5, CB * i + 7 * CB)
                        splitr(i, n0 + 7)
                        down(i, g - 1)
                    chain.leave((GROUPS - 1) // 2)
                g_part(0, FB - 1, GROUPS - 1)
                split(u0 + 66)
                split(u0 + 67)
                dve.wait_ge(dn_free, d0 + CB * (GROUPS - 1))
                for c in range(CB):
                    dve.wait_ge(dn_done, d0 + CB * (GROUPS - 1) + c + 1)
                    dve.tensor_tensor(A(c), A(c), dn(c), ADD).then_inc(dn_free, 1)
                    if c >= 1:
                        add_square(c == 1, f(F_ACC))
                add_square(False, f(F_ACC))
                split(u0 + 68)

            ffn(0, 1)
            dve.wait_ge(mod_out, 12)
            residual(1, V_POSTFFN, C_MOD + 5 * CB, True, V_PREMIX + CB, C_MOD + MODS + CB, C_MOD + MODS)

            U = [f(F_T, L + 2 * PAD), f(F_T + L + 2 * PAD, L + 2 * PAD)]
            for s in range(2):
                chain(dve.memset(U[s][:, 0:PAD], 0.0))
                chain(dve.memset(U[s][:, PAD + L:], 0.0))
            dve.wait_ge(blk_out, 16 * CB * 2)
            for i in range(CB):
                split(U_PW1 + 2 * i + 3)
                split(U_PW1 + 2 * i + 4)
                dve.wait_ge(sig_ready, i + 1)
                dve.scalar_tensor_tensor(out=U[i % 2][:, PAD:PAD + L], in0=pair(0), scalar=V[:, V_BPW1 + i:V_BPW1 + i + 1],
                                         in1=f(F_SQ + L), op0=ADD, op1=MUL).then_inc(mm_free, 2)
                dve.wait_ge(mm_free, M_PW1 + 2 * i + 2)
                chain(dve.tensor_scalar(A(i), U[i % 2][:, 0:L], V[:, V_WDW + i:V_WDW + i + 1], V[:, V_BDW + i:V_BDW + i + 1], MUL, ADD))
                for t in range(1, TAPS):
                    op = dve.scalar_tensor_tensor(out=A(i), in0=U[i % 2][:, t:t + L],
                                                  scalar=V[:, V_WDW + t * CB + i:V_WDW + t * CB + i + 1], in1=A(i), op0=MUL, op1=ADD)
                    if t < TAPS - 1:
                        chain(op)
                    else:
                        op.then_inc(u_ready, 1)
                        dve.wait_ge(u_ready, i + 1)
                if i == 0:
                    chain(dve.tensor_copy(f(F_ACC), A(i)))
                elif i < CB - 1:
                    chain(dve.tensor_tensor(f(F_ACC), f(F_ACC), A(i), ADD))
                else:
                    dve.tensor_tensor(f(F_ACC), f(F_ACC), A(i), ADD).then_inc(acc_ready, 1)
            dve.wait_ge(std_ready, n_norm[0] + 1)
            n_norm[0] += 1
            for k in range(CB):
                dve.tensor_tensor(A(k), A(k), RT, SUB).then_inc(y_ready, 1)
                if k >= 1:
                    add_square(k == 1, f(F_ACC))
            add_square(False, f(F_ACC))
            rstd(RT)
            h_blocks(A, lambda k: V[:, V_GLN + k:V_GLN + k + 1], RT, lambda k: h(k, 0), lambda k: h(k, 1), None)
            y_blocks(U_PW2)
            residual(2, V_POSTMIX + CB, C_MOD + MODS + 2 * CB, True, V_PREFFN + CB, C_MOD + MODS + 4 * CB, C_MOD + MODS + 3 * CB)
            ffn(1, 3)
            residual(3, V_POSTFFN + CB, C_MOD + MODS + 5 * CB, False, None, None, None)

        @block.tensor
        def _(pe):
            n_sq, n_h = [0], [0]

            def three(out, w_parts, x_parts, first, last):
                (wh, wl), (xh, xl) = w_parts, x_parts
                pe.matmul(out, wl, xh, start=first, stop=False)
                pe.matmul(out, wh, xl, start=False, stop=False)
                return pe.matmul(out, wh, xh, start=False, stop=last)

            def sums(count):
                n_sq[0] += count
                pe.wait_ge(sq_used, n_sq[0])
                for half in range(2):
                    mm = pe.matmul(bank(4 + half), ones[:, :], f(F_ACC + half * HALF, HALF), start=True, stop=True)
                mm.then_inc(sums_out, 1)

            def mod_sums(acc, at=0):
                for c in range(CB):
                    mm = pe.matmul(bank(7, 1, at + c), f(acc + c * P, P), ones[:, 0:1], start=True, stop=True)
                return mm

            def up(u, m, slot, par, ready=None):
                for k in range(CB):
                    if ready is not None:
                        pe.wait_ge(h_lo, ready + k + 1)
                    if k == 0:
                        pe.wait_ge(w_lo, u + 1)
                        if not isinstance(m, int) or m >= 2:
                            pe.wait_ge(mm_free, m - 1)
                    for half in range(2):
                        mm = three(pair(par)[:, half * HALF:(half + 1) * HALF], [w(slot, p, k * P, P) for p in range(2)],
                                   [h(k, p, half) for p in range(2)], k == 0, k == CB - 1)
                mm.then_inc(mm_done, 1)

            pe.wait_ge(const_set, 3)
            pe.sem_inc(pt_free, 4)
            pe.sem_inc(tp_lo, 2)
            pe.sem_inc(o_free, 1)
            for s in range(2):
                pe.sem_inc(o_stored[s], 16)
            pe.sem_inc(dn_done, DN_START)
            pe.sem_inc(dn_free, DN_START)
            n_sq[0] += CB
            pe.wait_ge(sq_used, n_sq[0])
            pe.matmul(SUMSX, ones[:, :], f(F_ACCX, CTX), start=True, stop=True).then_inc(sums_out, 1)
            sums(CB)
            for v in range(2):
                pe.wait_ge(mod_part, 2 * CB * (v + 1))
                wait(pe, mod_out, v)
                mod_sums(F_MD + 2 * L)
                mod_sums(F_SQ, CB).then_inc(mod_mm, 1)

            for n in range(6):
                if n in (3, 4):
                    pe.wait_ge(h_lo, 2 * CB)
                    pe.wait_ge(w_lo, n + 1)
                    for k in range(CB):
                        mm = three(bank(n + 1, CTX), [w(slot_of(n), p, k * P, P) for p in range(2)],
                                   [hx(k, p) for p in range(2)], k == 0, k == CB - 1)
                    mm.then_inc(mmx_done, 1)
                up(U_DQKV + n, M_DQKV + n, slot_of(n), n, 0 if n == 0 else None)
            n_h[0] += 2 * CB
            sums(QLORA_B)
            pe.wait_ge(ckv_sq, 1)
            pe.wait_ge(rstd_ready, 3)
            for at, width in KP:
                mm = pe.matmul(bank(4 + at // HALF, width), ones[:, :], f(F_SQ + at, width), start=True, stop=True)
            mm.then_inc(sums_out, 1)
            pe.wait_ge(lat_lo, QLORA_B + 2)
            pe.wait_ge(rstd_ready, 4)

            def proj(head, par, mods):
                slot = par % 2
                pe.wait_ge(w_lo, head + (U_HEAD + 1))
                for i, (kind, start, width) in enumerate(PIECES):
                    if i >= 2 or not (isinstance(head, int) and head == 0):
                        pe.wait_ge(pj_free, 10 * head + (i - 1))
                    if i == 1:
                        pe.wait_ge(mod_out, mods)
                    out = bank(6 + i % 2, width)
                    if kind == "v":
                        for b in range(width // P):
                            at = start + b * P
                            mm = three(out[:, b * P:(b + 1) * P], [r(R_CKV + p * KEYS + at, P) for p in range(2)],
                                       [w(slot, p, 7 * P, P) for p in range(2)], True, True)
                    elif kind == "k":
                        mm = three(out, [w(slot, p, 6 * P, P) for p in range(2)],
                                   [r(R_CKV + p * KEYS + start, width) for p in range(2)], True, True)
                    else:
                        for kb in range(QLORA_B):
                            mm = three(out, [w(slot, p, (2 * kb + (kind == "qr")) * P, P) for p in range(2)],
                                       [r(R_CQ + (p * QLORA_B + kb) * L + start, width) for p in range(2)],
                                       kb == 0, kb == QLORA_B - 1)
                    mm.then_inc(pj_done, 1)

            def scores(n, par, s, head):
                if s == 0 and par % 2 == 0 or (isinstance(n, int) and n == 0):
                    pe.wait_ge(pj_free, 10 * head + 10)
                if s or not (isinstance(n, int) and n == 0):
                    pe.wait_ge(s_free, 4 * n + s)
                q = (par % 2) * HALF + s * P
                for at, width in KP:
                    three(PS[:, at:at + width], [r(R_Q + p * L + q, P) for p in range(2)],
                          [r(R_K + p * KEYS + at, width) for p in range(2)], True, False)
                    mm = three(PS[:, at:at + width], [r(R_Q + (2 + p) * L + q, P) for p in range(2)],
                               [r(R_KR + p * KEYS + at, width) for p in range(2)], False, True)
                mm.then_inc(s_done, 1)

            def turn(n, par, kb):
                kbn = NKB * par + kb
                if kb == 0:
                    pe.wait_ge(p_ready, 4 * n + 4)
                pe.wait_ge(tp_lo, NKB * n + (kb + 1))
                for s in range(4):
                    mm = pe.transpose(bank(3 + kbn % 2, P, s * P), Pt(par, s)[:, kb * P:(kb + 1) * P], ident[:, :])
                mm.then_inc(tp_done, 1)

            def weigh(n, par, kb):
                kbn = NKB * par + kb
                pe.wait_ge(tp_lo, NKB * n + (kb + 3))
                if kb == 0:
                    pe.wait_ge(o_free, n + 1)
                vs, pt = VS[(par // 2) % 2] + kb * P, R_PT + (kbn % 4) * L
                mm = three(bank(5), [r(vs + p * KEYS, P) for p in range(2)], [r(pt + p * HALF, HALF) for p in range(2)],
                           kb == 0, kb == NKB - 1)
                mm.then_inc(pt_free, 1)

            def step(n, par, i, last=False):
                if par == 2:
                    pe.wait_ge(pj_free, 20 * i + 20)
                    pe.wait_ge(mod_acc, i + 1)
                    mod_sums(F_MD + 2 * L).then_inc(mod_mm, 1)
                for s in range(4):
                    if not last:
                        scores(n, par, s, 2 * i + par // 2)
                        if s == 3 and par % 2 == 1 and not (isinstance(n, int) and n == 15):
                            c = (par + 1) // 2
                            proj(2 * i + c, c, i + (3 if par == 3 else 2))
                    turns, weighs = list(TP_AFTER[s]), list(PV_AFTER[s])
                    while turns or weighs:
                        if turns:
                            turn(n - 1, par - 1, turns.pop(0))
                        if weighs and (not turns or weighs[0] + 2 <= turns[0] - 1 + 1):
                            kb = weighs.pop(0)
                            weigh(n - 1, par - 1, kb)

            proj(0, 0, 2)
            for s in range(4):
                scores(0, 0, s, 0)
            with pe.Fori(0, 3) as i:
                for q in range(1, 5):
                    step(4 * i + q, q, i)
            for q in range(1, 4):
                step(12 + q, q, 3)
            step(16, 4, 3, last=True)

            def boundary(more):
                sums(CB)
                if more:
                    sums(CB)

            for n in range(CB):
                up(U_WO + n, M_WO + n, slot_of(U_WO + n), n, n_h[0] if n == 0 else None)
            n_h[0] += CB
            boundary(True)

            def ffn(layer):
                u0, m0, j0, d0 = U_FFN[layer], M_FFN[layer], FB * layer, DN_START + CB * GROUPS * layer

                def mods(t, i):
                    pe.wait_ge(dn_free, 2 * CB * i + d0)
                    pe.wait_ge(mod_acc, t + 1)
                    mod_sums(F_MD + 2 * L).then_inc(mod_mm, 1)

                def down(i, g, u, taken=None):
                    pe.wait_ge(w_lo, 12 * i + (u + 2))
                    pe.wait_ge(g_lo, 4 * i + (j0 + 2 * g + 2))
                    if taken is not None:
                        pe.wait_ge(mod_out, taken)
                    for c in range(CB):
                        pe.wait_ge(dn_free, 2 * CB * i + (d0 + CB * g + c - 1))
                        for jj in range(2):
                            for half in range(2):
                                mm = three(dn(c)[:, half * HALF:(half + 1) * HALF],
                                           [w(slot_of(u + jj), p, c * P, P) for p in range(2)],
                                           [G(g, jj, p, half) for p in range(2)], jj == 0, jj == 1)
                        mm.then_inc(dn_done, 1)

                if layer == 0:
                    mods(4, 0)
                for q in range(4):
                    up(u0 + q, m0 + q, slot_of(u0 + q), q, n_h[0] if q == 0 else None)
                with pe.Fori(0, (GROUPS - 1) // 2) as i:
                    for g in (1, 2):
                        n0 = u0 + 4 + 6 * (g - 1)
                        if layer == 0 and g == 1:
                            mods(i + 5, i)
                        for q in range(4):
                            up(12 * i + (n0 + q), 8 * i + (m0 + 4 * g + q), slot_of(n0 + q), q)
                        down(i, g - 1, n0 + 4, i + 8 if layer == 0 else None)
                down(0, GROUPS - 1, u0 + 64)
                n_h[0] += CB

            ffn(0)
            boundary(True)
            for n in range(2 * CB):
                up(U_PW1 + n, M_PW1 + n, slot_of(U_PW1 + n), n, n_h[0] if n == 0 else None)
            n_h[0] += CB
            pe.wait_ge(acc_ready, 1)
            for half in range(2):
                mm = pe.matmul(bank(4 + half), ones[:, :], f(F_ACC + half * HALF, HALF), start=True, stop=True)
            mm.then_inc(sums_out, 1)
            sums(CB)
            for n in range(CB):
                up(U_PW2 + n, M_PW2 + n, slot_of(U_PW2 + n), n, n_h[0] if n == 0 else None)
            n_h[0] += CB
            boundary(True)
            ffn(1)
            boundary(False)


def rope_tables(np):
    quarter = ROPE // 4
    pos = np.arange(L)
    inv = (np.float32(10000.0) ** (-np.arange(quarter, dtype=np.float32) / np.float32(quarter))).astype(np.float32)
    rows = (pos // GRID_W).astype(np.float32)[:, None] * inv
    cols = (pos % GRID_W).astype(np.float32)[:, None] * inv
    angle = np.concatenate([rows, rows, cols, cols], axis=-1).T
    sign = np.tile(np.repeat(np.array([-1.0, 1.0], np.float32), quarter), 2)[:, None]
    return np.cos(angle).astype(np.float32), (np.sin(angle) * sign).astype(np.float32)


def up_units(np, w):
    n = w.shape[1] // P
    return np.ascontiguousarray(w.reshape(CB, P, n, P).transpose(2, 1, 0, 3)).reshape(n, P, D)


def pack_units(np, i):
    swap = np.arange(ROPE).reshape(2, 2, ROPE // 4)[:, ::-1].reshape(-1)
    dqkv = i["mla_w_dqkv"][0]
    kr = dqkv[:, 512:576]
    stream = [up_units(np, dqkv[:, :512]), up_units(np, np.concatenate([kr, kr], 1)),
              up_units(np, np.concatenate([kr[:, swap], kr[:, swap]], 1))]
    uq = i["mla_w_uq"][0].reshape(QLORA_B, P, HEADS, 192)
    ukv = i["mla_w_ukv"][0].reshape(P, HEADS, 256)
    for hd in range(HEADS):
        q = uq[:, :, hd]
        q = np.concatenate([q, q[:, :, 128:][:, :, swap]], -1).transpose(1, 0, 2).reshape(P, 768)
        stream.append(np.concatenate([q, ukv[:, hd]], -1)[None])
    stream.append(up_units(np, i["mla_w_o"][0]))

    def ffn(layer):
        ups, downs = up_units(np, i["ffn_w_up"][layer]), i["ffn_w_down"][layer].reshape(FB, P, D)
        out = []
        for g in range(GROUPS + 1):
            if g < GROUPS:
                out += [ups[2 * g], ups[FB + 2 * g], ups[2 * g + 1], ups[FB + 2 * g + 1]]
            if g:
                out += [downs[2 * g - 2], downs[2 * g - 1]]
        return np.stack(out)

    pw1 = up_units(np, i["cv_w_pw1"][0]).reshape(2, CB, P, D).transpose(1, 0, 2, 3).reshape(2 * CB, P, D)
    stream += [ffn(0), pw1, up_units(np, i["cv_w_pw2"][0]), ffn(1)]
    return np.concatenate(stream)


def pack_vectors(np, i):
    def cols(a):
        return np.asarray(a).reshape(-1, P).T

    names = ["g_pre_mix", "g_post_mix", "g_pre_ffn", "g_post_ffn", "mla_g_q", "mla_g_kv", "cv_b_pw1", "cv_w_dw",
             "cv_b_dw", "cv_g_ln", "cv_b_ln", "cv_b_pw2", "ffn_w_dw", "ffn_b_dw"]
    v = np.concatenate([cols(i["c"]), cols(i["c_ctx"]), cols(i["b_mod"])] + [cols(i[n]) for n in names], 1)
    assert v.shape == (P, NV)
    return np.ascontiguousarray(v)


def kernel(**inputs):
    import concourse.bacc as bacc
    import numpy as np
    from concourse.bass_utils import run_bass_kernel_spmd

    i = {name: np.asarray(a) for name, a in inputs.items()}
    cos, sin = rope_tables(np)
    arrays = {
        "x_t": np.ascontiguousarray(i["x"][0].T).reshape(CB, P, L),
        "ctx_t": np.ascontiguousarray(i["ctx"][0].T).reshape(CB, P, CTX),
        "units": pack_units(np, i),
        "mod_w": np.ascontiguousarray(i["w_mod"].reshape(2, CB, P, 6, D).transpose(0, 3, 1, 2, 4)).reshape(12, CB, P, D),
        "vectors_in": pack_vectors(np, i),
        "identity": np.eye(P, dtype=np.float32),
        "cos_sin": np.concatenate([cos, sin]),
        "cos_cos": np.concatenate([cos, cos]),
        "sin_sin": np.concatenate([sin, sin]),
    }
    nc = bacc.Bacc("TRN2", target_bir_lowering=False, num_devices=1, dynamic_dma_scratch_size=8192)
    args = [nc.dram_tensor(n, a.shape, mybir.dt.float32, kind="ExternalInput").ap() for n, a in arrays.items()]
    out = nc.dram_tensor("out_t", (CB, P, L), mybir.dt.float32, kind="ExternalOutput").ap()
    build(nc, *args, out)
    got = run_bass_kernel_spmd(nc, [arrays], core_ids=[0]).results[0]["out_t"]
    return np.ascontiguousarray(got.reshape(D, L).T)[None]
```

```python
import math
from contextlib import ExitStack

import concourse.bass as bass
from concourse import mybir

P = 128
D = 1024
L = 1024
CTX = 256
KEYS = L + CTX
CB = D // P
HALF = 512
HEADS = 8
DN_START = 2
ROPE = 64
GRID_W = 64
NKB = KEYS // P
QLORA_B = 3
TAPS = 31
PAD = TAPS // 2
FB = 22
GROUPS = FB // 2
EPS = 1e-6
SCALE = 1.0 / math.sqrt(192.0)

U_DQKV, U_HEAD, U_WO = 0, 6, 14
U_FFN = (22, 112)
U_PW1, U_PW2 = 88, 104
UNITS = 178
M_DQKV, M_WO, M_PW1, M_PW2 = 0, 6, 58, 74
M_FFN = (14, 82)

V_C, V_CCTX, V_BMOD = 0, 8, 16
V_PREMIX, V_POSTMIX, V_PREFFN, V_POSTFFN = 112, 128, 144, 160
V_GQ, V_GKV, V_BPW1, V_WDW, V_BDW, V_GLN, V_BLN, V_BPW2 = 176, 179, 180, 196, 444, 452, 460, 468
V_FW, V_FB = 476, 740
NV = 828
C_MOD, C_MODX, C_SC, C_EPS, C_MX, C_NM, C_RS, C_RI, C_GV, C_AV, C_AX, C_STD, C_RSTD = (
    0, 96, 112, 128, 129, 137, 145, 153, 161, 169, 177, 185, 195)
NC_SMALL = 205
MODS = 6 * CB
N_MOD, N_A, N_B, N_KV, N_Q = 0, 64, 80, 96, 106
PE_TAPS, PE_TAPS_LAST = 7, 12

F_A, F_T, F_SQ, F_ACC, F_RT, F_MD, F_RAW, F_ACCX, F_END = 0, 8192, 10240, 12288, 13312, 14592, 17664, 19712, 19968
R_H, R_W, R_G, R_END = 0, 16384, 24576, 33792
R_CQ, R_K0, R_V0, R_V1, R_K1, R_PT, R_CKV, R_KR, R_Q = 0, 6144, 8704, 11264, 13824, 20480, 24576, 27136, 29696


def slot_of(u):
    return u % 4 if u < U_HEAD else (u - U_HEAD) % 2 if u < U_WO else (u + 2) % 4


def prior(u):
    return u - 14 if u in (U_WO + 2, U_WO + 3) else u - 2 if U_HEAD <= u <= U_WO + 1 else u - 4


def freed(u):
    if U_HEAD <= u < U_WO:
        return "pj", 10 * (u - U_HEAD + 1)
    if u < U_HEAD:
        return "mm", M_DQKV + u + 1
    if u < U_FFN[0]:
        return "mm", M_WO + u - U_WO + 1
    if U_PW1 <= u < U_FFN[1]:
        return "mm", M_PW1 + u - U_PW1 + 1
    layer = int(u >= U_FFN[1])
    at, m0, d0 = u - U_FFN[layer], M_FFN[layer], DN_START + CB * GROUPS * layer
    if at < 4:
        return "mm", m0 + at + 1
    group, q = divmod(at - 4, 6)
    if q < 4 and group < GROUPS - 1:
        return "mm", m0 + 4 * (group + 1) + q + 1
    return "dn", d0 + CB * (group + 1)


class Chain:

    def __init__(self, engine, sem):
        self.engine, self.sem, self.n, self.term = engine, sem, 0, 0

    def __call__(self, ins):
        ins.then_inc(self.sem, 1)
        self.n += 1
        self.engine.wait_ge(self.sem, self.term + self.n)

    def lag(self, ins):
        ins.then_inc(self.sem, 1)
        self.n += 1
        self.engine.wait_ge(self.sem, self.n - 1)

    def enter(self, i, per):
        self.start, self.per, self.term = self.n, per, i * per

    def leave(self, trips):
        assert self.n - self.start == self.per, (self.n - self.start, self.per)
        self.n, self.term = self.start + trips * self.per, 0


def build(nc, xT, ctxT, units, modw, vecs, ident_d, cs_d, cosd_d, sind_d, outT):
    F32, F32R = mybir.dt.float32, mybir.dt.float32r
    ALU, ACT, AX = mybir.AluOpType, mybir.ActivationFunctionType, mybir.AxisListType
    MUL, ADD, SUB = ALU.mult, ALU.add, ALU.subtract
    xs_d = nc.dram_tensor("residual", (CB, P, L), F32, kind="Internal").ap()
    os_d = nc.dram_tensor("heads_out", (HEADS, P, L), F32, kind="Internal").ap()

    with ExitStack() as ctx:
        F = ctx.enter_context(nc.sbuf_tensor("f32_region", [P, F_END], F32))
        R = ctx.enter_context(nc.sbuf_tensor("f32r_region", [P, R_END], F32R))
        V = ctx.enter_context(nc.sbuf_tensor("vectors", [P, NV], F32))
        S = ctx.enter_context(nc.sbuf_tensor("small", [P, NC_SMALL], F32))
        ones = ctx.enter_context(nc.sbuf_tensor("ones", [P, P], F32))
        ident = ctx.enter_context(nc.sbuf_tensor("ident", [P, P], F32))
        PS = ctx.enter_context(nc.psum_tensor("psum", [P, 8 * HALF], F32))

        def sem(name):
            return ctx.enter_context(nc.semaphore(name))

        small_in, ctx_in, table_in = sem("small_in"), sem("ctx_in"), sem("table_in")
        x_in = [sem(f"x_in{s}") for s in range(2)]
        raw_in = [sem(f"raw_in{s}") for s in range(2)]
        w_hi, w_lo = sem("w_hi"), sem("w_lo")
        mm_done, mm_free = sem("mm_done"), sem("mm_free")
        const_set = sem("const_set")
        sq_ready, sq_used = sem("sq_ready"), sem("sq_used")
        acc_ready, mean_out, std_ready, diag_ready, rt_out = (
            sem("acc_ready"), sem("mean_out"), sem("std_ready"), sem("diag_ready"), sem("rt_out"))
        silu_c = sem("silu_c")
        mod_in = [sem(f"mod_in{s}") for s in range(3)]
        mod_used, mod_acc, mod_mm, mod_out = sem("mod_used"), sem("mod_acc"), sem("mod_mm"), sem("mod_out")
        ht_ready, h_act, h_hi, h_lo = sem("ht_ready"), sem("h_act"), sem("h_hi"), sem("h_lo")
        latent_in, mmx_done, rope_k, lat_scaled, lat_hi, lat_lo = (
            sem("latent_in"), sem("mmx_done"), sem("rope_k"), sem("lat_scaled"), sem("lat_hi"), sem("lat_lo"))
        pj_done, pj_free, pj_t, pj_hi = sem("pj_done"), sem("pj_free"), sem("pj_t"), sem("pj_hi")
        s_done, s_max, s_free, p_ready = sem("s_done"), sem("s_max"), sem("s_free"), sem("p_ready")
        tp_done, tp_hi, tp_lo, pt_free, o_free = sem("tp_done"), sem("tp_hi"), sem("tp_lo"), sem("pt_free"), sem("o_free")
        o_stored = [sem(f"o_stored{s}") for s in range(2)]
        blk_in = [sem(f"blk_in{k}") for k in range(CB)]
        blk_out = sem("blk_out")
        y_ready, y_new = sem("y_ready"), sem("y_new")
        y_zero = sem("y_zero")
        tap_done, silu_g, gp_ready, g_hi, g_lo = sem("tap_done"), sem("silu_g"), sem("gp_ready"), sem("g_hi"), sem("g_lo")
        dn_done, dn_free = sem("dn_done"), sem("dn_free")
        sig_ready, diag_in, start_in, taps_done, conv_done, conv_free = (
            sem("sig_ready"), sem("diag_in"), sem("start_in"), sem("taps_done"), sem("conv_done"), sem("conv_free"))
        dve_chain, act_chain, pool_chain = sem("dve_chain"), sem("act_chain"), sem("pool_chain")

        def f(at, n=L):
            return F[:, at:at + n]

        def r(at, n=L):
            return R[:, at:at + n]

        def A(k):
            return f(F_A + k * L)

        def h(k, part, half=None):
            at = R_H + part * CB * L + k * L
            return r(at) if half is None else r(at + half * HALF, HALF)

        def hx(k, part):
            return r(R_G + part * CB * CTX + k * CTX, CTX)

        def raw(s):
            return f(F_RAW + s * L)

        def w(slot, part, at=0, n=L):
            return r(R_W + slot * 2 * L + part * L + at, n)

        def sq(i):
            return f(F_SQ + (i % 2) * L)

        def pair(m):
            return PS[:, (m % 2) * 2 * HALF:(m % 2 + 1) * 2 * HALF]

        def bank(b, n=HALF, at=0):
            return PS[:, b * HALF + at:b * HALF + at + n]

        def dn(c):
            return PS[:, (4 + 2 * (c % 2)) * HALF:(6 + 2 * (c % 2)) * HALF]

        RT, RTX, RTKV = PS[:, 4 * HALF:6 * HALF], bank(6, CTX), PS[:, 4 * HALF:4 * HALF + KEYS]
        CQ, CKV, KRF = [f(F_A + k * L) for k in range(3)], f(3072, KEYS), f(4352, KEYS)
        COSD, SIND = f(5632), f(6656)
        def tap_diag(i, t):
            return f(F_MD + ((i % 2) * PE_TAPS_LAST + t) * P, P)

        def pe_taps(i):
            return PE_TAPS if i < CB - 1 else PE_TAPS_LAST

        def conv_out(i, half=None):
            b = 4 + 2 * (i % 2)
            return PS[:, b * HALF:(b + 2) * HALF] if half is None else bank(b + half)

        CS, ROPET, OST = f(F_SQ), [f(F_SQ + L + i * HALF, HALF) for i in range(2)], [f(F_ACC + i * HALF, HALF) for i in range(2)]
        U = [f(F_T, L + 2 * PAD), f(F_T + L + 2 * PAD, L + 2 * PAD)]
        VS, KS = [R_V0, R_V1], [R_K0, R_K1]

        def Pt(n, s):
            return f(F_A + ((n % 2) * 4 + s) * KEYS, KEYS)

        def G(g, jj, part, half=None):
            at = R_G + (g % 2) * 4 * L + jj * 2 * L + part * L
            return r(at) if half is None else r(at + half * HALF, HALF)

        def wait(engine, s, value):
            if not isinstance(value, int) or value > 0:
                engine.wait_ge(s, value)

        KP = [(0, HALF), (HALF, HALF), (2 * HALF, CTX)]
        PIECES = [("q", 0, HALF), ("qr", 0, HALF), ("k", *KP[0]), ("k", *KP[2]), ("k", *KP[1]),
                  ("q", HALF, HALF), ("qr", HALF, HALF)] + [("v", a, n) for a, n in KP]
        PIECES_AT = [[5], [6], [7, 8], [9]], [[0], [1], [2, 3], [4]]
        TURNS = [[0, 1], [2, 3, 4], [5, 6], [7, 8, 9]]
        WEIGHS = [[7, 8, 9], [0, 1], [2, 3, 4], [5, 6]]

        def piece_at(kind, head, start, n, part):
            base = VS[head % 2] if kind == "v" else KS[head % 2] if kind == "k" else {"q": R_Q, "qr": R_Q + 2 * L}[kind]
            return r(base + part * (KEYS if kind in "vk" else L) + start, n)

        def head_of(par, i):
            c = (par + 1) // 2
            return (2 * i + c, c)

        def half_steps(step):
            step(0, 0, 0, turned=False, weighed=False)
            step(1, 1, 0, weighed=False)
            yield 3
            step(14, 2, 3)
            step(15, 3, 3)
            step(16, 4, 3, scored=False)
            step(17, 5, 3, scored=False, turned=False)

        block = ctx.enter_context(nc.Block())

        @block.sync
        def _(sp):
            sp.dma_start(V[:, :], vecs).then_inc(small_in, 16)
            sp.dma_start(ident[:, :], ident_d).then_inc(small_in, 16)
            sp.dma_start(f(F_T, CB * CTX).rearrange("p (k n) -> p k n", k=CB), ctxT.rearrange("k p n -> p k n")).then_inc(ctx_in, 16)
            for k in range(0, CB, 4):
                sp.dma_start(f(F_A + k * L, 4 * L).rearrange("p (k n) -> p k n", k=4),
                             xT[k:k + 4].rearrange("k p n -> p k n")).then_inc(x_in[k // 4], 16)
            for s in range(2):
                sp.dma_start(raw(s), units[s]).then_inc(raw_in[s], 16)
            with sp.Fori(1, UNITS // 2) as i:
                for s in range(2):
                    sp.wait_ge(w_lo, 2 * i + (s - 1))
                    sp.dma_start(raw(s), units[2 * i + s]).then_inc(raw_in[s], 16)

        @block.gpsimd
        def _(pool):
            chain = Chain(pool, pool_chain)
            for t in range(2 * CB):
                if t >= 3:
                    pool.wait_ge(mod_used, t - 2)
                pool.dma_start(f(F_MD + (t % 3) * L), modw[t // CB, t % CB]).then_inc(mod_in[t % 3], 16)
            pool.wait_ge(silu_c, 2)
            pool.wait_ge(mod_used, 2 * CB)
            for t in range(10):
                for k in range(2):
                    pool.dma_start(f(F_MD + k * L), modw[t + 2, k]).then_inc(mod_in[k], 16)
                for k in range(CB):
                    pool.wait_ge(mod_in[k % 2], 16 * (7 - k % 2 + t * CB // 2 + k // 2))
                    part = f(F_MD + (k % 2) * L)
                    acc = f(F_MD + 2 * L)
                    if k == 0:
                        pool.wait_ge(mod_mm, t + 2)
                        chain(pool.tensor_scalar(acc, part, S[:, C_SC:C_SC + 1], 1.0, MUL, MUL))
                    else:
                        chain(pool.tensor_scalar(part, part, S[:, C_SC + 2 * k:C_SC + 2 * k + 1], 1.0, MUL, MUL))
                        add = pool.tensor_tensor(acc, acc, part, ADD)
                        if k < CB - 1:
                            chain(add)
                        else:
                            add.then_inc(mod_acc, 1)
                            pool.wait_ge(mod_acc, t + 1)
                    if k + 2 < CB:
                        pool.dma_start(part, modw[t + 2, k + 2]).then_inc(mod_in[k % 2], 16)

        @block.scalar
        def _(act):
            n_sq, n_norm, n_h, n_act = [0], [0], [0], [0]

            def copy(out, in_, scale=1.0):
                return act.activation(out, in_, ACT.Copy, scale=scale)

            def raw_count(u):
                return 16 * (u // 2 + 1)

            def split(u):
                if u >= UNITS:
                    return
                act.wait_ge(raw_in[u % 2], raw_count(u))
                if prior(u) >= 0:
                    by, count = freed(prior(u))
                    act.wait_ge({"mm": mm_done, "pj": pj_done, "dn": dn_done}[by], count)
                copy(w(slot_of(u), 0), raw(u % 2)).then_inc(w_hi, 1)

            def square(src, n=L):
                wait(act, sq_used, n_sq[0] - 1)
                out = f(F_SQ + (n_sq[0] % 2) * L, n)
                act.activation(out, src, ACT.Square).then_inc(sq_ready, 1)
                n_sq[0] += 1

            def std(at, width, n=CB, b=7):
                act.wait_ge(sq_used, n_sq[0])
                act.activation(S[:, C_STD:C_STD + n], bank(b, n, at), ACT.Sqrt, scale=1.0 / width,
                               bias=S[:, C_EPS:C_EPS + 1]).then_inc(std_ready, 1)
                n_norm[0] += 1

            def h_parts(src, dst, shift, func=None):
                n_h[0] += 1
                act.wait_ge(ht_ready, n_h[0])
                if func is not None:
                    act.activation(src, src, func, bias=shift).then_inc(h_act, 1)
                    n_act[0] += 1
                    act.wait_ge(h_act, n_act[0])
                    copy(dst, src).then_inc(h_hi, 1)
                else:
                    act.activation(dst, src, ACT.Identity, bias=shift).then_inc(h_hi, 1)

            act.wait_ge(small_in, 32)
            act.wait_ge(const_set, 3)
            act.activation(S[:, C_SC:C_SC + 2 * CB:2], V[:, V_C:V_C + CB], ACT.Silu).then_inc(silu_c, 1)
            act.activation(S[:, C_SC + 1:C_SC + 2 * CB:2], V[:, V_CCTX:V_CCTX + CB], ACT.Silu).then_inc(silu_c, 1)
            act.wait_ge(ctx_in, 16)
            for k in range(CB):
                square(f(F_T + k * CTX, CTX), CTX)
            std(N_B, D, CTX // P, 3)
            for k in range(CB):
                act.wait_ge(x_in[k // 4], 16)
                square(A(k))
            act.wait_ge(diag_ready, 1)
            std(N_A, D, b=2)
            for u in range(3):
                split(u)
            for k in range(CB):
                h_parts(sq(k), h(k, 0), S[:, C_MOD + k:C_MOD + k + 1])
            for k in range(CB):
                h_parts(f(F_SQ + (k % 2) * L, CTX), hx(k, 0), S[:, C_MODX + k:C_MODX + k + 1])

            split(3)
            act.wait_ge(mm_done, M_DQKV + 1)
            copy(f(3072 + CTX), pair(0)).then_inc(mm_free, 1)
            act.dma_start(COSD, cosd_d).then_inc(table_in, 16)
            act.dma_start(SIND, sind_d).then_inc(table_in, 16)
            act.wait_ge(mmx_done, 1)
            split(4)
            act.activation(f(3072, CTX), bank(4, CTX), ACT.Copy).then_inc(latent_in, 1)
            act.wait_ge(mmx_done, 2)
            split(5)
            act.wait_ge(mm_free, M_DQKV + 1)
            act.wait_ge(latent_in, 1)
            act.wait_ge(h_lo, 2 * CB)
            act.activation(f(F_SQ, KEYS), CKV, ACT.Square).then_inc(sq_ready, 1)
            n_sq[0] += 1
            std(N_KV, P, NKB)
            act.wait_ge(rope_k, 1)
            copy(r(R_KR, KEYS), KRF).then_inc(lat_hi, 1)
            act.wait_ge(lat_scaled, 1)
            copy(r(R_CKV, KEYS), CKV).then_inc(lat_hi, 1)
            act.wait_ge(mm_free, M_DQKV + 3)
            for k in range(QLORA_B):
                act.wait_ge(mm_done, M_DQKV + 4 + k)
                copy(CQ[k], pair(3 + k)).then_inc(mm_free, 1)
                act.wait_ge(mm_free, M_DQKV + 4 + k)
                square(CQ[k])
                if k == 0:
                    split(U_HEAD)
            std(N_Q, QLORA_B * P)
            for k in range(QLORA_B):
                act.wait_ge(lat_scaled, k + 2)
                copy(r(R_CQ + k * L), CQ[k]).then_inc(lat_hi, 1)
            act.dma_start(CS, cs_d).then_inc(table_in, 16)

            def piece_hi(head, par, i):
                kind, start, width = PIECES[i]
                if kind == "qr":
                    act.wait_ge(pj_t, 2 * head + (start // HALF + 1))
                    src = ROPET[start // HALF]
                else:
                    act.wait_ge(pj_done, 10 * head + (i + 1))
                    src = bank(6 + i % 2, width)
                copy(piece_at(kind, par, start, width, 0), src).then_inc(pj_hi, 1)

            def head_unit(head, c, i):
                act.wait_ge(raw_in[(c + 1) % 2], 16 * i + raw_count(U_HEAD + c + 1))
                if isinstance(head, int) and head == 0:
                    act.wait_ge(mm_done, M_DQKV + 6)
                else:
                    act.wait_ge(pj_done, 10 * head)
                copy(w((c + 1) % 2, 0), raw((c + 1) % 2)).then_inc(w_hi, 1)

            def exps(n, par, s):
                act.wait_ge(s_max, 4 * n + (s + 1))
                c = (par % 2) * 4 + s
                act.activation(Pt(par, s), PS[:, 0:KEYS], ACT.Exp, bias=S[:, C_NM + c:C_NM + c + 1], scale=SCALE,
                               accum_out=S[:, C_RS + c:C_RS + c + 1]).then_inc(s_free, 1)

            def tp_copy(n, par, kb):
                kbn = NKB * par + kb
                act.wait_ge(tp_done, NKB * n + (kb + 1))
                act.wait_ge(pt_free, NKB * n + (kb + 1))
                copy(r(R_PT + (kbn % 4) * L, HALF), bank(3 + kbn % 2)).then_inc(tp_hi, 1)

            def out_copy(n, par, head):
                act.wait_ge(pt_free, NKB * n + (4 + NKB))
                half = par % 2
                act.wait_ge(o_stored[half], 16 * head + 16)
                copy(OST[half], bank(5)).then_inc(o_free, 1)
                act.wait_ge(o_free, n + 2)
                act.dma_start(os_d[head, :, half * HALF:(half + 1) * HALF], OST[half]).then_inc(o_stored[half], 16)

            def step(n, par, i, scored=True, turned=True, weighed=True):
                for s in range(4):
                    turns = list(TURNS[s]) if turned else []
                    if turns:
                        tp_copy(n - 1, par - 1, turns.pop(0))
                    if scored:
                        exps(n, par, s)
                    if turns:
                        tp_copy(n - 1, par - 1, turns.pop(0))
                    if s == 0 and weighed:
                        out_copy(n - 2, par - 2, 2 * i + (par - 2) // 2)
                    head, c = head_of(par, i)
                    if scored and not (isinstance(n, int) and n == 2 * HEADS - 1):
                        for p in PIECES_AT[par % 2][s]:
                            piece_hi(head, c, p)
                    if scored and s == 1 and par % 2 == 0:
                        head_unit(head, c, i)
                    if turns:
                        tp_copy(n - 1, par - 1, turns.pop(0))

            for p in PIECES_AT[1]:
                for q in p:
                    piece_hi(0, 0, q)
            for trips in half_steps(step):
                with act.Fori(0, trips) as i:
                    for q in range(2, 6):
                        step(4 * i + q, q, i)
            for u in (U_WO + 1, U_WO + 2):
                split(u)
            for half in range(2):
                act.wait_ge(o_stored[half], 16 * HEADS + 16)
            for k in range(CB):
                act.dma_start(A(k), os_d[k]).then_inc(blk_in[k], 16)
            for k in range(CB):
                act.wait_ge(blk_in[k], 16)
                copy(h(k, 0), A(k)).then_inc(h_hi, 1)

            def y_blocks(u0, m0, bias):
                for n in range(CB):
                    split(u0 + n + 3)
                    act.wait_ge(mm_done, m0 + n + 1)
                    if bias is None:
                        copy(A(n), pair(n)).then_inc(mm_free, 1)
                    else:
                        act.activation(A(n), pair(n), ACT.Identity, bias=V[:, bias + n:bias + n + 1]).then_inc(mm_free, 1)
                    act.wait_ge(mm_free, m0 + n + 1)
                    square(A(n))

            def residual(b, x_src, out_dst, more, shift):
                if b:
                    act.wait_ge(blk_out, 16 * CB * b)
                for k in range(2):
                    act.dma_start(f(F_T + k * L), x_src[k]).then_inc(blk_in[k], 16)
                std(N_A, D)
                for k in range(CB):
                    act.wait_ge(y_new, CB * b + k + 1)
                    act.dma_start(out_dst[k], A(k)).then_inc(blk_out, 16)
                    if k + 2 < CB:
                        act.dma_start(f(F_T + (k % 2) * L), x_src[k + 2]).then_inc(blk_in[k + 2], 16)
                    if more:
                        square(A(k))
                if more:
                    std(N_B, D)
                    for k in range(CB):
                        h_parts(sq(k), h(k, 0), S[:, shift + k:shift + k + 1])

            y_blocks(U_WO, M_WO, None)
            residual(0, xT, xs_d, True, C_MOD + 3 * CB)

            def ffn(layer, b):
                u0, m0, j0, d0 = U_FFN[layer], M_FFN[layer], FB * layer, DN_START + CB * GROUPS * layer

                def splitr(i, c):
                    u = u0 + c
                    act.wait_ge(raw_in[u % 2], 96 * i + raw_count(u))
                    by, count = freed(prior(u))
                    if by == "mm":
                        act.wait_ge(mm_done, 8 * i + count)
                    if by == "dn" or c < 8:
                        act.wait_ge(dn_done, 2 * CB * i + (count if by == "dn" else d0))
                    copy(w(slot_of(u), 0), raw(u % 2)).then_inc(w_hi, 1)

                def g_part(i, j, g):
                    if j % 2 == 0:
                        wait(act, dn_done, 2 * CB * i + (d0 + CB * (g - 1)))
                    act.wait_ge(gp_ready, 4 * i + (j0 + j + 1))
                    copy(G(g, j % 2, 0), f(F_T + L)).then_inc(g_hi, 1)

                def up(i, g, q):
                    m, j, val = m0 + 4 * g + q, 2 * g + q // 2, q % 2
                    mi, ji = 8 * i + m, 4 * i + j
                    act.wait_ge(mm_done, mi + 1)
                    col = ji + FB * val
                    if val:
                        if not (isinstance(i, int) and j0 + j == 0):
                            act.wait_ge(g_lo, ji + j0)
                    elif not (isinstance(i, int) and j0 + j == 0):
                        act.wait_ge(gp_ready, ji + j0)
                    wv = V_FW + layer * 3 * 2 * FB
                    act.activation(f(F_T + val * L), pair(q), ACT.Identity, scale=V[:, bass.ds(wv + 2 * FB + col, 1)],
                                   bias=V[:, bass.ds(V_FB + layer * 2 * FB + col, 1)]).then_inc(tap_done, 1)
                    if not val:
                        if not (isinstance(i, int) and j == 0):
                            g_part(i, j - 1, (j - 1) // 2)
                        act.wait_ge(mm_free, mi + 1)
                        act.activation(f(F_T), f(F_T), ACT.Silu).then_inc(silu_g, 1)

                for q in range(4):
                    if q < 3:
                        split(u0 + q + 3)
                    up(0, 0, q)
                with act.Fori(0, (GROUPS - 1) // 2) as i:
                    for g in (1, 2):
                        n0 = 4 + 6 * (g - 1)
                        splitr(i, n0 + 2)
                        for q in range(4):
                            splitr(i, n0 + q + 3)
                            up(i, g, q)
                        splitr(i, n0 + 7)
                g_part(0, FB - 1, GROUPS - 1)
                split(u0 + 66)
                split(u0 + 67)
                for c in range(CB):
                    act.wait_ge(dn_free, d0 + CB * (GROUPS - 1) + c + 1)
                    square(A(c))
                split(u0 + 68)

            ffn(0, 1)
            residual(1, xs_d, xs_d, True, C_MOD + MODS)

            act.wait_ge(mod_mm, 12)
            act.wait_ge(blk_out, 16 * CB * 2)
            for i in range(CB):
                split(U_PW1 + 2 * i + 3)
                split(U_PW1 + 2 * i + 4)
                act.wait_ge(mm_done, M_PW1 + 2 * i + 2)
                act.activation(f(F_SQ + L), pair(1), ACT.Sigmoid,
                               bias=V[:, V_BPW1 + CB + i:V_BPW1 + CB + i + 1]).then_inc(sig_ready, 1)
                if i >= 2:
                    act.wait_ge(conv_done, i - 1)
                for t in range(pe_taps(i)):
                    tap = V_WDW + (TAPS - 1 - t) * CB + i
                    act.activation(tap_diag(i, t), ident[:, :], ACT.Copy, scale=V[:, tap:tap + 1]).then_inc(diag_in, 1)
                act.wait_ge(mm_free, M_PW1 + 2 * i + 2)
                act.activation(A(i), U[i % 2][:, 0:L], ACT.Identity, scale=V[:, V_WDW + i:V_WDW + i + 1],
                               bias=V[:, V_BDW + i:V_BDW + i + 1]).then_inc(start_in, 1)
                if i:
                    act.wait_ge(taps_done, i)
                copy(f(F_RT), U[i % 2][:, 1:L + 1], V[:, V_WDW + CB + i:V_WDW + CB + i + 1]).then_inc(start_in, 1)
            act.wait_ge(mean_out, 1)
            act.activation(S[:, C_STD:C_STD + CB], bank(7, CB, N_A), ACT.Copy, scale=1.0 / D).then_inc(std_ready, 1)
            n_norm[0] += 1
            for k in range(CB):
                act.wait_ge(y_ready, k + 1)
                square(A(k))
            std(N_B, D)
            for k in range(CB):
                h_parts(sq(k), h(k, 0), V[:, V_BLN + k:V_BLN + k + 1], ACT.Silu)
            y_blocks(U_PW2, M_PW2, V_BPW2)
            residual(2, xs_d, xs_d, True, C_MOD + MODS + 3 * CB)
            ffn(1, 3)
            residual(3, xs_d, outT, False, None)
            act.wait_ge(blk_out, 16 * CB * 4)

        @block.vector
        def _(dve):
            n_sq, n_norm, n_h, n_rt = [0], [0], [0], [0]
            chain = Chain(dve, dve_chain)

            def split(u):
                if u >= UNITS:
                    return
                dve.wait_ge(w_hi, u + 1)
                dve.tensor_tensor(w(slot_of(u), 1), raw(u % 2), w(slot_of(u), 0), SUB).then_inc(w_lo, 1)

            def add_square(first, acc, n=L):
                dve.wait_ge(sq_ready, n_sq[0] + 1)
                src = f(F_SQ + (n_sq[0] % 2) * L, n)
                if first:
                    dve.tensor_copy(acc, src).then_inc(sq_used, 1)
                else:
                    wait(dve, sq_used, n_sq[0])
                    dve.tensor_tensor(acc, acc, src, ADD).then_inc(sq_used, 1)
                n_sq[0] += 1

            def spread(n=CB, at=F_RT, inverse=True):
                dve.wait_ge(std_ready, n_norm[0] + 1)
                n_norm[0] += 1
                src = C_STD
                if inverse:
                    chain(dve.reciprocal(S[:, C_RSTD:C_RSTD + n], S[:, C_STD:C_STD + n]))
                    src = C_RSTD
                for a, b in ([(0, n // 2), (n // 2, n)] if n >= CB else [(0, n)]):
                    dve.tensor_tensor(f(at + a * P, (b - a) * P).rearrange("p (c n) -> p c n", c=b - a),
                                      ident[:, :].unsqueeze(1).to_broadcast([P, b - a, P]),
                                      S[:, src + a:src + b].unsqueeze(2).to_broadcast([P, b - a, P]), MUL).then_inc(diag_ready, 1)
                n_rt[0] += 1

            def rt_here():
                dve.wait_ge(rt_out, n_rt[0])

            def h_blocks(src, gain, rt, dst_hi, dst_lo, shift, n=L, done=None):
                def lo(k):
                    dve.wait_ge(h_hi, n_h[0] + k + 1)
                    t = f(F_SQ + (k % 2) * L, n)
                    if shift is None:
                        dve.tensor_tensor(dst_lo(k), t, dst_hi(k), SUB).then_inc(h_lo, 1)
                    else:
                        dve.scalar_tensor_tensor(out=dst_lo(k), in0=t, scalar=shift(k), in1=dst_hi(k), op0=ADD, op1=SUB).then_inc(h_lo, 1)
                for k in range(CB):
                    if k >= 2:
                        dve.wait_ge(h_lo, n_h[0] + k - 1)
                    dve.scalar_tensor_tensor(out=f(F_SQ + (k % 2) * L, n), in0=src(k), scalar=gain(k), in1=rt,
                                             op0=MUL, op1=MUL).then_inc(ht_ready, 1)
                    if k >= 1:
                        lo(k - 1)
                lo(CB - 1)
                n_h[0] += CB
                dve.wait_ge(h_lo, n_h[0])

            dve.memset(ones[:, :], 1.0).then_inc(const_set, 1)
            dve.memset(S[:, :], 0.0).then_inc(const_set, 1)
            dve.wait_ge(const_set, 2)
            dve.memset(S[:, C_EPS:C_EPS + 1], EPS).then_inc(const_set, 1)
            dve.wait_ge(small_in, 32)
            spread(CTX // P, F_RT + L)
            spread()
            for vec in range(2):
                dve.wait_ge(mod_mm, vec + 1)
                b = V[:, V_BMOD + vec * CB:V_BMOD + (vec + 1) * CB]
                for s, at in enumerate((C_MOD, C_MODX)):
                    mod = dve.tensor_tensor(S[:, at + vec * CB:at + (vec + 1) * CB],
                                            PS[:, vec * HALF + s:vec * HALF + 2 * CB:2], b, ADD)
                    if s == 0:
                        chain(mod)
                    else:
                        mod.then_inc(mod_out, 1)
                        dve.wait_ge(mod_out, vec + 1)

            def gain(dst, g, mod, one):
                chain(dve.scalar_tensor_tensor(out=S[:, dst:dst + CB], in0=S[:, mod:mod + CB], scalar=float(one),
                                               in1=V[:, g:g + CB], op0=ADD, op1=MUL))

            gain(C_AV, V_PREMIX, C_MOD + CB, 1)
            gain(C_AX, V_PREMIX, C_MODX + CB, 1)

            def col(at):
                return lambda k: S[:, at + k:at + k + 1]

            for u in range(3):
                split(u)
            rt_here()
            h_blocks(A, col(C_AV), RT, lambda k: h(k, 0), lambda k: h(k, 1), col(C_MOD))
            h_blocks(lambda k: f(F_T + k * CTX, CTX), col(C_AX), RTX, lambda k: hx(k, 0), lambda k: hx(k, 1), col(C_MODX), CTX)

            split(3)
            split(4)
            dve.wait_ge(mmx_done, 2)
            chain(dve.tensor_copy(f(4352, CTX), bank(5, CTX)))
            dve.wait_ge(table_in, 32)
            dve.wait_ge(mm_free, M_DQKV + 1)
            dve.wait_ge(mm_done, M_DQKV + 2)
            dve.tensor_tensor(f(4352 + CTX), pair(1), COSD, MUL).then_inc(mm_free, 1)
            split(5)
            dve.wait_ge(mm_done, M_DQKV + 3)
            dve.tensor_tensor(f(F_T), pair(0), SIND, MUL).then_inc(mm_free, 1)
            dve.wait_ge(mm_free, M_DQKV + 3)
            dve.tensor_tensor(f(4352 + CTX), f(4352 + CTX), f(F_T), ADD).then_inc(rope_k, 1)
            spread(NKB)
            rt_here()
            dve.scalar_tensor_tensor(out=CKV, in0=CKV, scalar=V[:, V_GKV:V_GKV + 1], in1=RTKV,
                                     op0=MUL, op1=MUL).then_inc(lat_scaled, 1)
            for k, (at, src) in enumerate([(R_KR, KRF), (R_CKV, CKV)]):
                dve.wait_ge(lat_hi, k + 1)
                dve.tensor_tensor(r(at + KEYS, KEYS), src, r(at, KEYS), SUB).then_inc(lat_lo, 1)
            split(U_HEAD)
            spread()
            rt_here()
            for k in range(QLORA_B):
                dve.scalar_tensor_tensor(out=CQ[k], in0=CQ[k], scalar=V[:, V_GQ + k:V_GQ + k + 1], in1=RT,
                                         op0=MUL, op1=MUL).then_inc(lat_scaled, 1)
            for k in range(QLORA_B):
                dve.wait_ge(lat_hi, k + 3)
                dve.tensor_tensor(r(R_CQ + (QLORA_B + k) * L), CQ[k], r(R_CQ + k * L), SUB).then_inc(lat_lo, 1)
            dve.wait_ge(lat_lo, QLORA_B + 2)
            n_sq[0] += 2 * CB + 1 + QLORA_B
            dve.wait_ge(table_in, 48)

            def piece_lo(head, par, i):
                kind, start, width = PIECES[i]
                src = bank(6 + i % 2, width)
                if kind == "qr":
                    dve.wait_ge(pj_done, 10 * head + (i + 1))
                    dve.tensor_tensor(ROPET[start // HALF], src, CS[:, start:start + HALF], MUL).then_inc(pj_t, 1)
                    src = ROPET[start // HALF]
                dve.wait_ge(pj_hi, 10 * head + (i + 1))
                dve.tensor_tensor(piece_at(kind, par, start, width, 1), src,
                                  piece_at(kind, par, start, width, 0), SUB).then_inc(pj_free, 1)

            def head_unit(head, c):
                dve.wait_ge(w_hi, U_HEAD + 2 + head)
                other = (c + 1) % 2
                dve.tensor_tensor(w(other, 1), raw(other), w(other, 0), SUB).then_inc(w_lo, 1)

            def maxes(n, par, s):
                c = (par % 2) * 4 + s
                dve.wait_ge(s_done, 4 * n + (s + 1))
                chain(dve.reduce_max(S[:, C_MX + c:C_MX + c + 1], PS[:, 0:KEYS], AX.X))
                dve.tensor_scalar(S[:, C_NM + c:C_NM + c + 1], S[:, C_MX + c:C_MX + c + 1], -SCALE, None, MUL).then_inc(s_max, 1)

            def scales(n, par, s):
                c = (par % 2) * 4 + s
                dve.wait_ge(s_free, 4 * n + (s + 1))
                chain(dve.reciprocal(S[:, C_RI + c:C_RI + c + 1], S[:, C_RS + c:C_RS + c + 1]))
                dve.tensor_scalar(Pt(par, s), Pt(par, s), S[:, C_RI + c:C_RI + c + 1], None, MUL).then_inc(p_ready, 1)

            def tp_sub(n, par, kb):
                kbn = NKB * par + kb
                dve.wait_ge(tp_hi, NKB * n + (kb + 1))
                at = R_PT + (kbn % 4) * L
                dve.tensor_tensor(r(at + HALF, HALF), bank(3 + kbn % 2), r(at, HALF), SUB).then_inc(tp_lo, 1)

            def mod_add(t, dst):
                dve.wait_ge(mod_mm, t + 3)
                dve.tensor_tensor(S[:, bass.ds(C_MOD + dst, CB)], bank(7, CB), V[:, bass.ds(V_BMOD + dst, CB)],
                                  ADD).then_inc(mod_out, 1)

            def step(n, par, i, scored=True, turned=True, weighed=True):
                for s in range(4):
                    turns = list(TURNS[s]) if turned else []
                    if scored:
                        maxes(n, par, s)
                        if s == 0 and par % 4 == 2:
                            mod_add(i, CB * i + 2 * CB)
                    if turns:
                        tp_sub(n - 1, par - 1, turns.pop(0))
                    if scored:
                        scales(n, par, s)
                    if turns:
                        tp_sub(n - 1, par - 1, turns.pop(0))
                    head, c = head_of(par, i)
                    if scored and not (isinstance(n, int) and n == 2 * HEADS - 1):
                        for p in PIECES_AT[par % 2][s]:
                            piece_lo(head, c, p)
                    if scored and s == 1 and par % 2 == 0:
                        head_unit(head, c)
                    if turns:
                        tp_sub(n - 1, par - 1, turns.pop(0))

            for p in PIECES_AT[1]:
                for q in p:
                    piece_lo(0, 0, q)
            for trips in half_steps(step):
                with dve.Fori(0, trips) as i:
                    chain.enter(i, 32)
                    for q in range(2, 6):
                        step(4 * i + q, q, i)
                    chain.leave(trips)
            dve.wait_ge(mod_out, 6)
            for u in (U_WO + 1, U_WO + 2):
                split(u)
            for k in range(CB):
                dve.wait_ge(h_hi, n_h[0] + k + 1)
                dve.tensor_tensor(h(k, 1), A(k), h(k, 0), SUB).then_inc(h_lo, 1)
            n_h[0] += CB
            dve.wait_ge(h_lo, n_h[0])

            def y_blocks(u0):
                for n in range(CB):
                    split(u0 + n + 3)
                    if n < CB - 1:
                        add_square(n == 0, f(F_ACC))
                n_sq[0] += 1

            def residual(b, g_post, gate, more, g_pre, scale, shift):
                gain(C_GV, g_post, gate, 0)
                if more:
                    gain(C_AV, g_pre, scale, 1)
                spread()
                rt_here()
                for k in range(CB):
                    chain(dve.scalar_tensor_tensor(out=A(k), in0=A(k), scalar=S[:, C_GV + k:C_GV + k + 1], in1=RT, op0=MUL, op1=MUL))
                    dve.wait_ge(blk_in[k], 16 * (b + 2))
                    dve.tensor_tensor(A(k), A(k), f(F_T + (k % 2) * L), ADD).then_inc(y_new, 1)
                if more:
                    n_sq[0] += CB
                    spread()
                    rt_here()
                    h_blocks(A, col(C_AV), RT, lambda k: h(k, 0), lambda k: h(k, 1), col(shift))

            y_blocks(U_WO)
            residual(0, V_POSTMIX, C_MOD + 2 * CB, True, V_PREFFN, C_MOD + 4 * CB, C_MOD + 3 * CB)

            def ffn(layer, b):
                u0, m0, j0, d0 = U_FFN[layer], M_FFN[layer], FB * layer, DN_START + CB * GROUPS * layer

                def splitr(i, c):
                    u = u0 + c
                    dve.wait_ge(w_hi, 12 * i + (u + 1))
                    dve.tensor_tensor(w(slot_of(u), 1), raw(u % 2), w(slot_of(u), 0), SUB).then_inc(w_lo, 1)

                def g_part(i, j, g):
                    ji = 4 * i + j
                    dve.wait_ge(g_hi, ji + (j0 + 1))
                    dve.tensor_tensor(G(g, j % 2, 1), f(F_T + L), G(g, j % 2, 0), SUB).then_inc(g_lo, 1)

                def up(i, g, q):
                    m, j, val = m0 + 4 * g + q, 2 * g + q // 2, q % 2
                    mi, ji = 8 * i + m, 4 * i + j
                    c = ji + FB * val
                    wv = V_FW + layer * 6 * FB
                    at = F_T + val * L
                    dve.wait_ge(tap_done, 8 * i + (2 * FB * layer + 4 * g + q + 1))
                    chain(dve.scalar_tensor_tensor(out=f(at + 1, L - 1), in0=PS[:, (q % 2) * L:(q % 2) * L + L - 1],
                                                   scalar=V[:, bass.ds(wv + c, 1)], in1=f(at + 1, L - 1), op0=MUL, op1=ADD))
                    dve.scalar_tensor_tensor(out=f(at, L - 1), in0=PS[:, (q % 2) * L + 1:(q % 2) * L + L],
                                             scalar=V[:, bass.ds(wv + 4 * FB + c, 1)], in1=f(at, L - 1), op0=MUL, op1=ADD).then_inc(mm_free, 1)
                    if val:
                        dve.wait_ge(silu_g, ji + (j0 + 1))
                        dve.wait_ge(mm_free, mi + 1)
                        dve.tensor_tensor(f(F_T + L), f(F_T + L), f(F_T), MUL).then_inc(gp_ready, 1)
                    elif not (isinstance(i, int) and j == 0):
                        g_part(i, j - 1, (j - 1) // 2)

                def down(i, g):
                    dve.wait_ge(dn_free, 2 * CB * i + (d0 + CB * g))
                    for c in range(CB):
                        dve.wait_ge(dn_done, 2 * CB * i + (d0 + CB * g + c + 1))
                        dve.tensor_tensor(A(c), A(c), dn(c), ADD).then_inc(dn_free, 1)

                mods = layer == 0
                if mods:
                    mod_add(4, CB * 4 + 2 * CB)
                for q in range(4):
                    if q < 3:
                        split(u0 + q + 3)
                    up(0, 0, q)
                dve.wait_ge(blk_out, 16 * CB * b)
                for c in range(CB):
                    dve.memset(A(c), 0.0).then_inc(y_zero, 1)
                dve.wait_ge(y_zero, CB * (layer + 1))
                with dve.Fori(0, (GROUPS - 1) // 2) as i:
                    chain.enter(i, 8)
                    for g in (1, 2):
                        n0 = 4 + 6 * (g - 1)
                        splitr(i, n0 + 2)
                        for q in range(4):
                            splitr(i, n0 + q + 3)
                            up(i, g, q)
                            if mods and g == 1 and q == 0:
                                mod_add(i + 5, CB * i + 7 * CB)
                        splitr(i, n0 + 7)
                        down(i, g - 1)
                    chain.leave((GROUPS - 1) // 2)
                g_part(0, FB - 1, GROUPS - 1)
                split(u0 + 66)
                split(u0 + 67)
                dve.wait_ge(dn_free, d0 + CB * (GROUPS - 1))
                for c in range(CB):
                    dve.wait_ge(dn_done, d0 + CB * (GROUPS - 1) + c + 1)
                    dve.tensor_tensor(A(c), A(c), dn(c), ADD).then_inc(dn_free, 1)
                    if c >= 1:
                        add_square(c == 1, f(F_ACC))
                n_sq[0] += 1
                split(u0 + 68)

            ffn(0, 1)
            dve.wait_ge(mod_out, 12)
            residual(1, V_POSTFFN, C_MOD + 5 * CB, True, V_PREMIX + CB, C_MOD + MODS + CB, C_MOD + MODS)

            for s in range(2):
                chain(dve.memset(U[s][:, 0:PAD], 0.0))
                chain(dve.memset(U[s][:, PAD + L:], 0.0))

            def conv_finish(i):
                dve.wait_ge(conv_done, i + 1)
                dve.tensor_tensor(A(i), A(i), conv_out(i), ADD).then_inc(conv_free, 1)
                dve.wait_ge(conv_free, i + 1)
                if i == 0:
                    chain(dve.tensor_copy(f(F_ACC), A(i)))
                elif i < CB - 1:
                    chain(dve.tensor_tensor(f(F_ACC), f(F_ACC), A(i), ADD))
                else:
                    dve.tensor_tensor(f(F_ACC), f(F_ACC), A(i), ADD).then_inc(acc_ready, 1)

            for i in range(CB):
                dve.wait_ge(sig_ready, i + 1)
                if i >= 2:
                    dve.wait_ge(conv_done, i - 1)
                dve.scalar_tensor_tensor(out=U[i % 2][:, PAD:PAD + L], in0=pair(0), scalar=V[:, V_BPW1 + i:V_BPW1 + i + 1],
                                         in1=f(F_SQ + L), op0=ADD, op1=MUL).then_inc(mm_free, 2)
                split(U_PW1 + 2 * i + 3)
                split(U_PW1 + 2 * i + 4)
                dve.wait_ge(start_in, 2 * i + 2)
                for t in range(2, TAPS - pe_taps(i)):
                    chained = A(i) if t % 2 == 0 else f(F_RT)
                    chain.lag(dve.scalar_tensor_tensor(out=chained, in0=U[i % 2][:, t:t + L],
                                                       scalar=V[:, V_WDW + t * CB + i:V_WDW + t * CB + i + 1],
                                                       in1=chained, op0=MUL, op1=ADD))
                    if t == 12 and i:
                        conv_finish(i - 1)
                dve.wait_ge(dve_chain, chain.n)
                dve.tensor_tensor(A(i), A(i), f(F_RT), ADD).then_inc(taps_done, 1)
                dve.wait_ge(taps_done, i + 1)
            conv_finish(CB - 1)
            spread(inverse=False)
            rt_here()
            for k in range(CB):
                dve.tensor_tensor(A(k), A(k), RT, SUB).then_inc(y_ready, 1)
            n_sq[0] += CB
            spread()
            rt_here()
            h_blocks(A, lambda k: V[:, V_GLN + k:V_GLN + k + 1], RT, lambda k: h(k, 0), lambda k: h(k, 1), None)
            y_blocks(U_PW2)
            residual(2, V_POSTMIX + CB, C_MOD + MODS + 2 * CB, True, V_PREFFN + CB, C_MOD + MODS + 4 * CB, C_MOD + MODS + 3 * CB)
            ffn(1, 3)
            residual(3, V_POSTFFN + CB, C_MOD + MODS + 5 * CB, False, None, None, None)

        @block.tensor
        def _(pe):
            n_sq, n_h, n_diag = [0], [0], [0]

            def three(out, w_parts, x_parts, first, last):
                (wh, wl), (xh, xl) = w_parts, x_parts
                pe.matmul(out, wl, xh, start=first, stop=False)
                pe.matmul(out, wh, xl, start=False, stop=False)
                return pe.matmul(out, wh, xh, start=False, stop=last)

            def col_sums(src, at, first, last, n=CB, b=7):
                for c in range(n):
                    mm = pe.matmul(bank(b, 1, at + c), f(src + c * P, P), ones[:, 0:1],
                                   start=first and c == 0, stop=last and c == n - 1)
                return mm

            def square_sums(at, first, last, n=CB, b=7):
                n_sq[0] += 1
                pe.wait_ge(sq_ready, n_sq[0])
                slot = (n_sq[0] - 1) % 2 if n <= CB else 0
                col_sums(F_SQ + slot * L, at, first, last, n, b).then_inc(sq_used, 1)

            def spread(n=CB, src=F_RT, b=4):
                at = 0
                for width in ([n // 2 * P] * 2 if n >= CB else [n * P]):
                    n_diag[0] += 1
                    pe.wait_ge(diag_ready, n_diag[0])
                    end = at + width
                    while at < end:
                        step = min(end, (at // HALF + 1) * HALF) - at
                        mm = pe.matmul(bank(b, step, at), ones[:, :], f(src + at, step), start=True, stop=True)
                        at += step
                mm.then_inc(rt_out, 1)

            def mod_sums(acc):
                for c in range(CB):
                    mm = pe.matmul(bank(7, 1, N_MOD + c), f(acc + c * P, P), ones[:, 0:1], start=True, stop=True)
                return mm

            def up_block(u, m, slot, par, k):
                if k == 0:
                    pe.wait_ge(w_lo, u + 1)
                    if not isinstance(m, int) or m >= 2:
                        pe.wait_ge(mm_free, m - 1)
                for half in range(2):
                    mm = three(pair(par)[:, half * HALF:(half + 1) * HALF], [w(slot, p, k * P, P) for p in range(2)],
                               [h(k, p, half) for p in range(2)], k == 0, k == CB - 1)
                if k == CB - 1:
                    mm.then_inc(mm_done, 1)

            def up(u, m, slot, par):
                for k in range(CB):
                    up_block(u, m, slot, par, k)

            def first_two(u, m):
                for k in range(CB + 2):
                    if k < CB:
                        pe.wait_ge(h_lo, n_h[0] + k + 1)
                        up_block(u, m, slot_of(u), m % 2, k)
                    if k >= 2:
                        up_block(u + 1, m + 1, slot_of(u + 1), (m + 1) % 2, k - 2)
                n_h[0] += CB

            pe.wait_ge(const_set, 3)
            pe.sem_inc(pt_free, 4)
            pe.sem_inc(tp_lo, 2)
            pe.sem_inc(o_free, 1)
            for s in range(2):
                pe.sem_inc(o_stored[s], 16)
            pe.sem_inc(dn_done, DN_START)
            pe.sem_inc(dn_free, DN_START)
            pe.wait_ge(silu_c, 2)
            pe.wait_ge(small_in, 32)

            def mod_tile(t):
                vec, k = divmod(t, CB)
                pe.wait_ge(mod_in[t % 3], 16 * (t // 3 + 1))
                for c in range(CB):
                    mm = pe.matmul(bank(vec, 2, 2 * c), f(F_MD + (t % 3) * L + c * P, P),
                                   S[:, C_SC + 2 * k:C_SC + 2 * k + 2],
                                   start=k + c == 0, stop=k + c == 2 * CB - 2)
                mm.then_inc(mod_used, 1)
                if k == CB - 1:
                    pe.wait_ge(mod_used, t + 1)
                    pe.sem_inc(mod_mm, 1)

            for k in range(CB):
                square_sums(N_B, k == 0, k == CB - 1, CTX // P, 3)
            for k in range(CB):
                square_sums(N_A, k == 0, k == CB - 1, b=2)
                mod_tile(k)
                if k == 1:
                    spread(CTX // P, F_RT + L, 6)
            spread()
            for k in range(CB, 2 * CB):
                mod_tile(k)

            first_two(U_DQKV, M_DQKV)
            pe.wait_ge(h_lo, 2 * CB)
            n_h[0] += CB
            for n in range(2):
                for k in range(CB):
                    mm = three(bank(n + 4, CTX), [w(slot_of(n), p, k * P, P) for p in range(2)],
                               [hx(k, p) for p in range(2)], k == 0, k == CB - 1)
                mm.then_inc(mmx_done, 1)
            up(2, 2, 2, 0)
            square_sums(N_KV, True, True, NKB)
            up(3, 3, 3, 1)
            spread(NKB)
            up(4, 4, 0, 0)
            square_sums(N_Q, True, False)
            up(5, 5, 1, 1)
            square_sums(N_Q, False, False)
            square_sums(N_Q, False, True)
            spread()

            def piece(head, par, i, mods=None):
                slot = par % 2
                kind, start, width = PIECES[i]
                if i == 0:
                    pe.wait_ge(w_lo, head + (U_HEAD + 1))
                if i >= 2 or not (isinstance(head, int) and head == 0):
                    pe.wait_ge(pj_free, 10 * head + (i - 1))
                if mods is not None:
                    pe.wait_ge(mod_out, mods)
                out = bank(6 + i % 2, width)
                if kind == "v":
                    for b in range(width // P):
                        at = start + b * P
                        mm = three(out[:, b * P:(b + 1) * P], [r(R_CKV + p * KEYS + at, P) for p in range(2)],
                                   [w(slot, p, 7 * P, P) for p in range(2)], True, True)
                elif kind == "k":
                    mm = three(out, [w(slot, p, 6 * P, P) for p in range(2)],
                               [r(R_CKV + p * KEYS + start, width) for p in range(2)], True, True)
                else:
                    for kb in range(QLORA_B):
                        if i == 0 and isinstance(head, int) and head == 0:
                            pe.wait_ge(lat_lo, kb + 3)
                        mm = three(out, [w(slot, p, (2 * kb + (kind == "qr")) * P, P) for p in range(2)],
                                   [r(R_CQ + (p * QLORA_B + kb) * L + start, width) for p in range(2)],
                                   kb == 0, kb == QLORA_B - 1)
                mm.then_inc(pj_done, 1)

            def scores(n, par, s, head):
                if s == 0:
                    pe.wait_ge(pj_free, 10 * head + (7 if par % 2 else 5))
                if s or not (isinstance(n, int) and n == 0):
                    pe.wait_ge(s_free, 4 * n + s)
                q = (par % 2) * HALF + s * P
                for at, width in KP:
                    three(PS[:, at:at + width], [r(R_Q + p * L + q, P) for p in range(2)],
                          [r(KS[(par // 2) % 2] + p * KEYS + at, width) for p in range(2)], True, False)
                    mm = three(PS[:, at:at + width], [r(R_Q + (2 + p) * L + q, P) for p in range(2)],
                               [r(R_KR + p * KEYS + at, width) for p in range(2)], False, True)
                mm.then_inc(s_done, 1)

            def turn(n, par, kb):
                kbn = NKB * par + kb
                if kb == 0:
                    pe.wait_ge(p_ready, 4 * n + 4)
                pe.wait_ge(tp_lo, NKB * n + (kb + 1))
                for s in range(4):
                    mm = pe.transpose(bank(3 + kbn % 2, P, s * P), Pt(par, s)[:, kb * P:(kb + 1) * P], ident[:, :])
                mm.then_inc(tp_done, 1)

            def weigh(n, par, kb, head):
                kbn = NKB * par + kb
                pe.wait_ge(tp_lo, NKB * n + (kb + 3))
                if kb == 0:
                    pe.wait_ge(o_free, n + 1)
                    pe.wait_ge(pj_free, 10 * head + 10)
                vs, pt = VS[(par // 2) % 2] + kb * P, R_PT + (kbn % 4) * L
                mm = three(bank(5), [r(vs + p * KEYS, P) for p in range(2)], [r(pt + p * HALF, HALF) for p in range(2)],
                           kb == 0, kb == NKB - 1)
                mm.then_inc(pt_free, 1)

            def step(n, par, i, scored=True, turned=True, weighed=True):
                for s in range(4):
                    turns = list(TURNS[s]) if turned else []
                    mods = None
                    if scored:
                        scores(n, par, s, 2 * i + par // 2)
                        if s == 0 and par % 4 == 2:
                            pe.wait_ge(pj_free, 20 * i + 15)
                            pe.wait_ge(mod_acc, i + 1)
                            mod_sums(F_MD + 2 * L).then_inc(mod_mm, 1)
                            mods = i + 3
                    if turns:
                        turn(n - 1, par - 1, turns.pop(0))
                    back = 2 if s == 0 else 1
                    if weighed if s == 0 else turned:
                        for kb in WEIGHS[s]:
                            weigh(n - back, par - back, kb, 2 * i + (par - back) // 2)
                    if turns:
                        turn(n - 1, par - 1, turns.pop(0))
                    if scored and not (isinstance(n, int) and n == 2 * HEADS - 1):
                        head, c = head_of(par, i)
                        for p in PIECES_AT[par % 2][s]:
                            piece(head, c, p, mods)
                    if turns:
                        turn(n - 1, par - 1, turns.pop(0))

            for p in PIECES_AT[1]:
                for q in p:
                    piece(0, 0, q, 2 if q == 1 else None)
            for trips in half_steps(step):
                with pe.Fori(0, trips) as i:
                    for q in range(2, 6):
                        step(4 * i + q, q, i)

            def boundary(more):
                n_sq[0] += CB - 1
                pe.wait_ge(sq_used, n_sq[0])
                col_sums(F_ACC, N_A, True, False)
                square_sums(N_A, False, True)
                spread()
                if more:
                    for k in range(CB):
                        square_sums(N_B, k == 0, k == CB - 1)
                    spread()

            def mixer_out(u0, m0):
                first_two(u0, m0)
                for n in range(2, CB):
                    up(u0 + n, m0 + n, slot_of(u0 + n), n % 2)

            mixer_out(U_WO, M_WO)
            boundary(True)

            def ffn(layer):
                u0, m0, j0, d0 = U_FFN[layer], M_FFN[layer], FB * layer, DN_START + CB * GROUPS * layer

                def mods(t, i):
                    pe.wait_ge(dn_free, 2 * CB * i + d0)
                    pe.wait_ge(mod_acc, t + 1)
                    mod_sums(F_MD + 2 * L).then_inc(mod_mm, 1)

                def down(i, g, u, taken=None):
                    pe.wait_ge(w_lo, 12 * i + (u + 2))
                    pe.wait_ge(g_lo, 4 * i + (j0 + 2 * g + 2))
                    if taken is not None:
                        pe.wait_ge(mod_out, taken)
                    for c in range(CB):
                        pe.wait_ge(dn_free, 2 * CB * i + (d0 + CB * g + c - 1))
                        for jj in range(2):
                            for half in range(2):
                                mm = three(dn(c)[:, half * HALF:(half + 1) * HALF],
                                           [w(slot_of(u + jj), p, c * P, P) for p in range(2)],
                                           [G(g, jj, p, half) for p in range(2)], jj == 0, jj == 1)
                        mm.then_inc(dn_done, 1)

                if layer == 0:
                    mods(4, 0)
                first_two(u0, m0)
                for q in range(2, 4):
                    up(u0 + q, m0 + q, slot_of(u0 + q), q % 2)
                with pe.Fori(0, (GROUPS - 1) // 2) as i:
                    for g in (1, 2):
                        n0 = u0 + 4 + 6 * (g - 1)
                        if layer == 0 and g == 1:
                            mods(i + 5, i)
                        for q in range(4):
                            up(12 * i + (n0 + q), 8 * i + (m0 + 4 * g + q), slot_of(n0 + q), q % 2)
                        down(i, g - 1, n0 + 4, i + 8 if layer == 0 else None)
                down(0, GROUPS - 1, u0 + 64)

            ffn(0)
            boundary(True)
            def conv(i):
                pe.wait_ge(mm_free, M_PW1 + 2 * i + 2)
                if i >= 2:
                    pe.wait_ge(conv_free, i - 1)
                pe.wait_ge(diag_in, PE_TAPS * i + pe_taps(i))
                n = pe_taps(i)
                for t in range(n):
                    for half in range(2):
                        mm = pe.matmul(conv_out(i, half), tap_diag(i, t), U[i % 2][:, TAPS - 1 - t + half * HALF:TAPS - 1 - t + (half + 1) * HALF],
                                       start=t == 0, stop=t == n - 1)
                mm.then_inc(conv_done, 1)

            first_two(U_PW1, M_PW1)
            for i in range(CB):
                if i < CB - 1:
                    for n in (2 * i + 2, 2 * i + 3):
                        up(U_PW1 + n, M_PW1 + n, slot_of(U_PW1 + n), n % 2)
                conv(i)
            pe.wait_ge(acc_ready, 1)
            col_sums(F_ACC, N_A, True, True).then_inc(mean_out, 1)
            spread()
            for k in range(CB):
                square_sums(N_B, k == 0, k == CB - 1)
            spread()
            mixer_out(U_PW2, M_PW2)
            boundary(True)
            ffn(1)
            boundary(False)


def rope_tables(np):
    quarter = ROPE // 4
    pos = np.arange(L)
    inv = (np.float32(10000.0) ** (-np.arange(quarter, dtype=np.float32) / np.float32(quarter))).astype(np.float32)
    rows = (pos // GRID_W).astype(np.float32)[:, None] * inv
    cols = (pos % GRID_W).astype(np.float32)[:, None] * inv
    angle = np.concatenate([rows, rows, cols, cols], axis=-1).T
    sign = np.tile(np.repeat(np.array([-1.0, 1.0], np.float32), quarter), 2)[:, None]
    return np.cos(angle).astype(np.float32), (np.sin(angle) * sign).astype(np.float32)


def up_units(np, w):
    n = w.shape[1] // P
    return np.ascontiguousarray(w.reshape(CB, P, n, P).transpose(2, 1, 0, 3)).reshape(n, P, D)


def pack_units(np, i):
    swap = np.arange(ROPE).reshape(2, 2, ROPE // 4)[:, ::-1].reshape(-1)
    dqkv = i["mla_w_dqkv"][0]
    kr = dqkv[:, 512:576]
    stream = [up_units(np, dqkv[:, 384:512]), up_units(np, np.concatenate([kr, kr], 1)),
              up_units(np, np.concatenate([kr[:, swap], kr[:, swap]], 1)), up_units(np, dqkv[:, :384])]
    uq = i["mla_w_uq"][0].reshape(QLORA_B, P, HEADS, 192)
    ukv = i["mla_w_ukv"][0].reshape(P, HEADS, 256)
    for hd in range(HEADS):
        q = uq[:, :, hd]
        q = np.concatenate([q, q[:, :, 128:][:, :, swap]], -1).transpose(1, 0, 2).reshape(P, 768)
        stream.append(np.concatenate([q, ukv[:, hd]], -1)[None])
    stream.append(up_units(np, i["mla_w_o"][0]))

    def ffn(layer):
        ups, downs = up_units(np, i["ffn_w_up"][layer]), i["ffn_w_down"][layer].reshape(FB, P, D)
        out = []
        for g in range(GROUPS + 1):
            if g < GROUPS:
                out += [ups[2 * g], ups[FB + 2 * g], ups[2 * g + 1], ups[FB + 2 * g + 1]]
            if g:
                out += [downs[2 * g - 2], downs[2 * g - 1]]
        return np.stack(out)

    pw1 = up_units(np, i["cv_w_pw1"][0]).reshape(2, CB, P, D).transpose(1, 0, 2, 3).reshape(2 * CB, P, D)
    stream += [ffn(0), pw1, up_units(np, i["cv_w_pw2"][0]), ffn(1)]
    return np.concatenate(stream)


def pack_vectors(np, i):
    def cols(a):
        return np.asarray(a).reshape(-1, P).T

    names = ["g_pre_mix", "g_post_mix", "g_pre_ffn", "g_post_ffn", "mla_g_q", "mla_g_kv", "cv_b_pw1", "cv_w_dw",
             "cv_b_dw", "cv_g_ln", "cv_b_ln", "cv_b_pw2", "ffn_w_dw", "ffn_b_dw"]
    v = np.concatenate([cols(i["c"]), cols(i["c_ctx"]), cols(i["b_mod"])] + [cols(i[n]) for n in names], 1)
    assert v.shape == (P, NV)
    return np.ascontiguousarray(v)


def kernel(**inputs):
    import concourse.bacc as bacc
    import numpy as np
    from concourse.bass_utils import run_bass_kernel_spmd

    i = {name: np.asarray(a) for name, a in inputs.items()}
    cos, sin = rope_tables(np)
    arrays = {
        "x_t": np.ascontiguousarray(i["x"][0].T).reshape(CB, P, L),
        "ctx_t": np.ascontiguousarray(i["ctx"][0].T).reshape(CB, P, CTX),
        "units": pack_units(np, i),
        "mod_w": np.ascontiguousarray(i["w_mod"].reshape(2, CB, P, 6, D).transpose(0, 3, 1, 2, 4)).reshape(12, CB, P, D),
        "vectors_in": pack_vectors(np, i),
        "identity": np.eye(P, dtype=np.float32),
        "cos_sin": np.concatenate([cos, sin]),
        "cos_cos": np.concatenate([cos, cos]),
        "sin_sin": np.concatenate([sin, sin]),
    }
    nc = bacc.Bacc("TRN2", target_bir_lowering=False, num_devices=1, dynamic_dma_scratch_size=8192)
    args = [nc.dram_tensor(n, a.shape, mybir.dt.float32, kind="ExternalInput").ap() for n, a in arrays.items()]
    out = nc.dram_tensor("out_t", (CB, P, L), mybir.dt.float32, kind="ExternalOutput").ap()
    build(nc, *args, out)
    got = run_bass_kernel_spmd(nc, [arrays], core_ids=[0]).results[0]["out_t"]
    return np.ascontiguousarray(got.reshape(D, L).T)[None]
```

```python
import math
from contextlib import ExitStack

import concourse.bass as bass
from concourse import mybir

P = 128
D = 1024
L = 1024
CTX = 256
KEYS = L + CTX
CB = D // P
HALF = 512
HEADS = 8
DN_START = 2
ROPE = 64
GRID_W = 64
NKB = KEYS // P
QLORA_B = 3
TAPS = 31
PAD = TAPS // 2
FB = 22
GROUPS = FB // 2
EPS = 1e-6
SCALE = 1.0 / math.sqrt(192.0)

U_DQKV, U_HEAD, U_WO = 0, 6, 14
U_FFN = (22, 112)
U_PW1, U_PW2 = 88, 104
UNITS = 178
M_DQKV, M_WO, M_PW1, M_PW2 = 0, 6, 58, 74
M_FFN = (14, 82)

V_C, V_CCTX, V_BMOD = 0, 8, 16
V_PREMIX, V_POSTMIX, V_PREFFN, V_POSTFFN = 112, 128, 144, 160
V_GQ, V_GKV, V_BPW1, V_WDW, V_BDW, V_GLN, V_BLN, V_BPW2 = 176, 179, 180, 196, 444, 452, 460, 468
V_FW, V_FB = 476, 740
NV = 828
C_MOD, C_MODX, C_SC, C_EPS, C_MX, C_NM, C_RS, C_RI, C_GV, C_AV, C_AX, C_STD, C_RSTD = (
    0, 96, 112, 128, 129, 137, 145, 153, 161, 169, 177, 185, 195)
NC_SMALL = 205
MODS = 6 * CB
N_MOD, N_A, N_B, N_KV, N_Q = 0, 64, 80, 96, 106
PE_TAPS, PE_TAPS_LAST = 7, 14

F_A, F_T, F_SQ, F_ACC, F_RT, F_MD, F_RAW, F_ACCX, F_END = 0, 8192, 10240, 12288, 13312, 14592, 17664, 19712, 19968
R_H, R_W, R_G, R_END = 0, 16384, 24576, 33792
R_CQ, R_K0, R_V0, R_V1, R_K1, R_PT, R_CKV, R_KR, R_Q = 0, 6144, 8704, 11264, 13824, 20480, 24576, 27136, 29696


def slot_of(u):
    return u % 4 if u < U_HEAD else (u - U_HEAD) % 2 if u < U_WO else (u + 2) % 4


def prior(u):
    return u - 14 if u in (U_WO + 2, U_WO + 3) else u - 2 if U_HEAD <= u <= U_WO + 1 else u - 4


def freed(u):
    if U_HEAD <= u < U_WO:
        return "pj", 10 * (u - U_HEAD + 1)
    if u < U_HEAD:
        return "mm", M_DQKV + u + 1
    if u < U_FFN[0]:
        return "mm", M_WO + u - U_WO + 1
    if U_PW1 <= u < U_FFN[1]:
        return "mm", M_PW1 + u - U_PW1 + 1
    layer = int(u >= U_FFN[1])
    at, m0, d0 = u - U_FFN[layer], M_FFN[layer], DN_START + CB * GROUPS * layer
    if at < 4:
        return "mm", m0 + at + 1
    group, q = divmod(at - 4, 6)
    if q < 4 and group < GROUPS - 1:
        return "mm", m0 + 4 * (group + 1) + q + 1
    return "dn", d0 + CB * (group + 1)


class Chain:

    def __init__(self, engine, sem):
        self.engine, self.sem, self.n, self.term = engine, sem, 0, 0

    def __call__(self, ins):
        ins.then_inc(self.sem, 1)
        self.n += 1
        self.engine.wait_ge(self.sem, self.term + self.n)

    def lag(self, ins):
        ins.then_inc(self.sem, 1)
        self.n += 1
        self.engine.wait_ge(self.sem, self.n - 1)

    def enter(self, i, per):
        self.start, self.per, self.term = self.n, per, i * per

    def leave(self, trips):
        assert self.n - self.start == self.per, (self.n - self.start, self.per)
        self.n, self.term = self.start + trips * self.per, 0


def build(nc, xT, ctxT, units, modw, vecs, ident_d, fold_d, cs_d, cosd_d, sind_d, outT):
    F32, F32R = mybir.dt.float32, mybir.dt.float32r
    ALU, ACT, AX = mybir.AluOpType, mybir.ActivationFunctionType, mybir.AxisListType
    MUL, ADD, SUB = ALU.mult, ALU.add, ALU.subtract
    xs_d = nc.dram_tensor("residual", (CB, P, L), F32, kind="Internal").ap()
    os_d = nc.dram_tensor("heads_out", (HEADS, P, L), F32, kind="Internal").ap()

    with ExitStack() as ctx:
        F = ctx.enter_context(nc.sbuf_tensor("f32_region", [P, F_END], F32))
        with nc.sbuf_tensor("f32r_region", [P, R_END], F32R) as R:
            pass
        R32 = ctx.enter_context(nc.sbuf_tensor("f32r_region_plain", [P, R_END], F32))
        V = ctx.enter_context(nc.sbuf_tensor("vectors", [P, NV], F32))
        S = ctx.enter_context(nc.sbuf_tensor("small", [P, NC_SMALL], F32))
        ones = ctx.enter_context(nc.sbuf_tensor("ones", [P, P], F32))
        ident = ctx.enter_context(nc.sbuf_tensor("ident", [P, P], F32))
        PS = ctx.enter_context(nc.psum_tensor("psum", [P, 8 * HALF], F32))

        def sem(name):
            return ctx.enter_context(nc.semaphore(name))

        small_in, ctx_in, table_in = sem("small_in"), sem("ctx_in"), sem("table_in")
        x_in = [sem(f"x_in{s}") for s in range(CB // 2)]
        raw_in = [sem(f"raw_in{s}") for s in range(2)]
        w_hi, w_lo = sem("w_hi"), sem("w_lo")
        mm_done, mm_free = sem("mm_done"), sem("mm_free")
        const_set = sem("const_set")
        sq_ready, sq_used = sem("sq_ready"), sem("sq_used")
        acc_ready, sums_out, std_ready, diag_ready, rt_out = (
            sem("acc_ready"), sem("sums_out"), sem("std_ready"), sem("diag_ready"), sem("rt_out"))
        row_ready, cols_out = sem("row_ready"), sem("cols_out")
        silu_c = sem("silu_c")
        mod1_in = [[sem(f"mod1_in{v}_{j}") for j in range(CB // 2)] for v in range(2)]
        mod_in = [sem(f"mod_in{s}") for s in range(2)]
        shift_mm, mod_part = sem("shift_mm"), sem("mod_part")
        mod_used, mod_acc, mod_mm, mod_out = sem("mod_used"), sem("mod_acc"), sem("mod_mm"), sem("mod_out")
        ht_ready, h_act, h_hi, h_lo = sem("ht_ready"), sem("h_act"), sem("h_hi"), sem("h_lo")
        latent_in, mmx_done, rope_k, lat_scaled, lat_hi, lat_lo = (
            sem("latent_in"), sem("mmx_done"), sem("rope_k"), sem("lat_scaled"), sem("lat_hi"), sem("lat_lo"))
        pj_done, pj_free, pj_t, pj_hi, fold_done = sem("pj_done"), sem("pj_free"), sem("pj_t"), sem("pj_hi"), sem("fold_done")
        s_done, s_max, s_free, p_ready = sem("s_done"), sem("s_max"), sem("s_free"), sem("p_ready")
        tp_done, tp_hi, tp_lo, pt_free, o_free = sem("tp_done"), sem("tp_hi"), sem("tp_lo"), sem("pt_free"), sem("o_free")
        o_stored = [sem(f"o_stored{s}") for s in range(2)]
        blk_in = [sem(f"blk_in{k}") for k in range(CB)]
        blk_out = sem("blk_out")
        y_new, y_scaled, y_pool, half_sq, half_used = sem("y_new"), sem("y_scaled"), sem("y_pool"), sem("half_sq"), sem("half_used")
        y_zero = sem("y_zero")
        tap_done, silu_g, gp_ready, g_hi, g_lo = sem("tap_done"), sem("silu_g"), sem("gp_ready"), sem("g_hi"), sem("g_lo")
        dn_done, dn_free = sem("dn_done"), sem("dn_free")
        sig_ready, diag_in, start_in, taps_done, conv_done, conv_free = (
            sem("sig_ready"), sem("diag_in"), sem("start_in"), sem("taps_done"), sem("conv_done"), sem("conv_free"))
        dve_chain, pool_chain = sem("dve_chain"), sem("pool_chain")

        def f(at, n=L):
            return F[:, at:at + n]

        def r(at, n=L):
            return R[:, at:at + n]

        def A(k):
            return f(F_A + k * L)

        def h(k, part, half=None):
            at = R_H + part * CB * L + k * L
            return r(at) if half is None else r(at + half * HALF, HALF)

        def A_half(k, half):
            return f(F_A + k * L + half * HALF, HALF)

        def half_slot(n):
            return f(F_SQ + (n % 4) * HALF, HALF)

        def t_slot(n):
            return f(F_T + (n % 4) * HALF, HALF)

        def hx(k, part):
            return r(R_G + part * CB * CTX + k * CTX, CTX)

        def raw(s):
            return f(F_RAW + s * L)

        def w(slot, part, at=0, n=L):
            return r(R_W + slot * 2 * L + part * L + at, n)

        def sq(i):
            return f(F_SQ + (i % 2) * L)

        def pair(m):
            return PS[:, (m % 2) * 2 * HALF:(m % 2 + 1) * 2 * HALF]

        def bank(b, n=HALF, at=0):
            return PS[:, b * HALF + at:b * HALF + at + n]

        def dn(c):
            return PS[:, (4 + 2 * (c % 2)) * HALF:(6 + 2 * (c % 2)) * HALF]

        RT_OF = [bank(4), bank(5)]
        SUMROW = [PS[0:1, (6 + half) * HALF:(7 + half) * HALF] for half in range(2)]
        ROW = [F[0:1, F_RT + half * HALF:F_RT + (half + 1) * HALF] for half in range(2)]
        ROWCOLS = [bank(6 + half, CB // 2, N_B) for half in range(2)]
        RT, RTX, RTKV = PS[:, 4 * HALF:6 * HALF], bank(6, CTX), PS[:, 4 * HALF:4 * HALF + KEYS]
        CQ, CKV, KRF = [f(F_A + k * L) for k in range(3)], f(3072, KEYS), f(4352, KEYS)
        COSD, SIND = f(5632), f(6656)
        def tap_diag(i, t):
            return f(F_MD + ((i % 2) * PE_TAPS + t) * P, P)

        def pe_taps(i):
            return PE_TAPS if i < CB - 1 else PE_TAPS_LAST

        def mod1(v, k, n=1):
            return R32[:, R_H + (v * CB + k) * L:R_H + (v * CB + k + n) * L]

        def shift_acc(s):
            return R32[:, 28672 + s * L:28672 + (s + 1) * L]

        def x_at(at, k):
            return R32[:, at + k * L:at + (k + 1) * L]

        def conv_out(i, half=None):
            b = 4 + 2 * (i % 2)
            return PS[:, b * HALF:(b + 2) * HALF] if half is None else bank(b + half)

        FOLD = f(F_RT, P)
        CS, ROPET, OST = f(F_SQ), [f(F_SQ + L + i * HALF, HALF) for i in range(2)], [f(F_ACC + i * HALF, HALF) for i in range(2)]
        U = [f(F_T, L + 2 * PAD), f(F_T + L + 2 * PAD, L + 2 * PAD)]
        VS, KS = [R_V0, R_V1], [R_K0, R_K1]

        def Pt(n, s):
            return f(F_A + ((n % 2) * 4 + s) * KEYS, KEYS)

        def G(g, jj, part, half=None):
            at = R_G + (g % 2) * 4 * L + jj * 2 * L + part * L
            return r(at) if half is None else r(at + half * HALF, HALF)

        def wait(engine, s, value):
            if not isinstance(value, int) or value > 0:
                engine.wait_ge(s, value)

        KP = [(0, HALF), (HALF, HALF), (2 * HALF, CTX)]
        PIECES = [("q", 0, HALF), ("qr", 0, HALF), ("k", *KP[0]), ("k", *KP[2]), ("k", *KP[1]),
                  ("q", HALF, HALF), ("qr", HALF, HALF)] + [("v", a, n) for a, n in KP]
        PIECES_AT = [[5], [6], [7, 8], [9]], [[0], [1, 2], [3, 4], []]
        TURNS = [[0, 1], [2, 3, 4], [5, 6], [7, 8, 9]]
        WEIGHS = [[7, 8, 9], [0, 1], [2, 3, 4], [5, 6]]

        def piece_at(kind, head, start, n, part):
            base = VS[head % 2] if kind == "v" else KS[head % 2] if kind == "k" else {"q": R_Q, "qr": R_Q + 2 * L}[kind]
            return r(base + part * (KEYS if kind in "vk" else L) + start, n)

        def head_of(par, i):
            c = (par + 1) // 2
            return (2 * i + c, c)

        def half_steps(step):
            step(0, 0, 0, turned=False, weighed=False)
            step(1, 1, 0, weighed=False)
            yield 3
            step(14, 2, 3)
            step(15, 3, 3)
            step(16, 4, 3, scored=False)
            step(17, 5, 3, scored=False, turned=False)

        block = ctx.enter_context(nc.Block())

        @block.sync
        def _(sp):
            sp.dma_start(V[:, :], vecs).then_inc(small_in, 16)
            sp.dma_start(ident[:, :], ident_d).then_inc(small_in, 16)
            sp.dma_start(f(F_T, CB * CTX).rearrange("p (k n) -> p k n", k=CB), ctxT.rearrange("k p n -> p k n")).then_inc(ctx_in, 16)
            for k in range(0, CB, 2):
                sp.dma_start(f(F_A + k * L, 2 * L).rearrange("p (k n) -> p k n", k=2),
                             xT[k:k + 2].rearrange("k p n -> p k n")).then_inc(x_in[k // 2], 16)
            for s in range(2):
                sp.dma_start(raw(s), units[s]).then_inc(raw_in[s], 16)
            with sp.Fori(1, UNITS // 2) as i:
                for s in range(2):
                    sp.wait_ge(w_lo, 2 * i + (s - 1))
                    sp.dma_start(raw(s), units[2 * i + s]).then_inc(raw_in[s], 16)

        @block.gpsimd
        def _(pool):
            chain = Chain(pool, pool_chain)

            def odd_blocks(b):
                for half in range(2):
                    for k in range(1, CB, 2):
                        pool.wait_ge(y_scaled, CB * b + CB // 2 * half + k // 2 + 1)
                        pool.wait_ge(blk_in[k], 16 * (b + 2))
                        pool.tensor_tensor(A_half(k, half), A_half(k, half),
                                           x_at(R_H if b % 2 else R_G, k)[:, half * HALF:(half + 1) * HALF], ADD).then_inc(y_pool, 1)

            pool.wait_ge(silu_c, 2)
            pool.wait_ge(mod_used, CB)
            for t in range(10):
                for k in range(2):
                    pool.dma_start(f(F_MD + k * L), modw[t + 2, k]).then_inc(mod_in[k], 16)
                for k in range(CB):
                    pool.wait_ge(mod_in[k % 2], 16 * (1 + t * CB // 2 + k // 2))
                    part = f(F_MD + (k % 2) * L)
                    acc = f(F_MD + 2 * L)
                    if k == 0:
                        pool.wait_ge(mod_mm, t + 1)
                        chain(pool.tensor_scalar(acc, part, S[:, C_SC:C_SC + 1], 1.0, MUL, MUL))
                    else:
                        chain(pool.tensor_scalar(part, part, S[:, C_SC + 2 * k:C_SC + 2 * k + 1], 1.0, MUL, MUL))
                        add = pool.tensor_tensor(acc, acc, part, ADD)
                        if k < CB - 1:
                            chain(add)
                        else:
                            add.then_inc(mod_acc, 1)
                            pool.wait_ge(mod_acc, t + 1)
                    if k + 2 < CB:
                        pool.dma_start(part, modw[t + 2, k + 2]).then_inc(mod_in[k % 2], 16)
                if t == 4:
                    odd_blocks(0)
            for b in range(1, 4):
                odd_blocks(b)

        @block.scalar
        def _(act):
            n_sq, n_half, n_h, n_act, n_res, n_pool = [0], [0], [0], [0], [0], [0]

            def copy(out, in_, scale=1.0):
                return act.activation(out, in_, ACT.Copy, scale=scale)

            def raw_count(u):
                return 16 * (u // 2 + 1)

            def split(u):
                if u >= UNITS:
                    return
                act.wait_ge(raw_in[u % 2], raw_count(u))
                if prior(u) >= 0:
                    by, count = freed(prior(u))
                    act.wait_ge({"mm": mm_done, "pj": pj_done, "dn": dn_done}[by], count)
                copy(w(slot_of(u), 0), raw(u % 2)).then_inc(w_hi, 1)

            def square(src, n=L):
                wait(act, sq_used, n_sq[0] - 1)
                out = f(F_SQ + (n_sq[0] % 2) * L, n)
                act.activation(out, src, ACT.Square).then_inc(sq_ready, 1)
                n_sq[0] += 1

            def std(at, width, n=CB, b=7, sums=None):
                act.wait_ge(*((sq_used, n_sq[0]) if sums is None else (sums_out, sums)))
                act.activation(S[:, C_STD:C_STD + n], bank(b, n, at), ACT.Sqrt, scale=1.0 / width,
                               bias=S[:, C_EPS:C_EPS + 1]).then_inc(std_ready, 1)

            def half_square(src):
                n_half[0] += 1
                wait(act, half_used, n_half[0] - 4)
                act.activation(half_slot(n_half[0] - 1), src, ACT.Square).then_inc(half_sq, 1)

            def std_row(half, width):
                act.wait_ge(half_used, n_half[0])
                act.activation(ROW[half], SUMROW[half], ACT.Sqrt, scale=1.0 / width, bias=S[0:1, C_EPS:C_EPS + 1]).then_inc(row_ready, 1)

            def h_parts(src, dst, shift, func=None):
                n_h[0] += 1
                act.wait_ge(ht_ready, n_h[0])
                if func is not None:
                    act.activation(src, src, func, bias=shift).then_inc(h_act, 1)
                    n_act[0] += 1
                    act.wait_ge(h_act, n_act[0])
                    copy(dst, src).then_inc(h_hi, 1)
                else:
                    act.activation(dst, src, ACT.Identity, bias=shift).then_inc(h_hi, 1)

            for j in range(CB // 2):
                for v in (1, 0):
                    act.dma_start(mod1(v, 2 * j, 2).rearrange("p (k n) -> p k n", k=2),
                                  modw[v, 2 * j:2 * j + 2].rearrange("k p n -> p k n")).then_inc(mod1_in[v][j], 16)
            act.wait_ge(small_in, 32)
            act.wait_ge(const_set, 3)
            act.activation(S[:, C_SC:C_SC + 2 * CB:2], V[:, V_C:V_C + CB], ACT.Silu).then_inc(silu_c, 1)
            act.activation(S[:, C_SC + 1:C_SC + 2 * CB:2], V[:, V_CCTX:V_CCTX + CB], ACT.Silu).then_inc(silu_c, 1)
            act.wait_ge(ctx_in, 16)
            for k in range(CB):
                square(f(F_T + k * CTX, CTX), CTX)
            std(N_B, D, CTX // P, 3, 1)
            for k in range(CB):
                act.wait_ge(x_in[k // 2], 16)
                square(A(k))
            for u in range(2):
                split(u)
            act.wait_ge(diag_ready, 1)
            std(N_A, D, b=2, sums=2)
            for k in range(CB):
                h_parts(sq(k), h(k, 0), S[:, C_MOD + k:C_MOD + k + 1])
            split(2)
            for k in range(CB):
                h_parts(f(F_SQ + (k % 2) * L, CTX), hx(k, 0), S[:, C_MODX + k:C_MODX + k + 1])

            split(3)
            act.wait_ge(mm_done, M_DQKV + 1)
            copy(f(3072 + CTX), pair(0)).then_inc(mm_free, 1)
            act.dma_start(COSD, cosd_d).then_inc(table_in, 16)
            act.dma_start(SIND, sind_d).then_inc(table_in, 16)
            act.wait_ge(mmx_done, 1)
            split(4)
            act.activation(f(3072, CTX), bank(4, CTX), ACT.Copy).then_inc(latent_in, 1)
            act.wait_ge(mmx_done, 2)
            split(5)
            act.wait_ge(mm_free, M_DQKV + 1)
            act.wait_ge(latent_in, 1)
            act.wait_ge(h_lo, 2 * CB)
            act.activation(f(F_SQ, KEYS), CKV, ACT.Square).then_inc(sq_ready, 1)
            n_sq[0] += 1
            std(N_KV, P, NKB)
            act.wait_ge(rope_k, 1)
            copy(r(R_KR, KEYS), KRF).then_inc(lat_hi, 1)
            act.wait_ge(lat_scaled, 1)
            copy(r(R_CKV, KEYS), CKV).then_inc(lat_hi, 1)
            act.wait_ge(mm_free, M_DQKV + 3)
            for k in range(QLORA_B):
                act.wait_ge(mm_done, M_DQKV + 4 + k)
                copy(CQ[k], pair(3 + k)).then_inc(mm_free, 1)
                act.wait_ge(mm_free, M_DQKV + 4 + k)
                square(CQ[k])
                if k == 0:
                    split(U_HEAD)
            std(N_Q, QLORA_B * P)
            for k in range(QLORA_B):
                act.wait_ge(lat_scaled, k + 2)
                copy(r(R_CQ + k * L), CQ[k]).then_inc(lat_hi, 1)
            act.dma_start(CS, cs_d).then_inc(table_in, 16)
            act.wait_ge(lat_scaled, 1 + QLORA_B)
            act.dma_start(FOLD, fold_d).then_inc(table_in, 16)

            def piece_hi(head, par, i):
                kind, start, width = PIECES[i]
                if kind == "qr":
                    act.wait_ge(fold_done, 2 * head + (start // HALF + 1))
                else:
                    act.wait_ge(pj_done, 10 * head + (i + 1))
                src = bank(6 + i % 2, width)
                copy(piece_at(kind, par, start, width, 0), src).then_inc(pj_hi, 1)

            def head_unit(head, c, i):
                act.wait_ge(raw_in[(c + 1) % 2], 16 * i + raw_count(U_HEAD + c + 1))
                if isinstance(head, int) and head == 0:
                    act.wait_ge(mm_done, M_DQKV + 6)
                else:
                    act.wait_ge(pj_done, 10 * head)
                copy(w((c + 1) % 2, 0), raw((c + 1) % 2)).then_inc(w_hi, 1)

            def exps(n, par, s):
                act.wait_ge(s_max, 4 * n + (s + 1))
                c = (par % 2) * 4 + s
                act.activation(Pt(par, s), PS[:, 0:KEYS], ACT.Exp, bias=S[:, C_NM + c:C_NM + c + 1], scale=SCALE,
                               accum_out=S[:, C_RS + c:C_RS + c + 1]).then_inc(s_free, 1)

            def tp_copy(n, par, kb):
                kbn = NKB * par + kb
                act.wait_ge(tp_done, NKB * n + (kb + 1))
                act.wait_ge(pt_free, NKB * n + (kb + 1))
                copy(r(R_PT + (kbn % 4) * L, HALF), bank(3 + kbn % 2)).then_inc(tp_hi, 1)

            def out_copy(n, par, head):
                act.wait_ge(pt_free, NKB * n + (4 + NKB))
                half = par % 2
                act.wait_ge(o_stored[half], 16 * head + 16)
                copy(OST[half], bank(5)).then_inc(o_free, 1)
                act.wait_ge(o_free, n + 2)
                act.dma_start(os_d[head, :, half * HALF:(half + 1) * HALF], OST[half]).then_inc(o_stored[half], 16)

            def step(n, par, i, scored=True, turned=True, weighed=True):
                if isinstance(n, int) and n == 2 * HEADS:
                    for k in range(5):
                        heads_back(k)
                    split(U_WO + 1)
                for s in range(4):
                    turns = list(TURNS[s]) if turned else []
                    if turns:
                        tp_copy(n - 1, par - 1, turns.pop(0))
                    if scored:
                        exps(n, par, s)
                    if turns:
                        tp_copy(n - 1, par - 1, turns.pop(0))
                    if s == 0 and weighed:
                        out_copy(n - 2, par - 2, 2 * i + (par - 2) // 2)
                    head, c = head_of(par, i)
                    if turns:
                        tp_copy(n - 1, par - 1, turns.pop(0))
                    if scored and not (isinstance(n, int) and n == 2 * HEADS - 1):
                        for p in PIECES_AT[par % 2][s]:
                            piece_hi(head, c, p)
                    if scored and s == 1 and par % 2 == 0:
                        head_unit(head, c, i)
                    if isinstance(n, int) and n == 2 * HEADS:
                        head_hi(s)
                if isinstance(n, int) and n == 2 * HEADS:
                    for k in (5, 6):
                        heads_back(k)

            def heads_back(k):
                for half in range(2):
                    act.wait_ge(o_stored[half], 16 * k + 32)
                act.dma_start(A(k), os_d[k]).then_inc(blk_in[k], 16)

            def head_hi(k):
                act.wait_ge(blk_in[k], 16)
                copy(h(k, 0), A(k)).then_inc(h_hi, 1)

            for p in PIECES_AT[1]:
                for q in p:
                    piece_hi(0, 0, q)
            for trips in half_steps(step):
                with act.Fori(0, trips) as i:
                    for q in range(2, 6):
                        step(4 * i + q, q, i)
            heads_back(CB - 1)
            split(U_WO + 2)
            for k in range(4, CB):
                head_hi(k)

            def y_blocks(u0, m0, bias, b, x_src):
                for n in range(CB):
                    split(u0 + n + 3)
                    act.wait_ge(mm_done, m0 + n + 1)
                    if n == 0:
                        fetch(b, x_src, R_G)
                    if bias is None:
                        copy(A(n), pair(n)).then_inc(mm_free, 1)
                    else:
                        act.activation(A(n), pair(n), ACT.Identity, bias=V[:, bias + n:bias + n + 1]).then_inc(mm_free, 1)
                    act.wait_ge(mm_free, m0 + n + 1)
                    square(A(n))

            def fetch(b, x_src, at):
                if b:
                    act.wait_ge(blk_out, 16 * CB * b)
                for k in range(CB):
                    act.dma_start(x_at(at, k), x_src[k]).then_inc(blk_in[k], 16)

            def renorm(out_dst, shift, more=True, func=None, pooled=True):
                for half in range(2):
                    for k in range(CB):
                        if pooled and k % 2:
                            n_pool[0] += 1
                            act.wait_ge(y_pool, n_pool[0])
                        else:
                            n_res[0] += 1
                            act.wait_ge(y_new, n_res[0])
                        if half and out_dst is not None:
                            act.dma_start(out_dst[k], A(k)).then_inc(blk_out, 16)
                        if more:
                            half_square(A_half(k, half))
                    if more:
                        std_row(half, D)
                if more:
                    for half in range(2):
                        for k in range(CB):
                            h_parts(t_slot(half * CB + k), h(k, 0, half), shift(k), func)

            def col(at):
                return lambda k: S[:, at + k:at + k + 1]

            y_blocks(U_WO, M_WO, None, 0, xT)
            std(N_A, D)
            renorm(xs_d, col(C_MOD + 3 * CB))

            def ffn(layer, b):
                u0, m0, j0, d0 = U_FFN[layer], M_FFN[layer], FB * layer, DN_START + CB * GROUPS * layer

                def splitr(i, c):
                    u = u0 + c
                    act.wait_ge(raw_in[u % 2], 96 * i + raw_count(u))
                    by, count = freed(prior(u))
                    if by == "mm":
                        act.wait_ge(mm_done, 8 * i + count)
                    if by == "dn" or c < 8:
                        act.wait_ge(dn_done, 2 * CB * i + (count if by == "dn" else d0))
                    copy(w(slot_of(u), 0), raw(u % 2)).then_inc(w_hi, 1)

                def g_part(i, j, g):
                    if j % 2 == 0:
                        wait(act, dn_done, 2 * CB * i + (d0 + CB * (g - 1)))
                    act.wait_ge(gp_ready, 4 * i + (j0 + j + 1))
                    copy(G(g, j % 2, 0), f(F_T + L)).then_inc(g_hi, 1)

                def up(i, g, q):
                    m, j, val = m0 + 4 * g + q, 2 * g + q // 2, q % 2
                    mi, ji = 8 * i + m, 4 * i + j
                    act.wait_ge(mm_done, mi + 1)
                    col = ji + FB * val
                    if val:
                        if not (isinstance(i, int) and j0 + j == 0):
                            act.wait_ge(g_lo, ji + j0)
                    elif not (isinstance(i, int) and j0 + j == 0):
                        act.wait_ge(gp_ready, ji + j0)
                    wv = V_FW + layer * 3 * 2 * FB
                    act.activation(f(F_T + val * L), pair(q), ACT.Identity, scale=V[:, bass.ds(wv + 2 * FB + col, 1)],
                                   bias=V[:, bass.ds(V_FB + layer * 2 * FB + col, 1)]).then_inc(tap_done, 1)
                    if not val:
                        if not (isinstance(i, int) and j == 0):
                            g_part(i, j - 1, (j - 1) // 2)
                        act.wait_ge(mm_free, mi + 1)
                        act.activation(f(F_T), f(F_T), ACT.Silu).then_inc(silu_g, 1)

                for q in range(4):
                    if q < 3:
                        split(u0 + q + 3)
                    up(0, 0, q)
                with act.Fori(0, (GROUPS - 1) // 2) as i:
                    for g in (1, 2):
                        n0 = 4 + 6 * (g - 1)
                        splitr(i, n0 + 2)
                        for q in range(4):
                            splitr(i, n0 + q + 3)
                            up(i, g, q)
                        splitr(i, n0 + 7)
                g_part(0, FB - 1, GROUPS - 1)
                fetch(b, xs_d, R_H)
                split(u0 + 66)
                split(u0 + 67)
                for c in range(CB):
                    act.wait_ge(dn_free, d0 + CB * (GROUPS - 1) + c + 1)
                    square(A(c))
                split(u0 + 68)

            ffn(0, 1)
            std(N_A, D)
            renorm(xs_d, col(C_MOD + MODS))

            act.wait_ge(mod_mm, 11)
            act.wait_ge(blk_out, 16 * CB * 2)
            for i in range(CB):
                split(U_PW1 + 2 * i + 3)
                split(U_PW1 + 2 * i + 4)
                act.wait_ge(mm_done, M_PW1 + 2 * i + 2)
                act.activation(f(F_SQ + L), pair(1), ACT.Sigmoid,
                               bias=V[:, V_BPW1 + CB + i:V_BPW1 + CB + i + 1]).then_inc(sig_ready, 1)
                if i >= 2:
                    act.wait_ge(conv_done, i - 1)
                for t in range(pe_taps(i)):
                    tap = V_WDW + (TAPS - 1 - t) * CB + i
                    act.activation(tap_diag(i, t), ident[:, :], ACT.Copy, scale=V[:, tap:tap + 1]).then_inc(diag_in, 1)
                act.wait_ge(mm_free, M_PW1 + 2 * i + 2)
                act.activation(A(i), U[i % 2][:, 0:L], ACT.Identity, scale=V[:, V_WDW + i:V_WDW + i + 1],
                               bias=V[:, V_BDW + i:V_BDW + i + 1]).then_inc(start_in, 1)
                if i:
                    act.wait_ge(taps_done, i)
                copy(f(F_RT), U[i % 2][:, 1:L + 1], V[:, V_WDW + CB + i:V_WDW + CB + i + 1]).then_inc(start_in, 1)
            act.wait_ge(sums_out, 3)
            act.activation(S[:, C_STD:C_STD + CB], bank(5, CB, N_A), ACT.Copy, scale=1.0 / D).then_inc(std_ready, 1)
            renorm(None, lambda k: V[:, V_BLN + k:V_BLN + k + 1], func=ACT.Silu, pooled=False)
            y_blocks(U_PW2, M_PW2, V_BPW2, 2, xs_d)
            std(N_A, D)
            renorm(xs_d, col(C_MOD + MODS + 3 * CB))
            ffn(1, 3)
            std(N_A, D)
            renorm(outT, None, more=False)
            act.wait_ge(blk_out, 16 * CB * 4)

        @block.vector
        def _(dve):
            n_sq, n_norm, n_h, n_rt, n_row = [0], [0], [0], [0], [0]
            chain = Chain(dve, dve_chain)

            def split(u):
                if u >= UNITS:
                    return
                dve.wait_ge(w_hi, u + 1)
                dve.tensor_tensor(w(slot_of(u), 1), raw(u % 2), w(slot_of(u), 0), SUB).then_inc(w_lo, 1)

            def add_square(first, acc, n=L):
                dve.wait_ge(sq_ready, n_sq[0] + 1)
                src = f(F_SQ + (n_sq[0] % 2) * L, n)
                if first:
                    dve.tensor_copy(acc, src).then_inc(sq_used, 1)
                else:
                    wait(dve, sq_used, n_sq[0])
                    dve.tensor_tensor(acc, acc, src, ADD).then_inc(sq_used, 1)
                n_sq[0] += 1

            def diagonals(at, src, n):
                dve.tensor_tensor(f(at, n * P).rearrange("p (c n) -> p c n", c=n),
                                  ident[:, :].unsqueeze(1).to_broadcast([P, n, P]),
                                  S[:, src:src + n].unsqueeze(2).to_broadcast([P, n, P]), MUL).then_inc(diag_ready, 1)
                n_rt[0] += 1

            def spread(n=CB, at=F_RT, inverse=True):
                n_norm[0] += 1
                dve.wait_ge(std_ready, n_norm[0])
                src = C_STD
                if inverse:
                    chain(dve.reciprocal(S[:, C_RSTD:C_RSTD + n], S[:, C_STD:C_STD + n]))
                    src = C_RSTD
                for a, b in ([(0, n // 2), (n // 2, n)] if n >= CB else [(0, n)]):
                    diagonals(at + a * P, src + a, b - a)

            def spread_half(half):
                n_row[0] += 1
                dve.wait_ge(cols_out, n_row[0])
                chain(dve.reciprocal(S[:, C_RSTD:C_RSTD + CB // 2], ROWCOLS[half]))
                diagonals(F_RT + half * HALF, C_RSTD, CB // 2)

            def rt_here(less=0):
                dve.wait_ge(rt_out, n_rt[0] - less)

            def h_blocks(src, gain, rt, dst_hi, dst_lo, shift, n=L):
                def lo(k):
                    dve.wait_ge(h_hi, n_h[0] + k + 1)
                    t = f(F_SQ + (k % 2) * L, n)
                    if shift is None:
                        dve.tensor_tensor(dst_lo(k), t, dst_hi(k), SUB).then_inc(h_lo, 1)
                    else:
                        dve.scalar_tensor_tensor(out=dst_lo(k), in0=t, scalar=shift(k), in1=dst_hi(k), op0=ADD, op1=SUB).then_inc(h_lo, 1)
                for k in range(CB):
                    if k >= 2:
                        dve.wait_ge(h_lo, n_h[0] + k - 1)
                    dve.scalar_tensor_tensor(out=f(F_SQ + (k % 2) * L, n), in0=src(k), scalar=gain(k), in1=rt,
                                             op0=MUL, op1=MUL).then_inc(ht_ready, 1)
                    if k >= 1:
                        lo(k - 1)
                lo(CB - 1)
                n_h[0] += CB
                dve.wait_ge(h_lo, n_h[0])

            dve.memset(ones[:, :], 1.0).then_inc(const_set, 1)
            dve.memset(S[:, :], 0.0).then_inc(const_set, 1)
            dve.wait_ge(const_set, 2)
            dve.memset(S[:, C_EPS:C_EPS + 1], EPS).then_inc(const_set, 1)
            dve.wait_ge(small_in, 32)
            dve.wait_ge(silu_c, 2)
            for k in range(CB):
                add_square(k == 0, f(F_ACCX, CTX), CTX)
            for k in range(CB):
                dve.wait_ge(mod1_in[0][k // 2], 16)
                for s in range(2):
                    by = S[:, C_SC + 2 * k + s:C_SC + 2 * k + s + 1]
                    if k == 0:
                        dve.tensor_scalar(shift_acc(s), mod1(0, k), by, None, MUL).then_inc(mod_part, 1)
                    else:
                        dve.wait_ge(mod_part, 2 * k - 1 + s)
                        dve.scalar_tensor_tensor(out=shift_acc(s), in0=mod1(0, k), scalar=by, in1=shift_acc(s), op0=MUL, op1=ADD).then_inc(mod_part, 1)
                add_square(k == 0, f(F_ACC))
                if k == 3:
                    spread(CTX // P, F_RT + L)

            def mod_first(vec, at, cols):
                return dve.tensor_tensor(S[:, at + vec * CB:at + (vec + 1) * CB], cols, V[:, V_BMOD + vec * CB:V_BMOD + (vec + 1) * CB], ADD)

            def gain(dst, g, mod, one):
                chain(dve.scalar_tensor_tensor(out=S[:, dst:dst + CB], in0=S[:, mod:mod + CB], scalar=float(one),
                                               in1=V[:, g:g + CB], op0=ADD, op1=MUL))

            def col(at):
                return lambda k: S[:, at + k:at + k + 1]

            for u in range(2):
                split(u)
            dve.wait_ge(mod_used, CB)
            chain(mod_first(1, C_MOD, PS[:, HALF:HALF + 2 * CB:2]))
            mod_first(1, C_MODX, PS[:, HALF + 1:HALF + 2 * CB:2]).then_inc(mod_out, 1)
            dve.wait_ge(mod_out, 1)
            gain(C_AV, V_PREMIX, C_MOD + CB, 1)
            gain(C_AX, V_PREMIX, C_MODX + CB, 1)
            spread(CB, F_ACC)
            dve.wait_ge(shift_mm, 1)
            chain(mod_first(0, C_MOD, bank(0, CB)))
            rt_here()
            h_blocks(A, col(C_AV), RT, lambda k: h(k, 0), lambda k: h(k, 1), col(C_MOD))
            dve.wait_ge(mod_mm, 1)
            mod_first(0, C_MODX, bank(7, CB, N_MOD)).then_inc(mod_out, 1)
            dve.wait_ge(mod_out, 2)
            split(2)
            h_blocks(lambda k: f(F_T + k * CTX, CTX), col(C_AX), RTX, lambda k: hx(k, 0), lambda k: hx(k, 1), col(C_MODX), CTX)

            split(3)
            split(4)
            dve.wait_ge(mmx_done, 2)
            chain(dve.tensor_copy(f(4352, CTX), bank(5, CTX)))
            dve.wait_ge(table_in, 32)
            dve.wait_ge(mm_free, M_DQKV + 1)
            dve.wait_ge(mm_done, M_DQKV + 2)
            dve.tensor_tensor(f(4352 + CTX), pair(1), COSD, MUL).then_inc(mm_free, 1)
            split(5)
            dve.wait_ge(mm_done, M_DQKV + 3)
            dve.tensor_tensor(f(F_T), pair(0), SIND, MUL).then_inc(mm_free, 1)
            dve.wait_ge(mm_free, M_DQKV + 3)
            dve.tensor_tensor(f(4352 + CTX), f(4352 + CTX), f(F_T), ADD).then_inc(rope_k, 1)
            spread(NKB)
            rt_here()
            dve.scalar_tensor_tensor(out=CKV, in0=CKV, scalar=V[:, V_GKV:V_GKV + 1], in1=RTKV,
                                     op0=MUL, op1=MUL).then_inc(lat_scaled, 1)
            for k, (at, src) in enumerate([(R_KR, KRF), (R_CKV, CKV)]):
                dve.wait_ge(lat_hi, k + 1)
                dve.tensor_tensor(r(at + KEYS, KEYS), src, r(at, KEYS), SUB).then_inc(lat_lo, 1)
            split(U_HEAD)
            spread()
            rt_here()
            for k in range(QLORA_B):
                dve.scalar_tensor_tensor(out=CQ[k], in0=CQ[k], scalar=V[:, V_GQ + k:V_GQ + k + 1], in1=RT,
                                         op0=MUL, op1=MUL).then_inc(lat_scaled, 1)
            for k in range(QLORA_B):
                dve.wait_ge(lat_hi, k + 3)
                dve.tensor_tensor(r(R_CQ + (QLORA_B + k) * L), CQ[k], r(R_CQ + k * L), SUB).then_inc(lat_lo, 1)
            dve.wait_ge(lat_lo, QLORA_B + 2)
            n_sq[0] += 1 + QLORA_B
            dve.wait_ge(table_in, 64)

            def turn_rotary(head, i):
                kind, start, width = PIECES[i]
                if kind == "qr":
                    dve.wait_ge(pj_done, 10 * head + (i + 1))
                    dve.tensor_tensor(ROPET[start // HALF], bank(6 + i % 2), CS[:, start:start + HALF], MUL).then_inc(pj_t, 1)

            def piece_lo(head, par, i):
                kind, start, width = PIECES[i]
                dve.wait_ge(pj_hi, 10 * head + (i + 1))
                if kind == "qr":
                    below = piece_at(kind, par, start, width, 0)[ROPE:]
                    dve.tensor_tensor(below, bank(6 + i % 2)[ROPE:], below, SUB).then_inc(pj_free, 1)
                else:
                    dve.tensor_tensor(piece_at(kind, par, start, width, 1), bank(6 + i % 2, width),
                                      piece_at(kind, par, start, width, 0), SUB).then_inc(pj_free, 1)

            def head_unit(head, c):
                dve.wait_ge(w_hi, U_HEAD + 2 + head)
                other = (c + 1) % 2
                dve.tensor_tensor(w(other, 1), raw(other), w(other, 0), SUB).then_inc(w_lo, 1)

            def maxes(n, par, s):
                c = (par % 2) * 4 + s
                dve.wait_ge(s_done, 4 * n + (s + 1))
                chain(dve.reduce_max(S[:, C_MX + c:C_MX + c + 1], PS[:, 0:KEYS], AX.X))
                dve.tensor_scalar(S[:, C_NM + c:C_NM + c + 1], S[:, C_MX + c:C_MX + c + 1], -SCALE, None, MUL).then_inc(s_max, 1)

            def scales(n, par, s):
                c = (par % 2) * 4 + s
                dve.wait_ge(s_free, 4 * n + (s + 1))
                chain(dve.reciprocal(S[:, C_RI + c:C_RI + c + 1], S[:, C_RS + c:C_RS + c + 1]))
                dve.tensor_scalar(Pt(par, s), Pt(par, s), S[:, C_RI + c:C_RI + c + 1], None, MUL).then_inc(p_ready, 1)

            def tp_sub(n, par, kb):
                kbn = NKB * par + kb
                dve.wait_ge(tp_hi, NKB * n + (kb + 1))
                at = R_PT + (kbn % 4) * L
                dve.tensor_tensor(r(at + HALF, HALF), bank(3 + kbn % 2), r(at, HALF), SUB).then_inc(tp_lo, 1)

            def mod_add(t, dst):
                dve.wait_ge(mod_mm, t + 2)
                dve.tensor_tensor(S[:, bass.ds(C_MOD + dst, CB)], bank(7, CB), V[:, bass.ds(V_BMOD + dst, CB)],
                                  ADD).then_inc(mod_out, 1)

            def head_lo(k):
                dve.wait_ge(h_hi, n_h[0] + k + 1)
                dve.tensor_tensor(h(k, 1), A(k), h(k, 0), SUB).then_inc(h_lo, 1)

            def step(n, par, i, scored=True, turned=True, weighed=True):
                for s in range(4):
                    if isinstance(n, int) and n == 2 * HEADS:
                        if s == 0:
                            split(U_WO + 1)
                        else:
                            dve.wait_ge(pt_free, 4 + 15 * NKB)
                            head_lo(s - 1)
                    turns = list(TURNS[s]) if turned else []
                    if scored:
                        maxes(n, par, s)
                        if s == 0 and par % 4 == 2:
                            mod_add(i, CB * i + 2 * CB)
                    if turns:
                        tp_sub(n - 1, par - 1, turns.pop(0))
                    head, c = head_of(par, i)
                    if scored and not (isinstance(n, int) and n == 2 * HEADS - 1):
                        for p in PIECES_AT[par % 2][s]:
                            turn_rotary(head, p)
                    if scored:
                        scales(n, par, s)
                    if turns:
                        tp_sub(n - 1, par - 1, turns.pop(0))
                    if turns:
                        tp_sub(n - 1, par - 1, turns.pop(0))
                    if scored and not (isinstance(n, int) and n == 2 * HEADS - 1):
                        for p in PIECES_AT[par % 2][s]:
                            piece_lo(head, c, p)
                    if scored and s == 1 and par % 2 == 0:
                        head_unit(head, c)

            for p in PIECES_AT[1]:
                for q in p:
                    turn_rotary(0, q)
                for q in p:
                    piece_lo(0, 0, q)
            for trips in half_steps(step):
                with dve.Fori(0, trips) as i:
                    chain.enter(i, 32)
                    for q in range(2, 6):
                        step(4 * i + q, q, i)
                    chain.leave(trips)
            dve.wait_ge(mod_out, 6)
            split(U_WO + 2)
            dve.wait_ge(pt_free, 4 + 16 * NKB)
            for k in range(3, CB):
                head_lo(k)
            n_h[0] += CB
            dve.wait_ge(h_lo, n_h[0])

            def y_blocks(u0):
                for n in range(CB):
                    split(u0 + n + 3)
                    if n < CB - 1:
                        add_square(n == 0, f(F_ACC))
                n_sq[0] += 1

            def renorm(make, h_gain=None, h_shift=None, pooled=None):
                make(0, lambda k: None)
                rt_here()
                make(1, lambda k: k == 6 and h_gain is not None and spread_half(0))
                if h_gain is None:
                    return

                def lo(j):
                    half, k = divmod(j, CB)
                    dve.wait_ge(h_hi, n_h[0] + j + 1)
                    out, t, hi = h(k, 1, half), t_slot(j), h(k, 0, half)
                    if h_shift is None:
                        dve.tensor_tensor(out, t, hi, SUB).then_inc(h_lo, 1)
                    else:
                        dve.scalar_tensor_tensor(out=out, in0=t, scalar=h_shift(k), in1=hi, op0=ADD, op1=SUB).then_inc(h_lo, 1)

                rt_here()
                for j in range(2 * CB + 2):
                    if j < 2 * CB:
                        half, k = divmod(j, CB)
                        if j == CB:
                            rt_here()
                        wait(dve, h_lo, n_h[0] + j - 3 if j >= 4 else 0)
                        if pooled is not None and k % 2:
                            dve.wait_ge(y_pool, pooled + CB // 2 * half + k // 2 + 1)
                        dve.scalar_tensor_tensor(out=t_slot(j), in0=A_half(k, half), scalar=h_gain(k), in1=RT_OF[half],
                                                 op0=MUL, op1=MUL).then_inc(ht_ready, 1)
                    if j >= 2:
                        lo(j - 2)
                    if j == 3:
                        spread_half(1)
                n_h[0] += 2 * CB
                dve.wait_ge(h_lo, n_h[0])

            def residual(b, g_post, gate, more, g_pre, scale, shift):
                gain(C_GV, g_post, gate, 0)
                if more:
                    gain(C_AV, g_pre, scale, 1)
                spread()
                rt_here(1)

                def make(half, between):
                    for k in range(CB):
                        scaled = dve.scalar_tensor_tensor(out=A_half(k, half), in0=A_half(k, half), scalar=S[:, C_GV + k:C_GV + k + 1],
                                                          in1=RT_OF[half], op0=MUL, op1=MUL)
                        if k % 2 == 0:
                            scaled.then_inc(dve_chain, 1)
                            chain.n += 1
                        else:
                            scaled.then_inc(y_scaled, 1)
                            dve.wait_ge(dve_chain, chain.n)
                            dve.wait_ge(blk_in[k - 1], 16 * (b + 2))
                            dve.tensor_tensor(A_half(k - 1, half), A_half(k - 1, half),
                                              x_at(R_H if b % 2 else R_G, k - 1)[:, half * HALF:(half + 1) * HALF], ADD).then_inc(y_new, 1)
                        between(k)

                renorm(make, *((col(C_AV), col(shift), CB * b) if more else ()))

            y_blocks(U_WO)
            residual(0, V_POSTMIX, C_MOD + 2 * CB, True, V_PREFFN, C_MOD + 4 * CB, C_MOD + 3 * CB)

            def ffn(layer, b):
                u0, m0, j0, d0 = U_FFN[layer], M_FFN[layer], FB * layer, DN_START + CB * GROUPS * layer

                def splitr(i, c):
                    u = u0 + c
                    dve.wait_ge(w_hi, 12 * i + (u + 1))
                    dve.tensor_tensor(w(slot_of(u), 1), raw(u % 2), w(slot_of(u), 0), SUB).then_inc(w_lo, 1)

                def g_part(i, j, g):
                    ji = 4 * i + j
                    dve.wait_ge(g_hi, ji + (j0 + 1))
                    dve.tensor_tensor(G(g, j % 2, 1), f(F_T + L), G(g, j % 2, 0), SUB).then_inc(g_lo, 1)

                def taps(i, g, q):
                    m, val = m0 + 4 * g + q, q % 2
                    c = 4 * i + 2 * g + q // 2 + FB * val
                    wv = V_FW + layer * 6 * FB
                    at = F_T + val * L
                    dve.wait_ge(tap_done, 8 * i + (2 * FB * layer + 4 * g + q + 1))
                    chain(dve.scalar_tensor_tensor(out=f(at + 1, L - 1), in0=PS[:, (q % 2) * L:(q % 2) * L + L - 1],
                                                   scalar=V[:, bass.ds(wv + c, 1)], in1=f(at + 1, L - 1), op0=MUL, op1=ADD))
                    dve.scalar_tensor_tensor(out=f(at, L - 1), in0=PS[:, (q % 2) * L + 1:(q % 2) * L + L],
                                             scalar=V[:, bass.ds(wv + 4 * FB + c, 1)], in1=f(at, L - 1), op0=MUL, op1=ADD).then_inc(mm_free, 1)

                def product(i, g, q):
                    dve.wait_ge(silu_g, 4 * i + 2 * g + q // 2 + (j0 + 1))
                    dve.wait_ge(mm_free, 8 * i + m0 + 4 * g + q + 1)
                    dve.tensor_tensor(f(F_T + L), f(F_T + L), f(F_T), MUL).then_inc(gp_ready, 1)

                def down(i, g, blocks):
                    for c in blocks:
                        if c == 0:
                            dve.wait_ge(dn_free, 2 * CB * i + (d0 + CB * g))
                        dve.wait_ge(dn_done, 2 * CB * i + (d0 + CB * g + c + 1))
                        dve.tensor_tensor(A(c), A(c), dn(c), ADD).then_inc(dn_free, 1)

                mods = layer == 0
                for q in range(4):
                    if q < 3:
                        split(u0 + q + 3)
                    taps(0, 0, q)
                    if q == 0 and mods:
                        mod_add(4, CB * 4 + 2 * CB)
                    if q == 1:
                        dve.wait_ge(blk_out, 16 * CB * b)
                    if q:
                        for c in range(3 * q - 3, min(3 * q, CB)):
                            dve.memset(A(c), 0.0).then_inc(y_zero, 1)
                    if q == 2:
                        g_part(0, 0, 0)
                    if q % 2:
                        product(0, 0, q)
                dve.wait_ge(y_zero, CB * (layer + 1))
                with dve.Fori(0, (GROUPS - 1) // 2) as i:
                    chain.enter(i, 8)
                    for g in (1, 2):
                        n0 = 4 + 6 * (g - 1)
                        splitr(i, n0 + 2)
                        for q in range(4):
                            splitr(i, n0 + q + 3)
                            taps(i, g, q)
                            if q % 2 == 0:
                                g_part(i, 2 * g + q // 2 - 1, (2 * g + q // 2 - 1) // 2)
                            if q == 1:
                                product(i, g, q)
                            if mods and g == 2 and q == 0:
                                mod_add(i + 5, CB * i + 7 * CB)
                        down(i, g - 1, [0])
                        product(i, g, 3)
                        down(i, g - 1, [1])
                        splitr(i, n0 + 7)
                        down(i, g - 1, range(2, CB))
                    chain.leave((GROUPS - 1) // 2)
                g_part(0, FB - 1, GROUPS - 1)
                split(u0 + 66)
                split(u0 + 67)
                dve.wait_ge(dn_free, d0 + CB * (GROUPS - 1))
                for c in range(CB):
                    dve.wait_ge(dn_done, d0 + CB * (GROUPS - 1) + c + 1)
                    dve.tensor_tensor(A(c), A(c), dn(c), ADD).then_inc(dn_free, 1)
                    if c >= 1:
                        add_square(c == 1, f(F_ACC))
                n_sq[0] += 1
                split(u0 + 68)

            ffn(0, 1)
            dve.wait_ge(mod_out, 12)
            residual(1, V_POSTFFN, C_MOD + 5 * CB, True, V_PREMIX + CB, C_MOD + MODS + CB, C_MOD + MODS)

            for s in range(2):
                chain(dve.memset(U[s][:, 0:PAD], 0.0))
                chain(dve.memset(U[s][:, PAD + L:], 0.0))

            def conv_finish(i):
                dve.wait_ge(conv_done, i + 1)
                dve.tensor_tensor(A(i), A(i), conv_out(i), ADD).then_inc(conv_free, 1)
                dve.wait_ge(conv_free, i + 1)
                if i == 0:
                    chain(dve.tensor_copy(f(F_ACC), A(i)))
                elif i < CB - 2:
                    chain(dve.tensor_tensor(f(F_ACC), f(F_ACC), A(i), ADD))
                elif i == CB - 2:
                    dve.tensor_tensor(f(F_ACC), f(F_ACC), A(i), ADD).then_inc(acc_ready, 1)

            for i in range(CB):
                dve.wait_ge(sig_ready, i + 1)
                if i >= 2:
                    dve.wait_ge(conv_done, i - 1)
                dve.scalar_tensor_tensor(out=U[i % 2][:, PAD:PAD + L], in0=pair(0), scalar=V[:, V_BPW1 + i:V_BPW1 + i + 1],
                                         in1=f(F_SQ + L), op0=ADD, op1=MUL).then_inc(mm_free, 2)
                split(U_PW1 + 2 * i + 3)
                split(U_PW1 + 2 * i + 4)
                dve.wait_ge(start_in, 2 * i + 2)
                for t in range(2, TAPS - pe_taps(i)):
                    chained = A(i) if t % 2 == 0 else f(F_RT)
                    chain.lag(dve.scalar_tensor_tensor(out=chained, in0=U[i % 2][:, t:t + L],
                                                       scalar=V[:, V_WDW + t * CB + i:V_WDW + t * CB + i + 1],
                                                       in1=chained, op0=MUL, op1=ADD))
                    if t == 12 and i:
                        conv_finish(i - 1)
                dve.wait_ge(dve_chain, chain.n)
                dve.tensor_tensor(A(i), A(i), f(F_RT), ADD).then_inc(taps_done, 1)
                dve.wait_ge(taps_done, i + 1)
            conv_finish(CB - 1)
            spread(inverse=False)
            rt_here(1)

            def centre(half, between):
                for k in range(CB):
                    dve.tensor_tensor(A_half(k, half), A_half(k, half), RT_OF[half], SUB).then_inc(y_new, 1)
                    between(k)

            renorm(centre, lambda k: V[:, V_GLN + k:V_GLN + k + 1])
            y_blocks(U_PW2)
            residual(2, V_POSTMIX + CB, C_MOD + MODS + 2 * CB, True, V_PREFFN + CB, C_MOD + MODS + 4 * CB, C_MOD + MODS + 3 * CB)
            ffn(1, 3)
            residual(3, V_POSTFFN + CB, C_MOD + MODS + 5 * CB, False, None, None, None)

        @block.tensor
        def _(pe):
            n_sq, n_h, n_diag, n_row, n_half = [0], [0], [0], [0], [0]

            def three(out, w_parts, x_parts, first, last):
                (wh, wl), (xh, xl) = w_parts, x_parts
                pe.matmul(out, wl, xh, start=first, stop=False)
                pe.matmul(out, wh, xl, start=False, stop=False)
                return pe.matmul(out, wh, xh, start=False, stop=last)

            def col_sums(src, at, first, last, n=CB, b=7):
                for c in range(n):
                    mm = pe.matmul(bank(b, 1, at + c), f(src + c * P, P), ones[:, 0:1],
                                   start=first and c == 0, stop=last and c == n - 1)
                return mm

            def square_sums(at, first, last, n=CB, b=7):
                n_sq[0] += 1
                pe.wait_ge(sq_ready, n_sq[0])
                slot = (n_sq[0] - 1) % 2 if n <= CB else 0
                col_sums(F_SQ + slot * L, at, first, last, n, b).then_inc(sq_used, 1)

            def square_row(k, half):
                n_half[0] += 1
                pe.wait_ge(half_sq, n_half[0])
                pe.matmul(SUMROW[half], ones[:, 0:1], half_slot(n_half[0] - 1), start=k == 0, stop=k == CB - 1).then_inc(half_used, 1)

            def row_cols(half):
                n_row[0] += 1
                pe.wait_ge(row_ready, n_row[0])
                for c in range(CB // 2):
                    mm = pe.matmul(ROWCOLS[half][:, c:c + 1], ROW[half][:, c * P:(c + 1) * P], ones[0:1, 0:1], start=True, stop=True)
                mm.then_inc(cols_out, 1)

            def spread_half(half):
                n_diag[0] += 1
                pe.wait_ge(diag_ready, n_diag[0])
                pe.matmul(RT_OF[half], ones[:, :], f(F_RT + half * HALF, HALF), start=True, stop=True).then_inc(rt_out, 1)

            def renorm():
                for half in range(2):
                    for k in range(CB):
                        if half and k == CB - 2:
                            spread_half(0)
                        square_row(k, half)
                    row_cols(half)

            def spread(n=CB, src=F_RT, b=4):
                at = 0
                for width in ([n // 2 * P] * 2 if n >= CB else [n * P]):
                    n_diag[0] += 1
                    pe.wait_ge(diag_ready, n_diag[0])
                    end = at + width
                    while at < end:
                        step = min(end, (at // HALF + 1) * HALF) - at
                        mm = pe.matmul(bank(b, step, at), ones[:, :], f(src + at, step), start=True, stop=True)
                        at += step
                    mm.then_inc(rt_out, 1)

            def mod_sums(acc, b=7, at=N_MOD):
                for c in range(CB):
                    mm = pe.matmul(bank(b, 1, at + c), acc[:, c * P:(c + 1) * P], ones[:, 0:1], start=True, stop=True)
                return mm

            def up_block(u, m, slot, par, k, halves=(0, 1)):
                if k == 0 and halves[0] == 0:
                    pe.wait_ge(w_lo, u + 1)
                    if not isinstance(m, int) or m >= 2:
                        pe.wait_ge(mm_free, m - 1)
                for half in halves:
                    mm = three(pair(par)[:, half * HALF:(half + 1) * HALF], [w(slot, p, k * P, P) for p in range(2)],
                               [h(k, p, half) for p in range(2)], k == 0, k == CB - 1)
                if k == CB - 1 and halves[-1] == 1:
                    mm.then_inc(mm_done, 1)

            def up(u, m, slot, par):
                for k in range(CB):
                    up_block(u, m, slot, par, k)

            def first_two(u, m):
                for k in range(CB + 2):
                    if k < CB:
                        pe.wait_ge(h_lo, n_h[0] + k + 1)
                        up_block(u, m, slot_of(u), m % 2, k)
                    if k >= 2:
                        up_block(u + 1, m + 1, slot_of(u + 1), (m + 1) % 2, k - 2)
                n_h[0] += CB

            def first_two_halves(u, m):
                for k in range(CB):
                    pe.wait_ge(h_lo, n_h[0] + k + 1)
                    for n in range(2):
                        up_block(u + n, m + n, slot_of(u + n), (m + n) % 2, k, (0,))
                    if k == 1:
                        spread_half(1)
                for k in range(CB + 2):
                    if k < CB:
                        pe.wait_ge(h_lo, n_h[0] + CB + k + 1)
                        up_block(u, m, slot_of(u), m % 2, k, (1,))
                    if k >= 2:
                        up_block(u + 1, m + 1, slot_of(u + 1), (m + 1) % 2, k - 2, (1,))
                n_h[0] += 2 * CB

            pe.wait_ge(const_set, 3)
            pe.sem_inc(pt_free, 4)
            pe.sem_inc(tp_lo, 2)
            pe.sem_inc(o_free, 1)
            for s in range(2):
                pe.sem_inc(o_stored[s], 16)
            pe.sem_inc(dn_done, DN_START)
            pe.sem_inc(dn_free, DN_START)
            pe.wait_ge(silu_c, 2)
            pe.wait_ge(small_in, 32)

            for k in range(CB):
                pe.wait_ge(mod1_in[1][k // 2], 16)
                for c in range(CB):
                    mm = pe.matmul(bank(1, 2, 2 * c), mod1(1, k)[:, c * P:(c + 1) * P], S[:, C_SC + 2 * k:C_SC + 2 * k + 2],
                                   start=k + c == 0, stop=k + c == 2 * CB - 2)
                mm.then_inc(mod_used, 1)
                if k == 1:
                    n_sq[0] += CB
                    pe.wait_ge(sq_used, n_sq[0])
                    col_sums(F_ACCX, N_B, True, True, CTX // P, 3).then_inc(sums_out, 1)
                if k == 5:
                    spread(CTX // P, F_RT + L, 6)
            n_sq[0] += CB
            pe.wait_ge(sq_used, n_sq[0])
            col_sums(F_ACC, N_A, True, True, b=2).then_inc(sums_out, 1)
            pe.wait_ge(mod_part, 2 * CB)
            mod_sums(shift_acc(0), 0, 0).then_inc(shift_mm, 1)
            spread(src=F_ACC)
            mod_sums(shift_acc(1)).then_inc(mod_mm, 1)

            first_two(U_DQKV, M_DQKV)
            pe.wait_ge(h_lo, 2 * CB)
            n_h[0] += CB
            for n in range(2):
                for k in range(CB):
                    mm = three(bank(n + 4, CTX), [w(slot_of(n), p, k * P, P) for p in range(2)],
                               [hx(k, p) for p in range(2)], k == 0, k == CB - 1)
                mm.then_inc(mmx_done, 1)
            up(2, 2, 2, 0)
            square_sums(N_KV, True, True, NKB)
            up(3, 3, 3, 1)
            spread(NKB)
            up(4, 4, 0, 0)
            square_sums(N_Q, True, False)
            up(5, 5, 1, 1)
            square_sums(N_Q, False, False)
            square_sums(N_Q, False, True)
            spread()

            def piece(head, par, i, mods=None):
                slot = par % 2
                kind, start, width = PIECES[i]
                if i == 0:
                    pe.wait_ge(w_lo, head + (U_HEAD + 1))
                if i >= 2 or not (isinstance(head, int) and head == 0):
                    pe.wait_ge(pj_free, 10 * head + (i - 1))
                if mods is not None:
                    pe.wait_ge(mod_out, mods)
                out = bank(6 + i % 2, width)
                if kind == "v":
                    for b in range(width // P):
                        at = start + b * P
                        mm = three(out[:, b * P:(b + 1) * P], [r(R_CKV + p * KEYS + at, P) for p in range(2)],
                                   [w(slot, p, 7 * P, P) for p in range(2)], True, True)
                elif kind == "k":
                    mm = three(out, [w(slot, p, 6 * P, P) for p in range(2)],
                               [r(R_CKV + p * KEYS + start, width) for p in range(2)], True, True)
                else:
                    for kb in range(QLORA_B):
                        if i == 0 and isinstance(head, int) and head == 0:
                            pe.wait_ge(lat_lo, kb + 3)
                        mm = three(out, [w(slot, p, (2 * kb + (kind == "qr")) * P, P) for p in range(2)],
                                   [r(R_CQ + (p * QLORA_B + kb) * L + start, width) for p in range(2)],
                                   kb == 0, kb == QLORA_B - 1)
                mm.then_inc(pj_done, 1)

            def fold(head, i):
                kind, start, width = PIECES[i]
                if kind == "qr":
                    if i == 1 and isinstance(head, int) and head == 0:
                        pe.wait_ge(table_in, 64)
                    pe.wait_ge(pj_t, 2 * head + (start // HALF + 1))
                    pe.matmul(bank(6 + i % 2), FOLD, ROPET[start // HALF], start=True, stop=True).then_inc(fold_done, 1)

            def scores(n, par, s, head):
                if s == 0:
                    pe.wait_ge(pj_free, 10 * head + (7 if par % 2 else 5))
                if s or not (isinstance(n, int) and n == 0):
                    pe.wait_ge(s_free, 4 * n + s)
                q = (par % 2) * HALF + s * P
                for at, width in KP:
                    three(PS[:, at:at + width], [r(R_Q + p * L + q, P) for p in range(2)],
                          [r(KS[(par // 2) % 2] + p * KEYS + at, width) for p in range(2)], True, False)
                    pe.matmul(PS[:, at:at + width], r(R_Q + 2 * L + q, P)[:ROPE], r(R_KR + KEYS + at, width)[:ROPE],
                              start=False, stop=False)
                    mm = pe.matmul(PS[:, at:at + width], r(R_Q + 2 * L + q, P), r(R_KR + at, width), start=False, stop=True)
                mm.then_inc(s_done, 1)

            def turn(n, par, kb):
                kbn = NKB * par + kb
                if kb == 0:
                    pe.wait_ge(p_ready, 4 * n + 4)
                pe.wait_ge(tp_lo, NKB * n + (kb + 1))
                for s in range(4):
                    mm = pe.transpose(bank(3 + kbn % 2, P, s * P), Pt(par, s)[:, kb * P:(kb + 1) * P], ident[:, :])
                mm.then_inc(tp_done, 1)

            def weigh(n, par, kb, head):
                kbn = NKB * par + kb
                pe.wait_ge(tp_lo, NKB * n + (kb + 3))
                if kb == 0:
                    pe.wait_ge(o_free, n + 1)
                    pe.wait_ge(pj_free, 10 * head + 10)
                vs, pt = VS[(par // 2) % 2] + kb * P, R_PT + (kbn % 4) * L
                mm = three(bank(5), [r(vs + p * KEYS, P) for p in range(2)], [r(pt + p * HALF, HALF) for p in range(2)],
                           kb == 0, kb == NKB - 1)
                mm.then_inc(pt_free, 1)

            def step(n, par, i, scored=True, turned=True, weighed=True):
                for s in range(4):
                    turns = list(TURNS[s]) if turned else []
                    mods = None
                    if scored:
                        scores(n, par, s, 2 * i + par // 2)
                        if s == 0 and par % 4 == 2:
                            pe.wait_ge(pj_free, 20 * i + 15)
                            pe.wait_ge(mod_acc, i + 1)
                            mod_sums(f(F_MD + 2 * L)).then_inc(mod_mm, 1)
                            mods = i + 3
                    if turns:
                        turn(n - 1, par - 1, turns.pop(0))
                    head, c = head_of(par, i)
                    pieces = PIECES_AT[par % 2][s] if scored and not (isinstance(n, int) and n == 2 * HEADS - 1) else []
                    for p in pieces:
                        if PIECES[p][0] == "qr":
                            piece(head, c, p, mods)
                    back = 2 if s == 0 else 1
                    if weighed if s == 0 else turned:
                        for kb in WEIGHS[s]:
                            weigh(n - back, par - back, kb, 2 * i + (par - back) // 2)
                    if turns:
                        turn(n - 1, par - 1, turns.pop(0))
                    for p in pieces:
                        if PIECES[p][0] != "qr":
                            piece(head, c, p, mods)
                    if turns:
                        turn(n - 1, par - 1, turns.pop(0))
                    for p in pieces:
                        fold(head, p)

            for p in PIECES_AT[1]:
                for q in p:
                    piece(0, 0, q, 2 if q == 1 else None)
                for q in p:
                    fold(0, q)
            for trips in half_steps(step):
                with pe.Fori(0, trips) as i:
                    for q in range(2, 6):
                        step(4 * i + q, q, i)

            def boundary(more):
                n_sq[0] += CB - 1
                pe.wait_ge(sq_used, n_sq[0])
                col_sums(F_ACC, N_A, True, False)
                square_sums(N_A, False, True)
                spread()
                if more:
                    renorm()

            def mixer_out(u0, m0, first=first_two):
                first(u0, m0)
                for n in range(2, CB):
                    up(u0 + n, m0 + n, slot_of(u0 + n), n % 2)

            mixer_out(U_WO, M_WO)
            boundary(True)

            def ffn(layer):
                u0, m0, j0, d0 = U_FFN[layer], M_FFN[layer], FB * layer, DN_START + CB * GROUPS * layer

                def mods(t, freed):
                    pe.wait_ge(dn_free, freed)
                    pe.wait_ge(mod_acc, t + 1)
                    mod_sums(f(F_MD + 2 * L)).then_inc(mod_mm, 1)

                def down(i, g, u, taken=None):
                    pe.wait_ge(w_lo, 12 * i + (u + 2))
                    pe.wait_ge(g_lo, 4 * i + (j0 + 2 * g + 2))
                    if taken is not None:
                        pe.wait_ge(mod_out, taken)
                    for c in range(CB):
                        pe.wait_ge(dn_free, 2 * CB * i + (d0 + CB * g + c - 1))
                        for jj in range(2):
                            for half in range(2):
                                mm = three(dn(c)[:, half * HALF:(half + 1) * HALF],
                                           [w(slot_of(u + jj), p, c * P, P) for p in range(2)],
                                           [G(g, jj, p, half) for p in range(2)], jj == 0, jj == 1)
                        mm.then_inc(dn_done, 1)

                first_two_halves(u0, m0)
                if layer == 0:
                    mods(4, d0)
                for q in range(2, 4):
                    up(u0 + q, m0 + q, slot_of(u0 + q), q % 2)
                with pe.Fori(0, (GROUPS - 1) // 2) as i:
                    for g in (1, 2):
                        n0 = u0 + 4 + 6 * (g - 1)
                        for q in range(4):
                            up(12 * i + (n0 + q), 8 * i + (m0 + 4 * g + q), slot_of(n0 + q), q % 2)
                            if layer == 0 and g == 2 and q == 0:
                                mods(i + 5, 2 * CB * i + (d0 + CB))
                        down(i, g - 1, n0 + 4, i + 8 if layer == 0 and g == 2 else None)
                down(0, GROUPS - 1, u0 + 64)

            ffn(0)
            boundary(True)
            def conv(i):
                pe.wait_ge(mm_free, M_PW1 + 2 * i + 2)
                if i >= 2:
                    pe.wait_ge(conv_free, i - 1)
                pe.wait_ge(diag_in, PE_TAPS * i + pe_taps(i))
                n = pe_taps(i)
                for t in range(n):
                    for half in range(2):
                        mm = pe.matmul(conv_out(i, half), tap_diag(i, t), U[i % 2][:, TAPS - 1 - t + half * HALF:TAPS - 1 - t + (half + 1) * HALF],
                                       start=t == 0, stop=t == n - 1)
                mm.then_inc(conv_done, 1)

            first_two_halves(U_PW1, M_PW1)
            for i in range(CB):
                if i < CB - 1:
                    for n in (2 * i + 2, 2 * i + 3):
                        up(U_PW1 + n, M_PW1 + n, slot_of(U_PW1 + n), n % 2)
                conv(i)
            pe.wait_ge(acc_ready, 1)
            col_sums(F_ACC, N_A, True, False, b=5)
            pe.wait_ge(conv_free, CB)
            col_sums(F_A + (CB - 1) * L, N_A, False, True, b=5).then_inc(sums_out, 1)
            spread()
            renorm()
            mixer_out(U_PW2, M_PW2, first_two_halves)
            boundary(True)
            ffn(1)
            boundary(False)


def rope_tables(np):
    quarter = ROPE // 4
    pos = np.arange(L)
    inv = (np.float32(10000.0) ** (-np.arange(quarter, dtype=np.float32) / np.float32(quarter))).astype(np.float32)
    rows = (pos // GRID_W).astype(np.float32)[:, None] * inv
    cols = (pos % GRID_W).astype(np.float32)[:, None] * inv
    angle = np.concatenate([rows, rows, cols, cols], axis=-1).T
    sign = np.tile(np.repeat(np.array([-1.0, 1.0], np.float32), quarter), 2)[:, None]
    return np.cos(angle).astype(np.float32), (np.sin(angle) * sign).astype(np.float32)


def up_units(np, w):
    n = w.shape[1] // P
    return np.ascontiguousarray(w.reshape(CB, P, n, P).transpose(2, 1, 0, 3)).reshape(n, P, D)


def pack_units(np, i):
    swap = np.arange(ROPE).reshape(2, 2, ROPE // 4)[:, ::-1].reshape(-1)
    dqkv = i["mla_w_dqkv"][0]
    kr = dqkv[:, 512:576]
    stream = [up_units(np, dqkv[:, 384:512]), up_units(np, np.concatenate([kr, kr], 1)),
              up_units(np, np.concatenate([kr[:, swap], kr[:, swap]], 1)), up_units(np, dqkv[:, :384])]
    uq = i["mla_w_uq"][0].reshape(QLORA_B, P, HEADS, 192)
    ukv = i["mla_w_ukv"][0].reshape(P, HEADS, 256)
    for hd in range(HEADS):
        q = uq[:, :, hd]
        q = np.concatenate([q, q[:, :, 128:][:, :, swap]], -1).transpose(1, 0, 2).reshape(P, 768)
        stream.append(np.concatenate([q, ukv[:, hd]], -1)[None])
    stream.append(up_units(np, i["mla_w_o"][0]))

    def ffn(layer):
        ups, downs = up_units(np, i["ffn_w_up"][layer]), i["ffn_w_down"][layer].reshape(FB, P, D)
        out = []
        for g in range(GROUPS + 1):
            if g < GROUPS:
                out += [ups[2 * g], ups[FB + 2 * g], ups[2 * g + 1], ups[FB + 2 * g + 1]]
            if g:
                out += [downs[2 * g - 2], downs[2 * g - 1]]
        return np.stack(out)

    pw1 = up_units(np, i["cv_w_pw1"][0]).reshape(2, CB, P, D).transpose(1, 0, 2, 3).reshape(2 * CB, P, D)
    stream += [ffn(0), pw1, up_units(np, i["cv_w_pw2"][0]), ffn(1)]
    return np.concatenate(stream)


def pack_vectors(np, i):
    def cols(a):
        return np.asarray(a).reshape(-1, P).T

    names = ["g_pre_mix", "g_post_mix", "g_pre_ffn", "g_post_ffn", "mla_g_q", "mla_g_kv", "cv_b_pw1", "cv_w_dw",
             "cv_b_dw", "cv_g_ln", "cv_b_ln", "cv_b_pw2", "ffn_w_dw", "ffn_b_dw"]
    v = np.concatenate([cols(i["c"]), cols(i["c_ctx"]), cols(i["b_mod"])] + [cols(i[n]) for n in names], 1)
    assert v.shape == (P, NV)
    return np.ascontiguousarray(v)


def kernel(**inputs):
    import concourse.bacc as bacc
    import numpy as np
    from concourse.bass_utils import run_bass_kernel_spmd

    i = {name: np.asarray(a) for name, a in inputs.items()}
    cos, sin = rope_tables(np)
    arrays = {
        "x_t": np.ascontiguousarray(i["x"][0].T).reshape(CB, P, L),
        "ctx_t": np.ascontiguousarray(i["ctx"][0].T).reshape(CB, P, CTX),
        "units": pack_units(np, i),
        "mod_w": np.ascontiguousarray(i["w_mod"].reshape(2, CB, P, 6, D).transpose(0, 3, 1, 2, 4)).reshape(12, CB, P, D),
        "vectors_in": pack_vectors(np, i),
        "identity": np.eye(P, dtype=np.float32),
        "fold": np.tile(np.eye(ROPE, dtype=np.float32), (2, 2)),
        "cos_sin": np.concatenate([cos, sin]),
        "cos_cos": np.concatenate([cos, cos]),
        "sin_sin": np.concatenate([sin, sin]),
    }
    nc = bacc.Bacc("TRN2", target_bir_lowering=False, num_devices=1, dynamic_dma_scratch_size=8192)
    args = [nc.dram_tensor(n, a.shape, mybir.dt.float32, kind="ExternalInput").ap() for n, a in arrays.items()]
    out = nc.dram_tensor("out_t", (CB, P, L), mybir.dt.float32, kind="ExternalOutput").ap()
    build(nc, *args, out)
    got = run_bass_kernel_spmd(nc, [arrays], core_ids=[0]).results[0]["out_t"]
    return np.ascontiguousarray(got.reshape(D, L).T)[None]
```
